# Optimizing a Trainium2 kernel written in Bass

```python
import math
import jax, jax.numpy as jnp
from jax import lax
import numpy as np
import jax
import jax.numpy as jnp

D_MODEL = 1024
BATCH = 1
SEQ = 256
DEPTH = 1

D_CONV = D_MODEL
CONV_WIDTH = 3
N_HEADS = 16
HEAD_DIM = 64
D_ATTN = N_HEADS * HEAD_DIM
ATTN_PATTERNS = ((128, 1), (512, 4), (2048, 16))
QB = 128
IN_COLS = 4 * D_CONV + 4 * D_ATTN + 2 * D_MODEL
EPS = 1e-6


def rms_norm(x, g):
    xf = x.astype(jnp.float32)
    y = xf * lax.rsqrt(jnp.mean(xf * xf, axis=-1, keepdims=True) + EPS)
    return (y * g.astype(jnp.float32)).astype(x.dtype)

def alibi_slopes(n_heads):
    return jnp.exp2(-8.0 * jnp.arange(1, n_heads + 1, dtype=jnp.float32) / n_heads)

def causal_depthwise_conv(u, w):
    return lax.conv_general_dilated(
        u, w.astype(u.dtype)[:, None, :], window_strides=(1,),
        padding=[(CONV_WIDTH - 1, 0)],
        dimension_numbers=("NWC", "WIO", "NWC"),
        feature_group_count=u.shape[-1])

def dilated_window_attention(q, k, v, window, dilation, slopes):
    B, S, H, Dh = q.shape
    d = dilation
    win = window // dilation
    assert win == QB
    L = S // d
    nb = -(-L // QB)
    Lp = nb * QB

    def to_sub(t):
        t = t.reshape(B, L, d, H, Dh)
        return jnp.pad(t, ((0, 0), (0, Lp - L), (0, 0), (0, 0), (0, 0)))

    qs = (to_sub(q) * (Dh ** -0.5)).reshape(B, nb, QB, d, H, Dh)

    def key_blocks(t):
        tp = jnp.pad(to_sub(t), ((0, 0), (QB, 0), (0, 0), (0, 0), (0, 0)))
        prev = tp[:, :Lp].reshape(B, nb, QB, d, H, Dh)
        cur = tp[:, QB:QB + Lp].reshape(B, nb, QB, d, H, Dh)
        return jnp.concatenate([prev, cur], axis=2)

    kb = key_blocks(k)
    vb = key_blocks(v)

    s = jnp.einsum("bnqrhe,bnkrhe->bnrhqk", qs, kb,
                   preferred_element_type=jnp.float32)
    q_loc = jnp.arange(QB)[:, None] + QB
    k_loc = jnp.arange(2 * QB)[None, :]
    delta = q_loc - k_loc
    key_sub = jnp.arange(nb)[:, None] * QB - QB + jnp.arange(2 * QB)[None, :]
    valid = ((delta >= 0) & (delta <= win))[None] & (key_sub >= 0)[:, None, :]
    bias = -slopes[:, None, None] * (d * delta).astype(jnp.float32)[None]
    s = jnp.where(valid[None, :, None, None], s + bias, -jnp.inf)

    m = jnp.max(s, axis=-1, keepdims=True)
    p = jnp.exp(s - m)
    den = jnp.sum(p, axis=-1)
    lse = m[..., 0] + jnp.log(den)
    o = jnp.einsum("bnrhqk,bnkrhe->bnqrhe", p, vb.astype(jnp.float32))
    o = o / jnp.transpose(den, (0, 1, 4, 2, 3))[..., None]
    o = o.reshape(B, Lp, d, H, Dh)[:, :L].reshape(B, S, H, Dh)
    lse = jnp.transpose(lse, (0, 1, 4, 2, 3)).reshape(B, Lp, d, H)[:, :L].reshape(B, S, H)
    return o, lse

def mixture_of_dilations(q, k, v, slopes):
    outs, lses = [], []
    for window, dilation in ATTN_PATTERNS:
        o, lse = dilated_window_attention(q, k, v, window, dilation, slopes)
        outs.append(o)
        lses.append(lse)
    alpha = jax.nn.softmax(jnp.stack(lses, axis=0), axis=0)
    o = jnp.sum(alpha[..., None] * jnp.stack(outs, axis=0), axis=0)
    return o.astype(q.dtype)

def hybrid_mixer(h, w_in, b_merge, conv_w, w_out_conv, w_out_attn, w_o):
    B, S, _ = h.shape
    proj = jnp.einsum("bsd,dc->bsc", h, w_in)
    splits = np.cumsum([D_CONV] * 4 + [D_ATTN] * 4 + [D_MODEL])
    xc, bg, cg, zc, q, k, v, za, g_conv, g_attn = jnp.split(proj, splits, axis=-1)

    c = causal_depthwise_conv(cg * xc, conv_w)
    y_conv = jnp.einsum("bsc,cd->bsd", jax.nn.silu(zc) * bg * c, w_out_conv)

    shp = (B, S, N_HEADS, HEAD_DIM)
    o = mixture_of_dilations(q.reshape(shp), k.reshape(shp), v.reshape(shp),
                             alibi_slopes(N_HEADS)).reshape(B, S, D_ATTN)
    y_attn = jnp.einsum("bsc,cd->bsd", jax.nn.silu(za) * o, w_out_attn)

    g_conv = jax.nn.sigmoid(g_conv + b_merge[:D_MODEL])
    g_attn = jax.nn.sigmoid(g_attn + b_merge[D_MODEL:])
    merged = g_conv * y_conv + g_attn * y_attn
    return jnp.einsum("bsd,de->bse", merged, w_o)

def first_inputs(seed: int = 0) -> dict:
    key = jax.random.key(seed)
    ks = jax.random.split(key, 10)
    f32 = jnp.float32
    x = jax.random.normal(ks[0], (BATCH, SEQ, D_MODEL), f32)
    norm_g = 1.0 + 0.02 * jax.random.normal(ks[1], (DEPTH, D_MODEL), f32)
    w_in = jax.random.normal(ks[2], (DEPTH, D_MODEL, IN_COLS), f32) * D_MODEL ** -0.5
    b_merge = 0.01 * jax.random.normal(ks[3], (DEPTH, 2 * D_MODEL), f32)
    conv_w = jax.random.normal(ks[4], (DEPTH, CONV_WIDTH, D_CONV), f32) * CONV_WIDTH ** -0.5
    w_out_conv = jax.random.normal(ks[5], (DEPTH, D_CONV, D_MODEL), f32) * D_CONV ** -0.5
    w_out_attn = jax.random.normal(ks[6], (DEPTH, D_ATTN, D_MODEL), f32) * D_ATTN ** -0.5
    w_o = jax.random.normal(ks[7], (DEPTH, D_MODEL, D_MODEL), f32) * D_MODEL ** -0.5
    final_g = 1.0 + 0.02 * jax.random.normal(ks[8], (D_MODEL,), f32)
    return {"x": x, "norm_g": norm_g, "w_in": w_in, "b_merge": b_merge,
            "conv_w": conv_w, "w_out_conv": w_out_conv, "w_out_attn": w_out_attn,
            "w_o": w_o, "final_g": final_g}

def first_block(x, norm_g, w_in, b_merge, conv_w, w_out_conv, w_out_attn, w_o, final_g):
    h = x
    for layer in range(DEPTH):
        u = rms_norm(h, norm_g[layer])
        h = h + hybrid_mixer(u, w_in[layer], b_merge[layer], conv_w[layer],
                             w_out_conv[layer], w_out_attn[layer], w_o[layer])
    return rms_norm(h, final_g)


DEPTH_2 = 2

N_MEM = 256
MAIN_W = 3 * D_MODEL // 4
N_HEADS_2 = MAIN_W // HEAD_DIM
MEM_HEADS = 4
MEM_W = D_MODEL - MAIN_W
MEM_HEAD_DIM = MEM_W // MEM_HEADS
MIX_W = MAIN_W + MEM_W

NSA_KV_HEADS = 1
NSA_KV_W = NSA_KV_HEADS * HEAD_DIM
CMP_LEN = 32
CMP_STRIDE = 16
CMP_HIDDEN = 4 * HEAD_DIM
SLC_BLOCK = 64
SLC_TOPK = 16
WINDOW = 512
NSA_Q_CHUNK = 64
FORCE_SCORE = 1.0e4

MOBA_BLOCK = 256
MOBA_TOPK = 3
MOBA_Q_CHUNK = 8

REL_BUCKETS = 32
REL_MAX_DIST = 128

D_FF = 2816
CONV_W = 3

N_A = DEPTH_2 // 2
N_B = DEPTH_2 - N_A
ALPHA = (2.0 * DEPTH_2) ** 0.25
BETA = (8.0 * DEPTH_2) ** -0.25
LN_EPS = 1e-5
NEG_INF = -1e30
TINY = 1e-30

A_IN_SIZES = (MAIN_W, NSA_KV_W, NSA_KV_W, NSA_KV_W, NSA_KV_W, NSA_KV_W, NSA_KV_W, 3 * N_HEADS_2, MEM_W)
A_IN = sum(A_IN_SIZES)
B_IN_SIZES = (MAIN_W, MEM_W)
B_IN = sum(B_IN_SIZES)


def split_cols(h, sizes):
    return jnp.split(h, np.cumsum(sizes)[:-1].tolist(), axis=-1)

def layer_norm(x, g, b):
    xf = x.astype(jnp.float32)
    mu = xf.mean(-1, keepdims=True)
    var = jnp.square(xf - mu).mean(-1, keepdims=True)
    return ((xf - mu) * lax.rsqrt(var + LN_EPS) * g + b).astype(x.dtype)

def rel_bucket(dist):
    n = jnp.maximum(dist, 0)
    max_exact = REL_BUCKETS // 2
    nf = jnp.maximum(n, 1).astype(jnp.float32)
    large = max_exact + (jnp.log(nf / max_exact) / math.log(REL_MAX_DIST / max_exact)
                         * (REL_BUCKETS - max_exact)).astype(jnp.int32)
    large = jnp.minimum(large, REL_BUCKETS - 1)
    return jnp.where(n < max_exact, n, large)

def masked_softmax(logits, mask):
    logits = jnp.where(mask, logits, NEG_INF)
    m = jnp.max(logits, -1, keepdims=True)
    p = jnp.where(mask, jnp.exp(logits - m), 0.0)
    return p / jnp.maximum(p.sum(-1, keepdims=True), TINY)

def cmp_slc_overlap(n_cmp, n_slc):
    start = np.arange(n_cmp) * CMP_STRIDE
    end = start + CMP_LEN
    bs = np.arange(n_slc) * SLC_BLOCK
    m = (start[:, None] < bs[None, :] + SLC_BLOCK) & (end[:, None] > bs[None, :])
    return m.astype(np.float32)

def nsa_compress(k, pe, w1, w2):
    B, S, G, dh = k.shape
    n_cmp = (S - CMP_LEN) // CMP_STRIDE + 1
    idx = (np.arange(n_cmp, dtype=np.int32)[:, None] * CMP_STRIDE
           + np.arange(CMP_LEN, dtype=np.int32)[None, :])
    blocks = k[:, idx] + pe[:, None, :]
    blocks = blocks.transpose(0, 1, 3, 2, 4).reshape(B, n_cmp, G, CMP_LEN * dh)
    return jax.nn.gelu(blocks @ w1) @ w2

def nsa_attention(q, k_cmp, v_cmp, k_slc, v_slc, k_win, v_win, gates, rel_bias):
    B, S, H, dh = q.shape
    G = k_slc.shape[2]
    hpg = H // G
    n_cmp = k_cmp.shape[1]
    n_slc = S // SLC_BLOCK
    top = min(SLC_TOPK, n_slc)
    n_sel = top * SLC_BLOCK
    QC = NSA_Q_CHUNK
    KW = WINDOW + QC
    scale = dh ** -0.5

    cmp_end = jnp.asarray(np.arange(n_cmp) * CMP_STRIDE + CMP_LEN - 1, jnp.int32)
    overlap = jnp.asarray(cmp_slc_overlap(n_cmp, n_slc))
    blk_ids = jnp.arange(n_slc, dtype=jnp.int32)
    offs = jnp.arange(SLC_BLOCK, dtype=jnp.int32)
    k_blk = k_slc.reshape(B, n_slc, SLC_BLOCK, G, dh).transpose(0, 3, 1, 2, 4).reshape(B, G, n_slc, SLC_BLOCK * dh)
    v_blk = v_slc.reshape(B, n_slc, SLC_BLOCK, G, dh).transpose(0, 3, 1, 2, 4).reshape(B, G, n_slc, SLC_BLOCK * dh)
    k_win_pad = jnp.pad(k_win, ((0, 0), (WINDOW, 0), (0, 0), (0, 0)))
    v_win_pad = jnp.pad(v_win, ((0, 0), (WINDOW, 0), (0, 0), (0, 0)))
    table_g = rel_bias.reshape(REL_BUCKETS, G, hpg)
    g_idx = jnp.arange(G)[None, None, :, None]

    def head_bias(bucket):
        return rel_bias[bucket].reshape(bucket.shape + (G, hpg)).transpose(0, 2, 3, 1)

    def chunk(c):
        t0 = c * QC
        t = t0 + jnp.arange(QC, dtype=jnp.int32)
        qc = lax.dynamic_slice_in_dim(q, t0, QC, axis=1).reshape(B, QC, G, hpg, dh)
        gc = lax.dynamic_slice_in_dim(gates, t0, QC, axis=1).reshape(B, QC, G, hpg, 3)

        dist_c = t[:, None] - cmp_end[None, :]
        lg = jnp.einsum('bqgjd,bngd->bqgjn', qc, k_cmp).astype(jnp.float32) * scale + head_bias(rel_bucket(dist_c))
        p_c = masked_softmax(lg, (dist_c >= 0)[None, :, None, None, :])
        o_c = jnp.einsum('bqgjn,bngd->bqgjd', p_c, v_cmp)

        imp = jnp.einsum('bqgjn,ns->bqgs', p_c, overlap)
        cur = t // SLC_BLOCK
        bid = blk_ids[None, :]
        eligible = bid <= cur[:, None]
        forced = (bid == 0) | (bid == cur[:, None]) | (bid == cur[:, None] - 1)
        score = jnp.where(eligible, jnp.where(forced, FORCE_SCORE, 0.0), NEG_INF)[None, :, None, :] + imp
        _, sel = lax.top_k(score, top)
        idx = sel.transpose(0, 2, 1, 3).reshape(B, G, QC * top, 1)
        ks = jnp.take_along_axis(k_blk, idx, axis=2).reshape(B, G, QC, n_sel, dh)
        vs = jnp.take_along_axis(v_blk, idx, axis=2).reshape(B, G, QC, n_sel, dh)
        key_pos = (sel[..., None] * SLC_BLOCK + offs).reshape(B, QC, G, n_sel)
        dist_s = t[None, :, None, None] - key_pos
        bias_s = jnp.swapaxes(table_g[rel_bucket(dist_s), g_idx], -1, -2)
        lg = jnp.einsum('bqgjd,bgqkd->bqgjk', qc, ks).astype(jnp.float32) * scale + bias_s
        p_s = masked_softmax(lg, (dist_s >= 0)[:, :, :, None, :])
        o_s = jnp.einsum('bqgjk,bgqkd->bqgjd', p_s, vs)

        kw = lax.dynamic_slice_in_dim(k_win_pad, t0, KW, axis=1)
        vw = lax.dynamic_slice_in_dim(v_win_pad, t0, KW, axis=1)
        pos_w = t0 - WINDOW + jnp.arange(KW, dtype=jnp.int32)
        dist_w = t[:, None] - pos_w[None, :]
        mask_w = (pos_w[None, :] >= 0) & (dist_w >= 0) & (dist_w < WINDOW)
        lg = jnp.einsum('bqgjd,bkgd->bqgjk', qc, kw).astype(jnp.float32) * scale + head_bias(rel_bucket(dist_w))
        p_w = masked_softmax(lg, mask_w[None, :, None, None, :])
        o_w = jnp.einsum('bqgjk,bkgd->bqgjd', p_w, vw)

        o = gc[..., 0:1] * o_c + gc[..., 1:2] * o_s + gc[..., 2:3] * o_w
        return o.reshape(B, QC, H * dh).astype(q.dtype)

    out = lax.map(chunk, jnp.arange(S // QC, dtype=jnp.int32))
    return out.transpose(1, 0, 2, 3).reshape(B, S, H * dh)

def moba_shared_kv(x, w_kv):
    B, S, _ = x.shape
    k, v = jnp.split(x @ w_kv, 2, axis=-1)
    nb = -(-S // MOBA_BLOCK)
    pad = nb * MOBA_BLOCK - S
    k = jnp.pad(k.reshape(B, S, N_HEADS_2, HEAD_DIM), ((0, 0), (0, pad), (0, 0), (0, 0)))
    v = jnp.pad(v.reshape(B, S, N_HEADS_2, HEAD_DIM), ((0, 0), (0, pad), (0, 0), (0, 0)))
    k_blocks = k.reshape(B, nb, MOBA_BLOCK, N_HEADS_2, HEAD_DIM)
    k_mean = k_blocks.astype(jnp.float32).mean(2).astype(k.dtype)
    k_blk = k_blocks.transpose(0, 3, 1, 2, 4).reshape(B, N_HEADS_2, nb, MOBA_BLOCK * HEAD_DIM)
    v_blk = v.reshape(B, nb, MOBA_BLOCK, N_HEADS_2, HEAD_DIM).transpose(0, 3, 1, 2, 4).reshape(B, N_HEADS_2, nb, MOBA_BLOCK * HEAD_DIM)
    return k_mean, k_blk, v_blk

def moba_attention(q, k_mean, k_blk, v_blk, rel_bias):
    B, S, H, dh = q.shape
    nb = k_mean.shape[1]
    top = min(MOBA_TOPK, nb - 1)
    n_p = top * MOBA_BLOCK
    QC = MOBA_Q_CHUNK
    scale = dh ** -0.5
    blk_ids = jnp.arange(nb, dtype=jnp.int32)
    offs = jnp.arange(MOBA_BLOCK, dtype=jnp.int32)
    h_idx = jnp.arange(H)[None, :, None, None]

    def chunk(c):
        t0 = c * QC
        t = t0 + jnp.arange(QC, dtype=jnp.int32)
        cb = t0 // MOBA_BLOCK
        qc = lax.dynamic_slice_in_dim(q, t0, QC, axis=1)
        ko = lax.dynamic_index_in_dim(k_blk, cb, axis=2, keepdims=False).reshape(B, H, MOBA_BLOCK, dh)
        vo = lax.dynamic_index_in_dim(v_blk, cb, axis=2, keepdims=False).reshape(B, H, MOBA_BLOCK, dh)
        dist_o = t[:, None] - (cb * MOBA_BLOCK + offs)[None, :]
        lg_o = (jnp.einsum('bqhd,bhkd->bhqk', qc, ko).astype(jnp.float32) * scale
                + rel_bias[rel_bucket(dist_o)].transpose(2, 0, 1))
        mask_o = jnp.broadcast_to(dist_o >= 0, lg_o.shape)
        if top == 0:
            p = masked_softmax(lg_o, mask_o)
            o = jnp.einsum('bhqk,bhkd->bqhd', p, vo)
        else:
            gate = jnp.einsum('bqhd,bnhd->bhqn', qc, k_mean).astype(jnp.float32)
            gate = jnp.where(blk_ids < cb, gate, NEG_INF)
            _, sel = lax.top_k(gate, top)
            idx = sel.reshape(B, H, QC * top, 1)
            kp = jnp.take_along_axis(k_blk, idx, axis=2).reshape(B, H, QC, n_p, dh)
            vp = jnp.take_along_axis(v_blk, idx, axis=2).reshape(B, H, QC, n_p, dh)
            pos_p = (sel[..., None] * MOBA_BLOCK + offs).reshape(B, H, QC, n_p)
            lg_p = (jnp.einsum('bqhd,bhqkd->bhqk', qc, kp).astype(jnp.float32) * scale
                    + rel_bias[rel_bucket(t[None, None, :, None] - pos_p), h_idx])
            mask_p = pos_p < cb * MOBA_BLOCK
            p = masked_softmax(jnp.concatenate([lg_p, lg_o], -1), jnp.concatenate([mask_p, mask_o], -1))
            o = (jnp.einsum('bhqk,bhqkd->bqhd', p[..., :n_p], vp)
                 + jnp.einsum('bhqk,bhkd->bqhd', p[..., n_p:], vo))
        return o.reshape(B, QC, H * dh).astype(q.dtype)

    out = lax.map(chunk, jnp.arange(S // QC, dtype=jnp.int32))
    return out.transpose(1, 0, 2, 3).reshape(B, S, H * dh)

def memory_attention(qm, mem, w_mem_kv):
    B, M, _ = mem.shape
    km, vm = jnp.split(mem @ w_mem_kv, 2, axis=-1)
    km = km.reshape(B, M, MEM_HEADS, MEM_HEAD_DIM)
    vm = vm.reshape(B, M, MEM_HEADS, MEM_HEAD_DIM)
    lg = jnp.einsum('bshd,bmhd->bhsm', qm, km).astype(jnp.float32) * (MEM_HEAD_DIM ** -0.5)
    p = jax.nn.softmax(lg, axis=-1)
    o = jnp.einsum('bhsm,bmhd->bshd', p, vm)
    return o.reshape(qm.shape[0], qm.shape[1], MEM_W).astype(qm.dtype)

def conv_ffn(x, w_in, conv_w, conv_b, w_out):
    S = x.shape[1]
    a, b = jnp.split(x @ w_in, 2, axis=-1)
    a_pad = jnp.pad(a, ((0, 0), (CONV_W - 1, 0), (0, 0)))
    a = sum(conv_w[k] * a_pad[:, k:k + S] for k in range(CONV_W)) + conv_b
    return (jax.nn.gelu(a) * b) @ w_out

def second_inputs(seed: int = 0) -> dict:
    key = jax.random.key(seed)
    keys = iter(jax.random.split(key, 32))

    def nrm(shape, scale):
        return jax.random.normal(next(keys), shape, jnp.float32) * scale

    L = CMP_LEN * HEAD_DIM
    return {
        'x': nrm((BATCH, SEQ, D_MODEL), 1.0),
        'mem': nrm((BATCH, N_MEM, D_MODEL), 1.0),
        'rel_bias': nrm((REL_BUCKETS, N_HEADS_2), 0.5),
        'a_w_in': nrm((N_A, D_MODEL, A_IN), D_MODEL ** -0.5),
        'a_cmp_pe_k': nrm((N_A, CMP_LEN, HEAD_DIM), 0.1),
        'a_cmp_w1_k': nrm((N_A, L, CMP_HIDDEN), L ** -0.5),
        'a_cmp_w2_k': nrm((N_A, CMP_HIDDEN, HEAD_DIM), CMP_HIDDEN ** -0.5),
        'a_cmp_pe_v': nrm((N_A, CMP_LEN, HEAD_DIM), 0.1),
        'a_cmp_w1_v': nrm((N_A, L, CMP_HIDDEN), L ** -0.5),
        'a_cmp_w2_v': nrm((N_A, CMP_HIDDEN, HEAD_DIM), CMP_HIDDEN ** -0.5),
        'a_w_mem_kv': nrm((N_A, D_MODEL, 2 * MEM_W), D_MODEL ** -0.5),
        'a_w_out': nrm((N_A, MIX_W, D_MODEL), BETA * MIX_W ** -0.5),
        'shared_w_kv': nrm((D_MODEL, 2 * MAIN_W), D_MODEL ** -0.5),
        'b_w_in': nrm((N_B, D_MODEL, B_IN), D_MODEL ** -0.5),
        'b_w_mem_kv': nrm((N_B, D_MODEL, 2 * MEM_W), D_MODEL ** -0.5),
        'b_w_out': nrm((N_B, MIX_W, D_MODEL), BETA * MIX_W ** -0.5),
        'ln1_g': 1.0 + nrm((DEPTH_2, D_MODEL), 0.02),
        'ln1_b': nrm((DEPTH_2, D_MODEL), 0.02),
        'ln2_g': 1.0 + nrm((DEPTH_2, D_MODEL), 0.02),
        'ln2_b': nrm((DEPTH_2, D_MODEL), 0.02),
        'ffn_w_in': nrm((DEPTH_2, D_MODEL, 2 * D_FF), D_MODEL ** -0.5),
        'ffn_conv_w': nrm((DEPTH_2, CONV_W, D_FF), CONV_W ** -0.5),
        'ffn_conv_b': nrm((DEPTH_2, D_FF), 0.02),
        'ffn_w_out': nrm((DEPTH_2, D_FF, D_MODEL), BETA * D_FF ** -0.5),
    }

def second_block(x, mem, rel_bias, a_w_in, a_cmp_pe_k, a_cmp_w1_k, a_cmp_w2_k, a_cmp_pe_v, a_cmp_w1_v,
              a_cmp_w2_v, a_w_mem_kv, a_w_out, shared_w_kv, b_w_in, b_w_mem_kv, b_w_out,
              ln1_g, ln1_b, ln2_g, ln2_b, ffn_w_in, ffn_conv_w, ffn_conv_b, ffn_w_out):
    B, S, _ = x.shape

    def heads(z):
        return z.reshape(B, S, -1, HEAD_DIM)

    k_mean = k_blk = v_blk = None
    for layer in range(DEPTH_2):
        if layer < N_A:
            i = layer
            q, kc, vc, ks, vs, kw, vw, g, qm = split_cols(x @ a_w_in[i], A_IN_SIZES)
            k_cmp = nsa_compress(heads(kc), a_cmp_pe_k[i], a_cmp_w1_k[i], a_cmp_w2_k[i])
            v_cmp = nsa_compress(heads(vc), a_cmp_pe_v[i], a_cmp_w1_v[i], a_cmp_w2_v[i])
            gates = jax.nn.sigmoid(g).reshape(B, S, N_HEADS_2, 3)
            o_main = nsa_attention(heads(q), k_cmp, v_cmp, heads(ks), heads(vs), heads(kw), heads(vw),
                                   gates, rel_bias)
            w_mem_kv, w_out = a_w_mem_kv[i], a_w_out[i]
        else:
            if layer == N_A:
                k_mean, k_blk, v_blk = moba_shared_kv(x, shared_w_kv)
            i = layer - N_A
            q, qm = split_cols(x @ b_w_in[i], B_IN_SIZES)
            o_main = moba_attention(heads(q), k_mean, k_blk, v_blk, rel_bias)
            w_mem_kv, w_out = b_w_mem_kv[i], b_w_out[i]
        o_mem = memory_attention(qm.reshape(B, S, MEM_HEADS, MEM_HEAD_DIM), mem, w_mem_kv)
        mix = jnp.concatenate([o_main, o_mem], axis=-1) @ w_out
        x = layer_norm(ALPHA * x + mix, ln1_g[layer], ln1_b[layer])
        ffn = conv_ffn(x, ffn_w_in[layer], ffn_conv_w[layer], ffn_conv_b[layer], ffn_w_out[layer])
        x = layer_norm(ALPHA * x + ffn, ln2_g[layer], ln2_b[layer])
    return x


def setup_inputs(seed=0):
    out = dict(first_inputs(seed))
    for name, value in second_inputs(seed + 1).items():
        if name != "x":
            out[name + "_2"] = value
    return out


def reference(
    x, norm_g, w_in, b_merge, conv_w, w_out_conv, w_out_attn, w_o, final_g, mem_2, rel_bias_2,
    a_w_in_2, a_cmp_pe_k_2, a_cmp_w1_k_2, a_cmp_w2_k_2, a_cmp_pe_v_2, a_cmp_w1_v_2,
    a_cmp_w2_v_2, a_w_mem_kv_2, a_w_out_2, shared_w_kv_2, b_w_in_2, b_w_mem_kv_2, b_w_out_2,
    ln1_g_2, ln1_b_2, ln2_g_2, ln2_b_2, ffn_w_in_2, ffn_conv_w_2, ffn_conv_b_2, ffn_w_out_2,
):
    x = first_block(
        x, norm_g, w_in, b_merge, conv_w, w_out_conv, w_out_attn, w_o, final_g,
    )
    return second_block(
        x, mem_2, rel_bias_2, a_w_in_2, a_cmp_pe_k_2, a_cmp_w1_k_2, a_cmp_w2_k_2, a_cmp_pe_v_2,
        a_cmp_w1_v_2, a_cmp_w2_v_2, a_w_mem_kv_2, a_w_out_2, shared_w_kv_2, b_w_in_2,
        b_w_mem_kv_2, b_w_out_2, ln1_g_2, ln1_b_2, ln2_g_2, ln2_b_2, ffn_w_in_2, ffn_conv_w_2,
        ffn_conv_b_2, ffn_w_out_2,
    )


_drawn_inputs = setup_inputs


def setup_inputs(seed=0):
    import zlib

    import numpy as np

    out = dict(_drawn_inputs(seed))
    spreads = {}
    factors = {'norm_g': 3.77,
     'b_merge': 8.0,
     'final_g': 2.834,
     'a_cmp_pe_k_2': 8.0,
     'a_cmp_w1_k_2': 3.04,
     'a_cmp_w2_k_2': 3.168,
     'a_cmp_pe_v_2': 5.93,
     'a_w_mem_kv_2': 2.859,
     'b_w_mem_kv_2': 2.878,
     'ffn_conv_b_2': 8.0}
    for name, (base, spread) in spreads.items():
        noise = np.random.default_rng([zlib.crc32(name.encode()), seed]).standard_normal(out[name].shape)
        drawn = base * np.exp(spread * noise) if base else spread * noise
        out[name] = jnp.asarray(drawn.astype(out[name].dtype))
    for name, factor in factors.items():
        out[name] = (out[name] * factor).astype(out[name].dtype)
    return out
```

```python
from contextlib import ExitStack

import numpy as np

import concourse.bass as bass
from concourse import mybir

F32 = mybir.dt.float32
F32R = mybir.dt.float32r
BF16 = mybir.dt.bfloat16
ALU = mybir.AluOpType
ACT = mybir.ActivationFunctionType
AX = mybir.AxisListType

P = 128
T = 256
NT = T // P
D = 1024
KT = D // P
DH = 64
PAIRS1 = 8
PAIRS2 = 6
NCMP = 15
CMP_STRIDE, CMP_LEN = 16, 32
FT = 2816 // P
EPS_RMS, EPS_LN = 1e-6, 1e-5
ALPHA = 4.0 ** 0.25
TINY = 1e-30
MASKED = 1e30
NO_KEY = 1e20
BIASW = 384
RELW = 512
CAUSAL = P + T

RING1, RING = 5, 3
PER1 = 10
B_MIX = PAIRS1 * PER1
B_NSA = B_MIX + 3 * KT
NSA_FRONT = 12
B_PAIRS = B_NSA + NSA_FRONT
B_ROWS0 = B_PAIRS + PAIRS2 + 6
B_KM = B_ROWS0 + KT
B_FFN0 = B_KM + 2
B_VM = B_FFN0 + 3 * FT
B_MOBA = B_VM + 2
B_ROWS1 = B_MOBA + 3 * PAIRS2 + 2
B_FFN1 = B_ROWS1 + KT
N_BLOCKS = B_FFN1 + 3 * FT


def slot_of(b):
    return b % RING1 if b < B_MIX else (b - B_MIX) % RING


def loads_of(b):
    return b // RING1 + 1 if b < B_MIX else PAIRS1 * PER1 // RING1 + (b - B_MIX) // RING + 1


def next_in_slot(b):
    if b < B_MIX:
        n = b + RING1
        if n < B_MIX:
            return n
        return n if n - B_MIX < RING else None
    return b + RING if b + RING < N_BLOCKS else None


class Chain:

    def __init__(self, engine, sem, per=0):
        self.engine, self.sem, self.per, self.n, self.i = engine, sem, per, 0, 0

    def begin(self, i):
        self.i, self.n = i, 0

    def link(self, instruction):
        self.n += 1
        instruction.then_inc(self.sem, 1)
        self.engine.wait_ge(self.sem, self.i * self.per + self.n if self.per else self.n)

    def end(self):
        assert self.n == self.per, self.n


def build_program(nc, a):
    ctx = ExitStack()
    with ctx:
        def sb(name, shape, dt=F32):
            return ctx.enter_context(nc.sbuf_tensor("sb_" + name, shape, dt))

        def sem(name):
            return ctx.enter_context(nc.semaphore(name))

        bank = [ctx.enter_context(nc.psum_tensor(f"bank{n}", [P, 512], F32)) for n in range(4)]
        ysum = [ctx.enter_context(nc.psum_tensor(f"ysum{t}", [P, D], F32)) for t in range(NT)]
        bank += [ysum[t][:, n * 512:(n + 1) * 512] for t in range(NT) for n in range(2)]
        rel_rows = nc.dram_tensor("rel_rows", (2 * PAIRS2, P, RELW), F32, kind="Internal").ap()

        raw = [sb(f"raw{n}", [P, KT, P]) for n in range(RING1)]
        wh = [sb(f"wh{n}", [P, KT, P], F32R) for n in range(RING1)]
        wl = [sb(f"wl{n}", [P, KT, P], F32R) for n in range(RING1)]
        x_tok = sb("x_tok", [P, NT, D])
        z = sb("z", [P, NT, D])
        xh = sb("xh", [P, KT, T], F32R)
        xl = sb("xl", [P, KT, T], F32R)
        gb = sb("gb", [P, 2, D])
        gbt = sb("gbt", [P, 10, KT])
        mixh = sb("mixh", [P, 2, KT, T], F32R)
        mixl = sb("mixl", [P, 2, KT, T], F32R)
        gates = sb("gates", [P, 2, KT, T])
        oh, ol = mixh[:, 0], mixl[:, 0]
        memh, meml = mixh[:, 1], mixl[:, 1]
        memf = gates[:, 0]
        qall = gates[:, 1]
        mh = sb("mh", [P, T], F32R)
        ml = sb("ml", [P, T], F32R)
        bias = sb("bias", [P, 2, BIASW])
        q_s = sb("q_s", [P, T])
        k_s = sb("k_s", [P, T])
        v_s = sb("v_s", [P, NT, P])
        ks2 = sb("ks2", [P, T])
        kw2 = sb("kw2", [P, T])
        kc2 = sb("kc2", [P, 16])
        vc = sb("vc", [16, DH])
        g_nsa = sb("g_nsa", [P, NT, 36])
        km = sb("km", [P, 2, T])
        vm = sb("vm", [P, NT, T])
        blkh = sb("blkh", [P, 2, 16, 16], F32R)
        blkl = sb("blkl", [P, 2, 16, 16], F32R)
        hid = sb("hid", [P, 2, 2, 16])
        w2 = sb("w2", [P, 2, 2, DH])
        pe_kv = sb("pe_kv", [P, 2, 16])
        sc = sb("sc", [P, 2, 2, 512])
        pr = sb("pr", [P, 2, 2, 512])
        pt = sb("pt", [P, 2, 2, 512])
        scc = sb("scc", [P, 2, NT, 16])
        prc = sb("prc", [P, 2, NT, 16])
        ptc = sb("ptc", [16, 2, T])
        mx = sb("mx", [P, 12])
        den = sb("den", [P, 12])
        deng = sb("deng", [P, 12])
        rden = sb("rden", [P, 12])
        rg = sb("rg", [P, 12])
        t_a = sb("t_a", [P, T])
        t_b = sb("t_b", [P, T])
        t_c = sb("t_c", [P, T])
        t_d = sb("t_d", [P, T])
        t_e = sb("t_e", [P, T])
        t_f = sb("t_f", [P, T])
        t_g = sb("t_g", [P, T])
        ident = sb("ident", [P, P])
        zeros = sb("zeros", [P, 512], BF16)
        relb = sb("relb", [33, 2 * PAIRS2])
        relf = sb("relf", [2 * PAIRS2, RELW])
        convw = sb("convw", [P, KT, 4])
        convf = sb("convf", [P, 2, FT, 4])
        bm = sb("bm", [P, 2, KT])
        bmh = sb("bmh", [P, 2, KT])
        st = sb("st", [P, 16])
        half = sb("half", [P, 1])
        xf = pt[:, 1, :, :].rearrange("p a (s t) -> p (a s) t", s=2)
        blk = pt[:, 0, 0, :].rearrange("p (s l n) -> p s l n", s=2, l=16)
        onehot = sc[0:33, 0, 0, :]
        sq = pr[:, 0, :, :].rearrange("p h c -> p (h c)")

        landed = [sem(f"landed{n}") for n in range(RING1)]
        split_h, split_l, used = sem("split_h"), sem("split_l"), sem("used")
        gains_in, kv_free = sem("gains_in"), sem("kv_free")
        consts_in, ident_up, set_up = sem("consts_in"), sem("ident_up"), sem("set_up")
        dch, ach, pch = sem("dve_chain"), sem("act_chain"), sem("pool_chain")
        dch1, dch2, dch3, dch5 = sem("dve_c1"), sem("dve_c2"), sem("dve_c3"), sem("dve_c5")
        dchf = [sem("dve_cf0"), sem("dve_cf1")]
        rel_ps, rel_sb, rel_out = sem("rel_ps"), sem("rel_sb"), sem("rel_out")
        mem_in, mem_h, mem_l = sem("mem_in"), sem("mem_h"), sem("mem_l")
        out_done, seen = sem("out_done"), sem("scores_seen")
        S = {}
        norms = ["n0", "n1", "n2", "n3", "n4", "n5"]
        per_norm = {"sum": 2, "mean": 2, "var": 2, "rstd": 2, "z": 2, "x": 2, "half": 1, "off": 2,
                    "turned": KT, "xf": 6, "xf_act": 2, "xh": KT, "xl_dve": 4, "xl_pool": 4}
        first_norm = {"sum": 1, "mean": 2, "x": 1, "half": 1, "off": 5}
        for what in per_norm:
            one = sem(f"norm_{what}")
            for nm in norms:
                S[nm, what] = one
        x_in, gb_in = sem("x_in"), sem("gb_in")

        def norm_wait(engine, nm, what, count):
            before = norms.index(nm) - first_norm.get(what, 0)
            engine.wait_ge(S[nm, what], before * per_norm[what] + count)

        for ph in ("p1", "p3", "p5", "pm3", "pm5"):
            for what in ("s", "max", "exp", "prob", "turned", "pt_act", "pt_dve", "o", "oh", "ol"):
                S[ph, what] = sem(f"{ph}_{what}")
        for ph in ("p1", "p3", "p5"):
            for what in ("bias_in", "free_act", "free_dve"):
                S[ph, what] = sem(f"{ph}_{what}")
        for what in ("xc", "tz", "yc", "yc_h", "ta", "ya", "ya_h"):
            S["p1", what] = sem(f"p1_{what}")
        for ph in ("p2", "f0", "f1"):
            for what in ("free_a", "free_b", "m", "mh", "ml", "base", "g"):
                S[ph, what] = sem(f"{ph}_{what}")
        for what in ("blk", "blkh", "blkl", "hid", "w2", "cmp", "q", "gate", "fill", "parts"):
            S["p3", what] = sem(f"p3_{what}")

        block = ctx.enter_context(nc.Block())

        def s384(t):
            return slice(0, P) if t == 0 else slice(P, CAUSAL)

        @block.sync
        def _(sp):
            def load(b, slot):
                sp.dma_start(raw[slot][:, :, :], a["stream"][bass.ds(b, 1)].rearrange(
                    "a p (k c) -> p (a k) c", k=KT)).then_inc(landed[slot], 16)

            for t in range(NT):
                sp.dma_start(x_tok[:, t, :], a["x"][0, t * P:(t + 1) * P, :]).then_inc(x_in, 16)
            sp.dma_start(gbt[:, :, :], a["gains_t"]).then_inc(gains_in, 16)
            for b in range(RING1):
                load(b, slot_of(b))
            sp.dma_start(convw[:, :, :], a["conv_t"]).then_inc(consts_in, 16)
            sp.dma_start(bm[:, :, :], a["b_merge_t"]).then_inc(consts_in, 16)
            sp.dma_start(onehot[:, :], a["distance_hot"]).then_inc(consts_in, 16)
            sp.dma_start(relb[0:32, :], a["rel_bias_2"]).then_inc(consts_in, 16)
            sp.dma_start(convf[:, :, :, :], a["conv_f_t"]).then_inc(consts_in, 16)
            sp.dma_start(pe_kv[:, :, :], a["pe_t"]).then_inc(consts_in, 16)
            sp.dma_start(w2[:, :, :, :], a["w2_t"]).then_inc(consts_in, 16)
            with sp.Fori(1, B_MIX // RING1) as i:
                for n in range(RING1):
                    sp.wait_ge(split_l, i * RING1 + (n - RING1 + 1))
                    load(i * RING1 + n, n)
            for b in range(B_MIX, B_MIX + RING):
                sp.wait_ge(split_l, b - RING1 + 1)
                load(b, slot_of(b))
            rest = N_BLOCKS - B_MIX
            with sp.Fori(1, rest // RING) as i:
                for n in range(RING):
                    sp.wait_ge(split_l, i * RING + (B_MIX + n - RING + 1))
                    load(i * RING + (B_MIX + n), n)
            for b in range(B_MIX + rest // RING * RING, N_BLOCKS):
                sp.wait_ge(split_l, b - RING + 1)
                load(b, slot_of(b))
            for t in range(NT):
                norm_wait(sp, "n5", "z", t + 1)
                sp.dma_start(a["out"][0, t * P:(t + 1) * P, :], x_tok[:, t, :]).then_inc(out_done, 16)
            sp.wait_ge(out_done, 16 * NT)

        @block.gpsimd
        def _(pool):
            chain = Chain(pool, pch)
            pool.memset(half[:, :], -0.5).then_inc(set_up, 1)
            chain.link(pool.memset(ident[:, :], 0.0))
            pool.affine_select(out=ident[:, :], in_=ident[:, :], compare_op=ALU.not_equal, fill=1.0,
                               base=0, pattern=[[-1, P]], channel_multiplier=1).then_inc(ident_up, 1)
            pool.memset(zeros[:, :], 0.0).then_inc(set_up, 1)
            pool.wait_ge(set_up, 5)

            def rstd(nm, t, eps):
                norm_wait(pool, nm, "var", t + 1)
                chain.link(pool.tensor_scalar(st[:, 8 + t:9 + t], st[:, 6 + t:7 + t], 1.0 / D, eps,
                                              ALU.mult, ALU.add))
                pool.tensor_tensor(st[:, 10 + t:11 + t], st[:, 8 + t:9 + t], half[:, :],
                                   ALU.pow).then_inc(S[nm, "rstd"], 1)

            def load_gb(nm, gain, shift):
                pool.dma_start(gb[:, 0, :], gain.partition_broadcast(P)).then_inc(gb_in, 16)
                if shift is not None:
                    pool.dma_start(gb[:, 1, :], shift.partition_broadcast(P)).then_inc(gb_in, 16)

            def tail(nm, shift):
                pool.wait_ge(gb_in, 16 + 32 * (norms.index(nm) - 1))
                for t in range(NT):
                    norm_wait(pool, nm, "z", t + 1)
                    last = pool.tensor_tensor(x_tok[:, t, :], z[:, t, :], gb[:, 0, :], ALU.mult)
                    if shift:
                        chain.link(last)
                        last = pool.tensor_tensor(x_tok[:, t, :], x_tok[:, t, :], gb[:, 1, :], ALU.add)
                    last.then_inc(S[nm, "x"], 1)

            def low_odd(nm):
                for k in range(1, KT, 2):
                    norm_wait(pool, nm, "xh", k + 1)
                    pool.tensor_tensor(xl[:, k, :], xf[:, k % 4, :], xh[:, k, :].bitcast(F32), ALU.subtract
                                       ).then_inc(S[nm, "xl_pool"], 1)

            for t in range(NT):
                rstd("n0", t, EPS_RMS)
            low_odd("n0")
            load_gb("n1", a["final_g"], None)
            pool.wait_ge(rel_sb, 1)
            pool.dma_start(rel_rows, relf[:, :].unsqueeze(1).to_broadcast([2 * PAIRS2, P, RELW])
                           ).then_inc(rel_out, 16)

            def alibi(i):
                if not isinstance(i, int) or i > 0:
                    pool.wait_ge(S["p1", "max"], i * 4)
                pool.dma_start(bias[:, :, 0:T], a["alibi"][bass.ds(i, 1)].rearrange(
                    "a p (h c) -> p (a h) c", h=2)).then_inc(S["p1", "bias_in"], 16)

            alibi(0)
            with pool.Fori(1, PAIRS1) as i:
                alibi(i)
            pool.wait_ge(rel_out, 16)

            def relative(ph, i, per):
                if not isinstance(i, int) or i > 0:
                    pool.wait_ge(S[ph, "max"], i * per)
                src = bass.AP(rel_rows.tensor, 0, [[RELW - 1, P], [P * RELW, 2 * PAIRS2], [1, BIASW]])
                pool.dma_start(bias[:, :, :], src_pair(src, i)).then_inc(S[ph, "bias_in"], 16)

            def src_pair(src, i):
                base = bass.AP(rel_rows.tensor, P - 1,
                               [[RELW - 1, P], [P * RELW, 2 * PAIRS2], [1, BIASW]])
                return base[:, bass.ds(i * 2, 2), :]

            pool.wait_ge(S["p1", "max"], 4 * PAIRS1)
            relative("p3", 0, 12)
            pool.wait_ge(S["p2", "ml"], KT)
            pool.dma_start(memf, a["mem_t"]).then_inc(mem_in, 16)
            for t in range(NT):
                rstd("n1", t, EPS_RMS)
            low_odd("n1")
            tail("n1", False)
            norm_wait(pool, "n1", "x", 2)
            load_gb("n2", a["ln1_g_2"][0], a["ln1_b_2"][0])
            for i in range(1, PAIRS2):
                relative("p3", i, 12)
            for nm, nx, g, b, row in (("n2", "n3", "ln2_g_2", "ln2_b_2", 0),
                                      ("n3", "n4", "ln1_g_2", "ln1_b_2", 1),
                                      ("n4", "n5", "ln2_g_2", "ln2_b_2", 1)):
                for t in range(NT):
                    rstd(nm, t, EPS_LN)
                low_odd(nm)
                tail(nm, True)
                norm_wait(pool, nm, "x", 2)
                load_gb(nx, a[g][row], a[b][row])
                if nm == "n3":
                    pool.wait_ge(S["p3", "max"], 12 * PAIRS2)
                    relative("p5", 0, 4)
                    with pool.Fori(1, PAIRS2) as i:
                        relative("p5", i, 4)
            for t in range(NT):
                rstd("n5", t, EPS_LN)

        @block.scalar
        def _(act):
            chain = Chain(act, ach)

            def make_high(b, slot, loads):
                act.wait_ge(landed[slot], loads * 16)
                act.activation(wh[slot][:, :, :], raw[slot][:, :, :], ACT.Copy).then_inc(split_h, 1)

            def refill1(i, p):
                act.wait_ge(used, i * PER1 + (p + 1))
                if isinstance(i, int):
                    nb = next_in_slot(i * PER1 + p)
                    if nb is not None:
                        make_high(nb, slot_of(nb), loads_of(nb))
                else:
                    make_high(None, p % RING1, i * (PER1 // RING1) + (p // RING1 + 2))

            def refill(i, b):
                act.wait_ge(used, i * RING + (b + 1))
                if isinstance(i, int):
                    nb = next_in_slot(b + RING * i)
                    if nb is not None:
                        make_high(nb, slot_of(nb), loads_of(nb))
                else:
                    make_high(None, slot_of(b), i + loads_of(b + RING))

            def norm_var(nm, centred):
                for t in range(NT):
                    norm_wait(act, nm, "mean" if centred else "sum", t + 1)
                    if t:
                        norm_wait(act, nm, "var", t)
                    act.activation(sq[:, :], (z if nm != "n0" else x_tok)[:, t, :], ACT.Square,
                                   bias=st[:, 4 + t:5 + t] if centred else 0.0,
                                   accum_out=st[:, 6 + t:7 + t]).then_inc(S[nm, "var"], 1)

            def norm_high(nm, g, b):
                def high(k):
                    if k < 6:
                        norm_wait(act, nm, "xf", k + 1)
                    else:
                        norm_wait(act, nm, "xf_act", k - 5)
                    act.activation(xh[:, k, :], xf[:, k % 4, :], ACT.Copy).then_inc(S[nm, "xh"], 1)

                for k in range(4):
                    high(k)
                norm_wait(act, nm, "turned", KT)
                for k in (6, 7):
                    norm_wait(act, nm, "xh", k - 3)
                    norm_wait(act, nm, "xl_dve" if k == 6 else "xl_pool", 2)
                    act.activation(xf[:, k % 4, :], bank[7][:, (k % 2) * T:(k % 2 + 1) * T], ACT.Identity,
                                   scale=gbt[:, g, k:k + 1], bias=0.0 if b is None else gbt[:, b, k:k + 1]
                                   ).then_inc(S[nm, "xf_act"], 1)
                for k in range(4, KT):
                    high(k)

            def exps(ph, i, branch, h, sizes, causal=True):
                for t in range(NT):
                    c = branch * 4 + h * 2 + t
                    cols = s384(t) if causal else slice(t * T, (t + 1) * T)
                    src = sc[:, branch, h, cols] if causal else bank[h][:, cols]
                    act.activation(pr[:, branch, h, cols], src, ACT.Exp, bias=mx[:, c:c + 1], scale=-1.0,
                                   accum_out=den[:, c:c + 1]).then_inc(S[ph, "exp"], 1)

            act.wait_ge(x_in, 32)
            for t in range(NT):
                act.activation(z[:, t, :], x_tok[:, t, :], ACT.Square,
                               accum_out=st[:, 6 + t:7 + t]).then_inc(S["n0", "var"], 1)
            for b in range(2):
                make_high(b, slot_of(b), 1)
            act.wait_ge(gains_in, 16)
            norm_high("n0", 0, None)
            for b in range(2, RING1):
                make_high(b, slot_of(b), 1)
            act.wait_ge(consts_in, 16 * 7)
            act.activation(bmh[:, :, :], bm[:, :, :], ACT.Copy, scale=0.5).then_inc(ach, 1)
            chain.n += 1
            act.wait_ge(ach, chain.n)

            def first(i):
                act.wait_ge(used, i * PER1 + 1)
                act.activation(q_s[:, :], bank[0][:, 0:T], ACT.Copy, scale=-0.125
                               ).then_inc(S["p1", "free_act"], 1)
                refill1(i, 0)
                act.wait_ge(used, i * PER1 + 2)
                act.activation(k_s[:, :], bank[1][:, 0:T], ACT.Copy).then_inc(S["p1", "free_act"], 1)
                refill1(i, 1)
                refill1(i, 2)
                for h in range(2):
                    act.wait_ge(S["p1", "max"], i * 4 + (2 * h + 2))
                    exps("p1", i, 0, h, None)
                act.wait_ge(used, i * PER1 + 4)
                act.activation(t_a[:, :], bank[0][:, 0:T], ACT.Copy).then_inc(S["p1", "free_act"], 1)
                act.wait_ge(S["p1", "free_act"], i * 5 + 8)
                act.sem_inc(S["p1", "xc"], 1)
                refill1(i, 3)
                refill1(i, 4)
                refill1(i, 5)
                act.wait_ge(S["p1", "turned"], i * 2 + 1)
                act.activation(pt[:, 0, 0, 0:CAUSAL], bank[5][:, 0:CAUSAL], ACT.Copy
                               ).then_inc(S["p1", "pt_act"], 1)
                act.wait_ge(used, i * PER1 + 7)
                act.activation(t_c[:, :], bank[0][:, 0:T], ACT.Tanh, scale=0.5).then_inc(S["p1", "tz"], 1)
                refill1(i, 6)
                act.wait_ge(used, i * PER1 + 8)
                act.activation(t_d[:, :], bank[1][:, 0:T], ACT.Tanh, scale=0.5).then_inc(S["p1", "ta"], 1)
                act.wait_ge(S["p1", "yc"], i + 1)
                act.activation(mixh[:, 0, bass.ds(i, 1), :], t_e[:, :].unsqueeze(1), ACT.Copy
                               ).then_inc(S["p1", "yc_h"], 1)
                refill1(i, 7)
                act.wait_ge(used, i * PER1 + 9)
                act.activation(gates[:, 0, bass.ds(i, 1), :], bank[2][:, 0:T].unsqueeze(1), ACT.Tanh,
                               scale=0.5, bias=bmh[:, 0, bass.ds(i, 1)]).then_inc(S["p1", "free_act"], 1)
                refill1(i, 8)
                act.wait_ge(S["p1", "ya"], i + 1)
                act.activation(mixh[:, 1, bass.ds(i, 1), :], t_g[:, :].unsqueeze(1), ACT.Copy
                               ).then_inc(S["p1", "ya_h"], 1)
                act.wait_ge(used, i * PER1 + 10)
                act.activation(gates[:, 1, bass.ds(i, 1), :], bank[1][:, 0:T].unsqueeze(1), ACT.Tanh,
                               scale=0.5, bias=bmh[:, 1, bass.ds(i, 1)]).then_inc(S["p1", "free_act"], 1)
                refill1(i, 9)

            with act.Fori(0, PAIRS1 - 1) as i:
                first(i)
            first(PAIRS1 - 1)

            def merge(i, b):
                act.wait_ge(S["p2", "m"], i + 1)
                act.activation(mh[:, :], t_c[:, :], ACT.Copy, scale=0.5).then_inc(S["p2", "mh"], 1)

            refill(0, B_MIX)
            refill(0, B_MIX + 1)
            merge(0, None)
            with act.Fori(0, KT - 1) as i:
                for n in range(3):
                    refill(i, B_MIX + 2 + n)
                merge(i + 1, None)

            def refills(b0, n):
                for b in range(b0, b0 + n):
                    refill(0, b)

            norm_var("n1", False)
            refill(0, B_NSA - 1)
            norm_high("n1", 1, None)
            act.wait_ge(mem_in, 16)
            act.activation(memh, memf, ACT.Copy).then_inc(mem_h, 1)

            def pt_evac(ph, want, dst, src):
                act.wait_ge(S[ph, "turned"], want)
                act.activation(dst, src, ACT.Copy).then_inc(S[ph, "pt_act"], 1)

            def o_high(ph, i, j, b):
                act.wait_ge(S[ph, "o"], i + 1)
                act.activation(oh[:, bass.ds(j, 1), :], bank[b][:, 0:T].unsqueeze(1), ACT.Copy
                               ).then_inc(S[ph, "oh"], 1)

            def finish(ph, r0):
                def memory_exps(j):
                    for h in range(2):
                        act.wait_ge(S[ph, "max"], 2 * j + h + 1)
                        exps(ph, j, 0, h, None, causal=False)

                memory_exps(0)
                refill(0, r0)
                pt_evac(ph, 1, pt[:, 0, 0, :], bank[2][:, :])
                refill(0, r0 + 1)
                o_high(ph, 0, PAIRS2, 0)
                refill(0, r0 + 2)
                refill(0, r0 + 3)
                memory_exps(1)
                refill(0, r0 + 4)
                pt_evac(ph, 3, pt[:, 0, 0, :], bank[2][:, :])
                refill(0, r0 + 5)
                o_high(ph, 1, PAIRS2 + 1, 0)
                refill(0, r0 + 6)

            b = B_NSA
            act.wait_ge(used, b + 1)
            refill(0, b)
            act.wait_ge(used, b + 2)
            act.activation(ks2[0:DH, :], bank[1][0:DH, 0:T], ACT.Copy).then_inc(S["p3", "free_act"], 1)
            act.activation(ks2[DH:P, :], bank[1][0:DH, 0:T], ACT.Copy).then_inc(S["p3", "free_act"], 1)
            act.activation(kw2[0:DH, :], bank[1][DH:P, 0:T], ACT.Copy).then_inc(S["p3", "free_act"], 1)
            act.activation(kw2[DH:P, :], bank[1][DH:P, 0:T], ACT.Copy).then_inc(S["p3", "free_act"], 1)
            refill(0, b + 1)
            act.wait_ge(S["p3", "blk"], 1)
            act.activation(blkh[:, :, :, :], blk[:, :, :, :], ACT.Copy).then_inc(S["p3", "blkh"], 1)
            refill(0, b + 2)
            act.wait_ge(used, b + 4)
            act.activation(t_c[:, 0:72].rearrange("p (t g) -> p t g", t=NT),
                           bank[0][:, 0:T].rearrange("p (t g) -> p t g", t=NT)[:, :, 0:36], ACT.Tanh,
                           scale=0.5).then_inc(S["p3", "free_act"], 1)
            refills(b + 3, 9)
            act.activation(hid[:, :, :, :], bank[3][:, 0:64].rearrange("p (s h n) -> p s h n", s=2, h=2),
                           ACT.Gelu_apprx_tanh).then_inc(S["p3", "hid"], 1)

            def queries(i):
                n = 2 * i - 1 if i else 0
                act.wait_ge(used, B_PAIRS + n + 1)
                act.activation(qall[:, i, :], bank[5 + n % 2][:, 0:T], ACT.Copy, scale=-0.125
                               ).then_inc(S["p3", "q"], 1)
                refill(0, B_PAIRS + n)

            queries(0)
            act.wait_ge(S["p3", "w2"], 1)
            act.activation(kc2[0:DH, :], bank[3][0:DH, 128:144], ACT.Copy).then_inc(S["p3", "cmp"], 1)
            act.activation(kc2[DH:P, :], bank[3][0:DH, 128:144], ACT.Copy).then_inc(S["p3", "cmp"], 1)
            act.activation(vc[:, :], bank[3][0:16, 192:256], ACT.Copy).then_inc(S["p3", "cmp"], 1)

            def nsa(i):
                for br in range(2):
                    for h in range(2):
                        act.wait_ge(S["p3", "max"], i * 12 + (br * 4 + 2 * h + 2))
                        exps("p3", i, br, h, None)
                act.wait_ge(S["p3", "max"], i * 12 + 12)
                for h in range(2):
                    for t in range(NT):
                        c = 8 + 2 * h + t
                        act.activation(prc[:, h, t, 0:NCMP], scc[:, h, t, 0:NCMP], ACT.Exp,
                                       bias=mx[:, c:c + 1], scale=-1.0, accum_out=den[:, c:c + 1]
                                       ).then_inc(S["p3", "exp"], 1)
                if i + 1 < PAIRS2:
                    queries(i + 1)
                pt_evac("p3", i * 5 + 1, pt[:, 0, 0, 0:CAUSAL], bank[0][:, 0:CAUSAL])
                pt_evac("p3", i * 5 + 2, pt[:, 0, 1, 0:CAUSAL], bank[1][:, 0:CAUSAL])
                refill(0, B_PAIRS + min(2 * i + 2, 2 * PAIRS2 - 1))
                o_high("p3", i, i, 7)

            for i in range(PAIRS2):
                nsa(i)
            finish("pm3", B_ROWS0)
            norm_var("n2", True)
            refill(0, B_KM - 1)
            act.wait_ge(used, B_KM + 2)
            for n in range(2):
                act.activation(km[:, n, :], bank[n][:, 0:T], ACT.Copy).then_inc(kv_free, 1)
            refill(0, B_KM)
            norm_high("n2", 2, 3)
            refill(0, B_KM + 1)

            def ffn(ph, layer, b0):
                def base(i):
                    act.activation(t_a[:, :], bank[0][:, 0:T], ACT.Identity,
                                   bias=convf[:, layer, bass.ds(i, 1), 3], scale=convf[:, layer, bass.ds(i, 1), 2]
                                   ).then_inc(S[ph, "base"], 1)

                def gelu(i):
                    act.wait_ge(S[ph, "free_a"], i + 1)
                    act.activation(t_b[:, :], t_a[:, :], ACT.Gelu_apprx_tanh).then_inc(S[ph, "g"], 1)

                def high(i):
                    act.wait_ge(S[ph, "m"], i + 1)
                    act.activation(mh[:, :], t_c[:, :], ACT.Copy).then_inc(S[ph, "mh"], 1)

                act.wait_ge(used, b0 + 1)
                base(0)
                refill(0, b0)
                gelu(0)
                refill(0, b0 + 1)
                high(0)

                def body(i):
                    bb = b0 + 2
                    act.wait_ge(used, i * RING + (bb + 1))
                    base(i + 1)
                    refill(i, bb)
                    gelu(i + 1)
                    refill(i, bb + 1)
                    act.wait_ge(used, i * RING + (bb + 3))
                    high(i + 1)
                    refill(i, bb + 2)

                with act.Fori(0, FT - 2) as i:
                    body(i)
                body(FT - 2)

            ffn("f0", 0, B_FFN0)
            norm_var("n3", True)
            refill(0, B_VM - 1)
            act.wait_ge(used, B_VM + 2)
            for n in range(2):
                act.activation(vm[:, :, n * P:(n + 1) * P],
                               bank[n][:, 0:T].rearrange("p (t c) -> p t c", t=NT), ACT.Copy
                               ).then_inc(kv_free, 1)
            refill(0, B_VM)
            norm_high("n3", 4, 5)
            refill(0, B_VM + 1)

            def moba_end(i):
                pt_evac("p5", i * 2 + 1, pt[:, 0, 0, 0:CAUSAL], bank[5][:, 0:CAUSAL])

            def moba(i):
                b = B_MOBA
                act.wait_ge(used, i * RING + (b + 1))
                act.activation(q_s[:, :], bank[0][:, 0:T], ACT.Copy, scale=-0.125
                               ).then_inc(S["p5", "free_act"], 1)
                refill(i, b)
                act.wait_ge(used, i * RING + (b + 2))
                act.activation(k_s[:, :], bank[1][:, 0:T], ACT.Copy).then_inc(S["p5", "free_act"], 1)
                refill(i, b + 1)
                if not isinstance(i, int):
                    moba_end(i - 1)
                refill(i, b + 2)
                if not isinstance(i, int):
                    o_high("p5", i - 1, i - 1, 7)
                for h in range(2):
                    act.wait_ge(S["p5", "max"], i * 4 + (2 * h + 2))
                    exps("p5", i, 0, h, None)

            moba(0)
            with act.Fori(1, PAIRS2) as i:
                moba(i)
            b = B_ROWS1 - 2
            for n in range(2):
                act.wait_ge(used, b + 1 + n)
                act.activation(qall[:, PAIRS2 + n, :], bank[n][:, 0:T], ACT.Copy, scale=-0.125
                               ).then_inc(S["p5", "free_act"], 1)
                refill(0, b + n)
            moba_end(PAIRS2 - 1)
            o_high("p5", PAIRS2 - 1, PAIRS2 - 1, 7)
            finish("pm5", B_ROWS1)
            norm_var("n4", True)
            refill(0, B_FFN1 - 1)
            norm_high("n4", 6, 7)
            ffn("f1", 1, B_FFN1)
            norm_var("n5", True)

        @block.vector
        def _(dve):
            chain = Chain(dve, dch)

            def make_low(b, slot, count):
                dve.wait_ge(split_h, count)
                dve.tensor_tensor(wl[slot][:, :, :], raw[slot][:, :, :], wh[slot][:, :, :].bitcast(F32),
                                  ALU.subtract).then_inc(split_l, 1)

            def refill1(i, p):
                if isinstance(i, int):
                    nb = next_in_slot(i * PER1 + p)
                    if nb is not None:
                        make_low(nb, slot_of(nb), nb + 1)
                else:
                    make_low(None, p % RING1, i * PER1 + (p + RING1 + 1))

            def refill(i, b):
                if isinstance(i, int):
                    nb = next_in_slot(b + RING * i)
                    if nb is not None:
                        make_low(nb, slot_of(nb), nb + 1)
                else:
                    make_low(None, slot_of(b), i * RING + (b + RING + 1))

            def low(dst, src, high, s):
                dve.tensor_tensor(dst, src, high, ALU.subtract).then_inc(s, 1)

            def norm_x(nm, g, b):
                def fetch(k):
                    norm_wait(dve, nm, "turned", k // 2 * 2 + 2)
                    if k >= 4:
                        norm_wait(dve, nm, "xh", k - 3)
                        norm_wait(dve, nm, "xl_dve" if k == 4 else "xl_pool", 1)
                    ps = bank[4 + k // 2][:, (k % 2) * T:(k % 2 + 1) * T]
                    if b is None:
                        dve.tensor_scalar(xf[:, k % 4, :], ps, gbt[:, g, k:k + 1], None, ALU.mult
                                          ).then_inc(S[nm, "xf"], 1)
                    else:
                        dve.tensor_scalar(xf[:, k % 4, :], ps, gbt[:, g, k:k + 1], gbt[:, b, k:k + 1],
                                          ALU.mult, ALU.add).then_inc(S[nm, "xf"], 1)

                def low_even(k):
                    norm_wait(dve, nm, "xh", k + 1)
                    low(xl[:, k, :], xf[:, k % 4, :], xh[:, k, :].bitcast(F32), S[nm, "xl_dve"])

                for k in range(0, 6, 2):
                    fetch(k)
                    fetch(k + 1)
                    low_even(k)
                low_even(6)

            def norm_sum(nm, last_block, alpha, centred, x_from, fill=()):
                fill = list(fill)
                if x_from:
                    norm_wait(dve, x_from, "x", 2)
                for t in range(NT):
                    if t == 0:
                        norm_wait(dve, nm, "half", 1)
                    else:
                        dve.wait_ge(used, last_block + 1)
                    ins = dve.scalar_tensor_tensor(out=z[:, t, :], in0=x_tok[:, t, :], scalar=alpha,
                                                   in1=ysum[t][:, :], op0=ALU.mult, op1=ALU.add,
                                                   accum_out=st[:, t:t + 1])
                    if centred:
                        chain.link(ins)
                        dve.tensor_scalar(st[:, 4 + t:5 + t], st[:, t:t + 1], -1.0 / D, None,
                                          ALU.mult).then_inc(S[nm, "mean"], 1)
                    else:
                        ins.then_inc(S[nm, "sum"], 1)
                if nm == "n5":
                    dve.wait_ge(gb_in, 16 + 32 * 4)
                    for t in range(NT):
                        norm_wait(dve, nm, "mean", t + 1)
                        dve.scalar_tensor_tensor(out=x_tok[:, t, :], in0=z[:, t, :], scalar=st[:, 4 + t:5 + t],
                                                 in1=gb[:, 0, :], op0=ALU.add, op1=ALU.mult
                                                 ).then_inc(S[nm, "off"], 1)
                    for t in range(NT):
                        norm_wait(dve, nm, "off", t + 1)
                        norm_wait(dve, nm, "rstd", t + 1)
                        dve.scalar_tensor_tensor(out=x_tok[:, t, :], in0=x_tok[:, t, :],
                                                 scalar=st[:, 10 + t:11 + t], in1=gb[:, 1, :],
                                                 op0=ALU.mult, op1=ALU.add).then_inc(S[nm, "z"], 1)
                    return
                for t in range(NT):
                    norm_wait(dve, nm, "rstd", t + 1)
                    if centred:
                        norm_wait(dve, nm, "mean", t + 1)
                        dve.tensor_scalar(z[:, t, :], z[:, t, :], st[:, 4 + t:5 + t],
                                          st[:, 10 + t:11 + t], ALU.add, ALU.mult).then_inc(S[nm, "z"], 1)
                    else:
                        norm_wait(dve, nm, "sum", t + 1)
                        dve.tensor_scalar(z[:, t, :], z[:, t, :], st[:, 10 + t:11 + t], None,
                                          ALU.mult).then_inc(S[nm, "z"], 1)
                    if t == NT - 1:
                        for b in fill:
                            refill(0, b)

            def score_min(ph, branch, h, src, guard):
                dve.sem_inc(seen, 1)
                for t in range(NT):
                    c = branch * 4 + h * 2 + t
                    keys = slice(P, T) if t == 0 else slice(0, T)
                    dve.tensor_tensor_reduce(sc[:, branch, h, s384(t)], src[:, s384(t)], bias[:, h, keys],
                                             1.0, guard, ALU.add, ALU.min, mx[:, c:c + 1]
                                             ).then_inc(S[ph, "max"], 1)

            def scale_probs(ph, branch, h, factor, causal=True):
                for t in range(NT):
                    c = branch * 4 + h * 2 + t
                    cols = s384(t) if causal else slice(t * T, (t + 1) * T)
                    dve.tensor_scalar(pr[:, branch, h, cols], pr[:, branch, h, cols],
                                      factor[:, c:c + 1], None, ALU.mult).then_inc(S[ph, "prob"], 1)

            def o_low(ph, i, j, b):
                dve.wait_ge(S[ph, "oh"], i + 1)
                low(ol[:, bass.ds(j, 1), :], bank[b][:, 0:T].unsqueeze(1), oh[:, bass.ds(j, 1), :].bitcast(F32),
                    S[ph, "ol"])

            dve.memset(mx[:, :], 0.0).then_inc(set_up, 1)
            dve.memset(relb[32:33, :], MASKED).then_inc(set_up, 1)
            dve.memset(t_g[:, :], 0.0).then_inc(set_up, 1)
            dve.memset(t_f[:, :], 0.0).then_inc(S["p1", "free_dve"], 5)
            dve.memset(t_e[:, :], 0.0).then_inc(S["p1", "free_act"], 5)
            for t in range(NT):
                norm_wait(dve, "n0", "rstd", t + 1)
                dve.tensor_scalar(z[:, t, :], x_tok[:, t, :], st[:, 10 + t:11 + t], None,
                                  ALU.mult).then_inc(S["n0", "z"], 1)
            dve.wait_ge(gains_in, 16)
            for b in range(2):
                make_low(b, slot_of(b), b + 1)
            norm_x("n0", 0, None)
            dve.wait_ge(consts_in, 16 * 7)
            for b in range(2, RING1):
                make_low(b, slot_of(b), b + 1)
            dve.wait_ge(rel_ps, 1)
            dve.tensor_copy(relf[:, :], bank[3][0:2 * PAIRS2, :]).then_inc(rel_sb, 1)

            c1 = Chain(dve, dch1, 6)

            def first(i):
                c1.begin(i)
                refill1(i, 0)
                refill1(i, 1)
                dve.wait_ge(used, i * PER1 + 3)
                dve.tensor_copy(v_s[:, :, :], bank[2][:, 0:T].rearrange("p (t c) -> p t c", t=NT)
                                ).then_inc(S["p1", "free_dve"], 1)
                dve.wait_ge(S["p1", "bias_in"], i * 16 + 16)
                for h in range(2):
                    dve.wait_ge(S["p1", "s"], i * 2 + (h + 1))
                    score_min("p1", 0, h, bank[3 + h], 3e38)
                refill1(i, 2)
                refill1(i, 3)
                dve.wait_ge(S["p1", "exp"], i * 4 + 4)
                c1.link(dve.reciprocal(rden[:, 0:4], den[:, 0:4]))
                for h in range(2):
                    scale_probs("p1", 0, h, rden)
                dve.wait_ge(used, i * PER1 + 5)
                dve.wait_ge(S["p1", "xc"], i + 1)
                dve.tensor_tensor(t_b[:, :], bank[1][:, 0:T], t_a[:, :], ALU.mult
                                  ).then_inc(S["p1", "free_dve"], 1)
                dve.wait_ge(S["p1", "free_dve"], i * 5 + 7)
                c1.link(dve.tensor_scalar(t_f[:, :], t_b[:, :], convw[:, bass.ds(i, 1), 2], None, ALU.mult))
                c1.link(dve.scalar_tensor_tensor(out=t_f[:, 1:T], in0=t_b[:, 0:T - 1],
                                                 scalar=convw[:, bass.ds(i, 1), 1], in1=t_f[:, 1:T],
                                                 op0=ALU.mult, op1=ALU.add))
                c1.link(dve.scalar_tensor_tensor(out=t_f[:, 2:T], in0=t_b[:, 0:T - 2],
                                                 scalar=convw[:, bass.ds(i, 1), 0], in1=t_f[:, 2:T],
                                                 op0=ALU.mult, op1=ALU.add))
                refill1(i, 4)
                dve.wait_ge(used, i * PER1 + 6)
                dve.tensor_tensor(t_b[:, :], bank[2][:, 0:T], t_f[:, :], ALU.mult
                                  ).then_inc(S["p1", "free_dve"], 1)
                dve.wait_ge(S["p1", "turned"], i * 2 + 2)
                dve.tensor_copy(pt[:, 0, 1, 0:CAUSAL], bank[6][:, 0:CAUSAL]).then_inc(S["p1", "pt_dve"], 1)
                refill1(i, 5)
                dve.wait_ge(S["p1", "free_dve"], i * 5 + 8)
                dve.wait_ge(S["p1", "tz"], i + 1)
                dve.scalar_tensor_tensor(out=t_f[:, :], in0=t_c[:, :], scalar=1.0, in1=bank[0][:, 0:T],
                                         op0=ALU.add, op1=ALU.mult).then_inc(S["p1", "free_dve"], 1)
                dve.wait_ge(S["p1", "free_dve"], i * 5 + 9)
                dve.scalar_tensor_tensor(out=t_e[:, :], in0=t_f[:, :], scalar=0.5, in1=t_b[:, :],
                                         op0=ALU.mult, op1=ALU.mult).then_inc(S["p1", "yc"], 1)
                refill1(i, 6)
                dve.wait_ge(S["p1", "yc"], i + 1)
                dve.wait_ge(S["p1", "ta"], i + 1)
                c1_za = dve.scalar_tensor_tensor(out=t_f[:, :], in0=t_d[:, :], scalar=1.0,
                                                 in1=bank[1][:, 0:T], op0=ALU.add, op1=ALU.mult)
                c1_za.then_inc(S["p1", "free_dve"], 1)
                dve.wait_ge(S["p1", "yc_h"], i + 1)
                c1.link(dve.tensor_tensor(mixl[:, 0, bass.ds(i, 1), :], t_e[:, :].unsqueeze(1),
                                          mixh[:, 0, bass.ds(i, 1), :].bitcast(F32), ALU.subtract))
                refill1(i, 7)
                dve.wait_ge(S["p1", "o"], i + 1)
                dve.wait_ge(S["p1", "free_dve"], i * 5 + 10)
                dve.scalar_tensor_tensor(out=t_g[:, :], in0=bank[7][:, 0:T], scalar=0.5, in1=t_f[:, :],
                                         op0=ALU.mult, op1=ALU.mult).then_inc(S["p1", "ya"], 1)
                refill1(i, 8)
                dve.wait_ge(S["p1", "ya_h"], i + 1)
                c1.link(dve.tensor_tensor(mixl[:, 1, bass.ds(i, 1), :], t_g[:, :].unsqueeze(1),
                                          mixh[:, 1, bass.ds(i, 1), :].bitcast(F32), ALU.subtract))
                refill1(i, 9)
                c1.end()

            with dve.Fori(0, PAIRS1 - 1) as i:
                first(i)
            first(PAIRS1 - 1)

            c2 = Chain(dve, dch2, 2)

            def part_c(i, b):
                dve.wait_ge(used, b)
                if isinstance(i, int):
                    dve.wait_ge(S["p1", "free_act"], 5 * PAIRS1 + 5)
                dve.scalar_tensor_tensor(out=t_a[:, :].unsqueeze(1), in0=gates[:, 0, bass.ds(i, 1), :], scalar=1.0,
                                         in1=bank[0][:, 0:T].unsqueeze(1), op0=ALU.add, op1=ALU.mult
                                         ).then_inc(S["p2", "free_a"], 1)

            def part_a(i, b):
                dve.wait_ge(used, b)
                c2.begin(i)
                c2.link(dve.scalar_tensor_tensor(out=t_b[:, :].unsqueeze(1), in0=gates[:, 1, bass.ds(i, 1), :],
                                                 scalar=1.0, in1=bank[1][:, 0:T].unsqueeze(1),
                                                 op0=ALU.add, op1=ALU.mult))
                dve.wait_ge(S["p2", "free_a"], i + 1)
                c2.link(dve.tensor_tensor(t_c[:, :], t_a[:, :], t_b[:, :], ALU.add))
                c2.end()
                dve.sem_inc(S["p2", "m"], 1)
                dve.wait_ge(S["p2", "mh"], i + 1)
                dve.scalar_tensor_tensor(out=ml[:, :], in0=t_c[:, :], scalar=0.5, in1=mh[:, :].bitcast(F32),
                                         op0=ALU.mult, op1=ALU.subtract).then_inc(S["p2", "ml"], 1)

            part_c(0, B_MIX + 1)
            refill(0, B_MIX)
            part_a(0, B_MIX + 2)
            refill(0, B_MIX + 1)
            with dve.Fori(0, KT - 1) as i:
                part_c(i + 1, i * RING + (B_MIX + 3))
                refill(i, B_MIX + 2)
                refill(i, B_MIX + 3)
                part_a(i + 1, i * RING + (B_MIX + 5))
                refill(i, B_MIX + 4)

            norm_sum("n1", B_NSA - 1, 1.0, False, None, fill=[B_NSA - 1])
            norm_x("n1", 1, None)
            dve.wait_ge(mem_h, 1)
            dve.tensor_tensor(meml, memf, memh.bitcast(F32), ALU.subtract).then_inc(mem_l, 1)

            def finish(ph, r0):
                def softmax(j):
                    for h in range(2):
                        dve.wait_ge(S[ph, "s"], 2 * j + h + 1)
                        dve.tensor_reduce(mx[:, 2 * h:2 * h + 2],
                                          bank[h][:, :].rearrange("p (t c) -> p t c", t=NT), AX.X, ALU.min
                                          ).then_inc(S[ph, "max"], 1)
                    dve.wait_ge(S[ph, "exp"], 4 * j + 4)
                    chain.link(dve.reciprocal(rden[:, 0:4], den[:, 0:4]))
                    for h in range(2):
                        scale_probs(ph, 0, h, rden, causal=False)

                def transposed(j):
                    dve.wait_ge(S[ph, "turned"], 2 * j + 2)
                    dve.tensor_copy(pt[:, 0, 1, :], bank[3][:, :]).then_inc(S[ph, "pt_dve"], 1)

                softmax(0)
                refill(0, r0)
                transposed(0)
                refill(0, r0 + 1)
                o_low(ph, 0, PAIRS2, 0)
                refill(0, r0 + 2)
                refill(0, r0 + 3)
                softmax(1)
                refill(0, r0 + 4)
                transposed(1)
                refill(0, r0 + 5)
                o_low(ph, 1, PAIRS2 + 1, 0)
                refill(0, r0 + 6)

            b = B_NSA
            dve.wait_ge(used, b + 1)
            chain.link(dve.memset(blk[:, :, :, :], 0.0))
            for s in range(2):
                for par in range(2):
                    src = bank[0][s * DH:(s + 1) * DH, 0:T].rearrange("p (n l) -> p l n", l=16)
                    for lo in range(2):
                        dst = blk[par * DH:(par + 1) * DH, s, 8 * lo:8 * lo + 8, 0:NCMP]
                        taps = pe_kv[par * DH:(par + 1) * DH, s, 8 * lo:8 * lo + 8].unsqueeze(2)
                        ins = dve.tensor_tensor(dst, src[:, par:16:2, lo:lo + NCMP],
                                                taps.to_broadcast([DH, 8, NCMP]), ALU.add)
                        if (s, par, lo) != (1, 1, 1):
                            ins.then_inc(S["p3", "parts"], 1)
            ins.then_inc(S["p3", "blk"], 1)
            refill(0, b)
            refill(0, b + 1)
            dve.wait_ge(S["p3", "blkh"], 1)
            low(blkl[:, :, :, :], blk[:, :, :, :], blkh[:, :, :, :].bitcast(F32), S["p3", "blkl"])
            dve.wait_ge(used, b + 3)
            dve.tensor_copy(v_s[:, :, :], bank[2][:, 0:T].rearrange("p (t c) -> p t c", t=NT)
                            ).then_inc(S["p3", "free_dve"], 1)
            refill(0, b + 2)
            dve.wait_ge(S["p3", "free_act"], 5)
            dve.tensor_scalar(g_nsa[:, :, :], t_c[:, 0:72].rearrange("p (t g) -> p t g", t=NT), 0.5, 0.5,
                              ALU.mult, ALU.add).then_inc(S["p3", "gate"], 1)
            for n in range(3, NSA_FRONT + 1):
                refill(0, b + n)
            dve.wait_ge(S["p3", "gate"], 1)

            def filler(i):
                n = min(2 * i + 2, 2 * PAIRS2 - 1)
                src = bank[5 + n % 2][:, 0:T]
                dve.wait_ge(used, B_PAIRS + n + 1)
                if i < 2:
                    ins = dve.tensor_scalar(qall[:, PAIRS2 + i, :], src, -0.125, None, ALU.mult)
                elif i < 4:
                    ins = dve.tensor_copy(km[:, i - 2, :], src)
                else:
                    ins = dve.tensor_copy(vm[:, :, (i - 4) * P:(i - 3) * P],
                                          src.rearrange("p (t c) -> p t c", t=NT))
                ins.then_inc(S["p3", "fill"], 1)

            def nsa(i):
                dve.wait_ge(S["p3", "bias_in"], i * 16 + 16)
                for br in range(2):
                    for h in range(2):
                        dve.wait_ge(S["p3", "s"], i * 4 + (2 * br + h + 1))
                        score_min("p3", br, h, bank[2 * br + h], NO_KEY)
                for h in range(2):
                    for t in range(NT):
                        c = 8 + 2 * h + t
                        first_key = (P if t == 0 else 0) + CMP_LEN - 1
                        dve.tensor_tensor_reduce(
                            scc[:, h, t, 0:NCMP], bank[h][:, CAUSAL + 16 * t:CAUSAL + 16 * t + NCMP],
                            bias[:, h, first_key:first_key + CMP_STRIDE * (NCMP - 1) + 1:CMP_STRIDE],
                            1.0, NO_KEY, ALU.add, ALU.min, mx[:, c:c + 1]).then_inc(S["p3", "max"], 1)
                gate = g_nsa[:, :, i * 6:i * 6 + 6].rearrange("p t (h r) -> p r h t", r=3)
                for n, r in enumerate((1, 2, 0)):
                    c = slice(4 * n, 4 * n + 4)
                    dve.wait_ge(S["p3", "exp"], i * 12 + 4 * n + 4)
                    chain.link(dve.tensor_scalar(deng[:, c], den[:, c], TINY, None, ALU.max))
                    chain.link(dve.reciprocal(rden[:, c], deng[:, c]))
                    chain.link(dve.tensor_tensor(rg[:, c].rearrange("p (h t) -> p h t", h=2),
                                                 rden[:, c].rearrange("p (h t) -> p h t", h=2),
                                                 gate[:, r], ALU.mult))
                    if n < 2:
                        for h in range(2):
                            scale_probs("p3", n, h, rg)
                for h in range(2):
                    for t in range(NT):
                        c = 8 + 2 * h + t
                        dve.tensor_scalar(prc[:, h, t, 0:NCMP], prc[:, h, t, 0:NCMP], rg[:, c:c + 1], None,
                                          ALU.mult).then_inc(S["p3", "prob"], 1)
                if i + 1 < PAIRS2:
                    refill(0, B_PAIRS + 2 * i + 1)
                else:
                    filler(i)
                for h in range(2):
                    dve.wait_ge(S["p3", "turned"], i * 5 + (3 + h))
                    dve.tensor_copy(pt[:, 1, h, 0:CAUSAL], bank[2 + h][:, 0:CAUSAL]
                                    ).then_inc(S["p3", "pt_dve"], 1)
                dve.wait_ge(S["p3", "turned"], i * 5 + 5)
                dve.tensor_copy(ptc[0:NCMP, :, :], bank[4][0:NCMP, :].rearrange("p (h t) -> p h t", h=2)
                                ).then_inc(S["p3", "pt_dve"], 1)
                if i + 1 < PAIRS2:
                    filler(i)
                refill(0, B_PAIRS + min(2 * i + 2, 2 * PAIRS2 - 1))
                o_low("p3", i, i, 7)

            for i in range(PAIRS2):
                nsa(i)
            finish("pm3", B_ROWS0)
            norm_sum("n2", B_KM - 1, ALPHA, True, "n1", fill=[B_KM - 1, B_KM])
            norm_x("n2", 2, 3)
            refill(0, B_KM + 1)

            def ffn(ph, layer, b0):
                cf = Chain(dve, dchf[layer], 1)

                def taps(i):
                    cf.begin(i)
                    dve.wait_ge(S[ph, "base"], i + 1)
                    cf.link(dve.scalar_tensor_tensor(out=t_a[:, 1:T], in0=bank[0][:, 0:T - 1],
                                                     scalar=convf[:, layer, bass.ds(i, 1), 1], in1=t_a[:, 1:T],
                                                     op0=ALU.mult, op1=ALU.add))
                    dve.scalar_tensor_tensor(out=t_a[:, 2:T], in0=bank[0][:, 0:T - 2],
                                             scalar=convf[:, layer, bass.ds(i, 1), 0], in1=t_a[:, 2:T],
                                             op0=ALU.mult, op1=ALU.add).then_inc(S[ph, "free_a"], 1)
                    cf.end()

                def gated(i, b):
                    dve.wait_ge(used, b)
                    dve.wait_ge(S[ph, "g"], i + 1)
                    dve.tensor_tensor(t_c[:, :], bank[1][:, 0:T], t_b[:, :], ALU.mult).then_inc(S[ph, "m"], 1)
                    dve.wait_ge(S[ph, "mh"], i + 1)
                    low(ml[:, :], t_c[:, :], mh[:, :].bitcast(F32), S[ph, "ml"])

                taps(0)
                refill(0, b0)
                gated(0, b0 + 2)
                refill(0, b0 + 1)

                def body(i):
                    taps(i + 1)
                    refill(i, b0 + 2)
                    refill(i, b0 + 3)
                    gated(i + 1, i * RING + (b0 + 5))
                    refill(i, b0 + 4)

                with dve.Fori(0, FT - 2) as i:
                    body(i)
                body(FT - 2)

            ffn("f0", 0, B_FFN0)
            norm_sum("n3", B_VM - 1, ALPHA, True, "n2", fill=[B_VM - 1, B_VM])
            norm_x("n3", 4, 5)
            refill(0, B_VM + 1)

            c5 = Chain(dve, dch5, 2)

            def transposed(i):
                dve.wait_ge(S["p5", "turned"], i * 2 + 2)
                dve.tensor_copy(pt[:, 0, 1, 0:CAUSAL], bank[6][:, 0:CAUSAL]).then_inc(S["p5", "pt_dve"], 1)

            def moba(i):
                b = B_MOBA
                c5.begin(i)
                refill(i, b)
                refill(i, b + 1)
                if not isinstance(i, int):
                    transposed(i - 1)
                    dve.wait_ge(S["p5", "o"], i)
                dve.wait_ge(used, i * RING + (b + 3))
                dve.tensor_copy(v_s[:, :, :], bank[2][:, 0:T].rearrange("p (t c) -> p t c", t=NT)
                                ).then_inc(S["p5", "free_dve"], 1)
                if not isinstance(i, int):
                    o_low("p5", i - 1, i - 1, 7)
                dve.wait_ge(S["p5", "bias_in"], i * 16 + 16)
                for h in range(2):
                    dve.wait_ge(S["p5", "s"], i * 2 + (h + 1))
                    score_min("p5", 0, h, bank[3 + h], NO_KEY)
                refill(i, b + 2)
                dve.wait_ge(S["p5", "exp"], i * 4 + 4)
                c5.link(dve.tensor_scalar(deng[:, 0:4], den[:, 0:4], TINY, None, ALU.max))
                c5.link(dve.reciprocal(rden[:, 0:4], deng[:, 0:4]))
                for h in range(2):
                    scale_probs("p5", 0, h, rden)
                c5.end()

            moba(0)
            with dve.Fori(1, PAIRS2) as i:
                moba(i)
            refill(0, B_ROWS1 - 2)
            refill(0, B_ROWS1 - 1)
            transposed(PAIRS2 - 1)
            o_low("p5", PAIRS2 - 1, PAIRS2 - 1, 7)
            finish("pm5", B_ROWS1)
            norm_sum("n4", B_FFN1 - 1, ALPHA, True, "n3", fill=[B_FFN1 - 1])
            norm_x("n4", 6, 7)
            ffn("f1", 1, B_FFN1)
            norm_sum("n5", N_BLOCKS - 1, ALPHA, True, "n4")

        @block.tensor
        def _(pe):
            def stationary(slot, out, mov_h, mov_l, each=None):
                for k in range(KT):
                    if each is not None:
                        each(k)
                    pe.matmul(out, wh[slot][:, k, :], mov_h(k), start=k == 0, stop=False)
                    pe.matmul(out, wh[slot][:, k, :], mov_l(k), start=False, stop=False)
                    last = pe.matmul(out, wl[slot][:, k, :], mov_h(k), start=False, stop=k == KT - 1)
                last.then_inc(used, 1)

            def moving(slot, bk, sh, sl, cols=P):
                for t in range(NT):
                    out = bk[:, t * P:t * P + cols]
                    for k in range(KT):
                        th, tl = sh[:, k, t * P:(t + 1) * P], sl[:, k, t * P:(t + 1) * P]
                        pe.matmul(out, th, wh[slot][:, k, 0:cols], start=k == 0, stop=False)
                        pe.matmul(out, th, wl[slot][:, k, 0:cols], start=False, stop=False)
                        last = pe.matmul(out, tl, wh[slot][:, k, 0:cols], start=False, stop=k == KT - 1)
                last.then_inc(used, 1)

            def x_ready(nm):
                def wait(k):
                    norm_wait(pe, nm, "xl_pool" if k % 2 else "xl_dve", k // 2 + 1)
                return wait

            def row(slot, th, tl, start, stop, half=None):
                for t in range(NT):
                    for n in range(2):
                        out = bank[4 + 2 * t + n][:, :]
                        hw = wh[slot][:, 4 * n:4 * n + 4, :].rearrange("p k c -> p (k c)")
                        lw = wl[slot][:, 4 * n:4 * n + 4, :].rearrange("p k c -> p (k c)")
                        pe.matmul(out, th[:, t * P:(t + 1) * P], hw, start=start, stop=False)
                        pe.matmul(out, th[:, t * P:(t + 1) * P], lw, start=False, stop=False)
                        last = pe.matmul(out, tl[:, t * P:(t + 1) * P], hw, start=False, stop=stop)
                    if t == 0 and half is not None:
                        last.then_inc(half, 1)
                last.then_inc(used, 1)

            def ready(b):
                pe.wait_ge(split_l, b)

            def xm(k):
                return xh[:, k, :]

            def xml(k):
                return xl[:, k, :]

            def turn_x(nm):
                for t in range(NT):
                    norm_wait(pe, nm, "z", t + 1)
                    for k in range(KT):
                        c = (k % 2) * T + t * P
                        ins = pe.transpose(bank[4 + k // 2][:, c:c + P], z[:, t, k * P:(k + 1) * P], ident[:, :])
                        if t == NT - 1:
                            ins.then_inc(S[nm, "turned"], 1)

            def scores(out, q, k, h, s=None, keep=False):
                r = slice(h * DH, (h + 1) * DH)
                for t in range(NT):
                    last = pe.matmul(out[:, s384(t)], q[r, t * P:(t + 1) * P], k[r, 0:(t + 1) * P],
                                     start=True, stop=True)
                if s is not None:
                    last.then_inc(s, 1)

            def turn_p(out, p, s):
                for c in range(3):
                    last = pe.transpose(out[:, c * P:(c + 1) * P], p[:, c * P:(c + 1) * P], ident[:, :])
                last.then_inc(s, 1)

            def pv(h, v, p, start, stop):
                r = slice(h * DH, (h + 1) * DH)
                pe.matmul(bank[7][r, 0:T], v[:, 0], p[:, 0:T], start=start, stop=False)
                return pe.matmul(bank[7][r, P:T], v[:, 1], p[:, T:CAUSAL], start=False, stop=stop)

            pe.wait_ge(ident_up, 1)
            turn_x("n0")
            pe.wait_ge(consts_in, 16 * 7)
            pe.wait_ge(set_up, 5)
            pe.matmul(bank[3][0:2 * PAIRS2, :], relb[:, :], onehot[:, :], start=True, stop=True
                      ).then_inc(rel_ps, 1)

            def first(i):
                fa, fd = S["p1", "free_act"], S["p1", "free_dve"]
                plan = [("q", 0, fd, 4), ("k", 1, fa, 5), ("v", 2, fa, 4), ("xc", 0, fa, 6), ("cg", 1, fa, 7),
                        ("bg", 2, fd, 6), ("zc", 0, fa, 8), ("za", 1, fd, 7), ("gc", 2, fd, 8), ("ga", 1, fd, 10)]
                for p, (kind, bk, free, count) in enumerate(plan):
                    ready(i * PER1 + (p + 1))
                    pe.wait_ge(free, i * 5 + count)
                    if kind == "v":
                        moving(p % RING1, bank[bk], xh, xl)
                        pe.wait_ge(fa, i * 5 + 7)
                        if not isinstance(i, int):
                            pe.wait_ge(rel_sb, 1)
                        for h in range(2):
                            scores(bank[3 + h], q_s, k_s, h, S["p1", "s"])
                    else:
                        stationary(p % RING1, bank[bk][:, 0:T], xm, xml,
                                   x_ready("n0") if kind == "q" and not isinstance(i, int) else None)
                    if kind == "bg":
                        for h in range(2):
                            pe.wait_ge(S["p1", "prob"], i * 4 + (2 * h + 2))
                            turn_p(bank[5 + h], pr[:, 0, h, :], S["p1", "turned"])
                    if kind == "za":
                        pe.wait_ge(S["p1", "pt_act"], i + 1)
                        pe.wait_ge(S["p1", "pt_dve"], i + 1)
                        pv(0, v_s[:, :, 0:DH], pt[:, 0, 0, :], True, True)
                        pv(1, v_s[:, :, DH:P], pt[:, 0, 1, :], True, True).then_inc(S["p1", "o"], 1)

            with pe.Fori(0, PAIRS1 - 1) as i:
                first(i)
            first(PAIRS1 - 1)

            def open_banks(ph):
                for n in range(4):
                    pe.matmul(bank[4 + n][:, :], zeros[:, 0:P], zeros[:, :], start=True, stop=False)

            def mix(which, slot, bk):
                stationary(slot, bk[:, 0:T], lambda k: mixh[:, which, k, :], lambda k: mixl[:, which, k, :])

            pe.wait_ge(dch1, 6 * PAIRS1)
            pe.wait_ge(S["p1", "free_act"], 5 + 5 * PAIRS1)
            open_banks("p2")
            ready(B_MIX + 1)
            mix(0, slot_of(B_MIX), bank[0])
            ready(B_MIX + 2)
            mix(1, slot_of(B_MIX + 1), bank[1])
            with pe.Fori(0, KT - 1) as i:
                ready(i * RING + (B_MIX + 3))
                pe.wait_ge(S["p2", "free_a"], i + 1)
                mix(0, slot_of(B_MIX + 2), bank[0])
                ready(i * RING + (B_MIX + 4))
                pe.wait_ge(S["p2", "ml"], i + 1)
                row(slot_of(B_MIX + 3), mh, ml, False, False)
                ready(i * RING + (B_MIX + 5))
                mix(1, slot_of(B_MIX + 4), bank[1])
            ready(B_NSA)
            pe.wait_ge(S["p2", "ml"], KT)
            row(slot_of(B_NSA - 1), mh, ml, False, True, S["n1", "half"])
            turn_x("n1")

            b = B_NSA
            fa, fd = S["p3", "free_act"], S["p3", "free_dve"]
            ready(b + 1)
            stationary(slot_of(b), bank[0][:, 0:T], xm, xml, x_ready("n1"))
            ready(b + 2)
            stationary(slot_of(b + 1), bank[1][:, 0:T], xm, xml)
            ready(b + 3)
            moving(slot_of(b + 2), bank[2], xh, xl)
            ready(b + 4)
            pe.wait_ge(S["p3", "blk"], 1)
            moving(slot_of(b + 3), bank[0], xh, xl, cols=36)
            pe.wait_ge(S["p3", "blkl"], 1)
            for s in range(2):
                for hf in range(2):
                    out = bank[3][:, (2 * s + hf) * 16:(2 * s + hf + 1) * 16]
                    for q in range(2):
                        n = 4 + 4 * s + 2 * hf + q
                        ready(b + n + 1)
                        sl = slot_of(b + n)
                        for k in range(KT):
                            l2 = 8 * q + k
                            pe.matmul(out, wh[sl][:, k, :], blkh[:, s, l2, :], start=l2 == 0, stop=False)
                            pe.matmul(out, wh[sl][:, k, :], blkl[:, s, l2, :], start=False, stop=False)
                            last = pe.matmul(out, wl[sl][:, k, :], blkh[:, s, l2, :], start=False, stop=l2 == 15)
                        last.then_inc(used, 1)

            def memory_keys(b, bk):
                stationary(slot_of(b), bk[:, 0:T], lambda k: memh[:, k, :], lambda k: meml[:, k, :])

            def pair_block(n):
                bk = bank[5 + n % 2]
                ready(B_PAIRS + n + 1)
                if n == 2:
                    pe.wait_ge(S["p3", "q"], 1)
                elif n >= 3 and n % 2:
                    pe.wait_ge(S["p3", "q"], (n - 1) // 2 + 1)
                elif n >= 4:
                    pe.wait_ge(S["p3", "fill"], n // 2 - 1)
                if n == 6:
                    pe.wait_ge(mem_l, 1)
                if n in (6, 8):
                    memory_keys(B_PAIRS + n, bk)
                elif n in (10, 11):
                    moving(slot_of(B_PAIRS + n), bk, memh, meml)
                else:
                    stationary(slot_of(B_PAIRS + n), bk[:, 0:T], xm, xml)

            pair_block(0)
            pe.wait_ge(S["p3", "hid"], 1)
            for hf in range(2):
                pe.matmul(bank[3][0:DH, 128:144], w2[:, 0, hf, :], hid[:, 0, hf, :],
                          start=hf == 0, stop=hf == 1)
            for hf in range(2):
                last = pe.matmul(bank[3][0:16, 192:256], hid[:, 1, hf, :], w2[:, 1, hf, :],
                                 start=hf == 0, stop=hf == 1)
            last.then_inc(S["p3", "w2"], 1)
            pe.wait_ge(fa, 5)
            pe.wait_ge(fd, 1)
            pe.wait_ge(S["p3", "cmp"], 3)

            def nsa(i):
                q = qall[:, i, :]
                pe.wait_ge(S["p3", "q"], i + 1)
                for br, keys in enumerate((ks2, kw2)):
                    for h in range(2):
                        if br == 0:
                            r = slice(h * DH, (h + 1) * DH)
                            for t in range(NT):
                                pe.matmul(bank[h][:, CAUSAL + 16 * t:CAUSAL + 16 * t + NCMP],
                                          q[r, t * P:(t + 1) * P], kc2[r, 0:NCMP], start=True, stop=True)
                        scores(bank[2 * br + h], q, keys, h, S["p3", "s"])
                pair_block(2 * i + 1)
                for br in range(2):
                    for h in range(2):
                        pe.wait_ge(S["p3", "prob"], i * 12 + (4 * br + 2 * h + 2))
                        turn_p(bank[2 * br + h], pr[:, br, h, :], S["p3", "turned"])
                pe.wait_ge(S["p3", "prob"], i * 12 + 12)
                for h in range(2):
                    for t in range(NT):
                        last = pe.matmul(bank[4][0:NCMP, h * T + t * P:h * T + (t + 1) * P],
                                         prc[:, h, t, 0:NCMP], ident[:, :], start=True, stop=True)
                last.then_inc(S["p3", "turned"], 1)
                if i + 1 < PAIRS2:
                    pair_block(2 * i + 2)
                if i:
                    pe.wait_ge(S["p3", "ol"], i)
                pe.wait_ge(S["p3", "pt_act"], i * 2 + 2)
                for h in range(2):
                    pv(h, v_s[:, :, 0:DH], pt[:, 0, h, :], True, False)
                    if h == 0:
                        pe.wait_ge(S["p3", "pt_dve"], i * 3 + 3)
                    pv(h, v_s[:, :, DH:P], pt[:, 1, h, :], False, False)
                    last = pe.matmul(bank[7][h * DH:(h + 1) * DH, 0:T], vc[0:NCMP, :], ptc[0:NCMP, h, :],
                                     start=False, stop=True)
                last.then_inc(S["p3", "o"], 1)

            for i in range(PAIRS2):
                nsa(i)

            def memory_scores(ph, j):
                for h in range(2):
                    r = slice(h * DH, (h + 1) * DH)
                    for t in range(NT):
                        last = pe.matmul(bank[h][:, t * T:(t + 1) * T],
                                         qall[r, PAIRS2 + j, t * P:(t + 1) * P], km[r, j, :],
                                         start=True, stop=True)
                    last.then_inc(S[ph, "s"], 1)

            def memory_turn(ph, j):
                for h in range(2):
                    pe.wait_ge(S[ph, "prob"], 4 * j + 2 * h + 2)
                    for kk in range(NT):
                        for t in range(NT):
                            last = pe.transpose(bank[2 + h][:, (kk * NT + t) * P:(kk * NT + t + 1) * P],
                                                pr[:, 0, h, t * T + kk * P:t * T + (kk + 1) * P], ident[:, :])
                    last.then_inc(S[ph, "turned"], 1)

            def memory_out(ph, j):
                for h in range(2):
                    pe.wait_ge(S[ph, "pt_act" if h == 0 else "pt_dve"], j + 1)
                    for kk in range(NT):
                        last = pe.matmul(bank[0][h * DH:(h + 1) * DH, 0:T],
                                         vm[:, kk, j * P + h * DH:j * P + (h + 1) * DH],
                                         pt[:, 0, h, kk * T:(kk + 1) * T], start=kk == 0, stop=kk == 1)
                last.then_inc(S[ph, "o"], 1)

            def finish(ph, main, r0, half):
                def rows(*ks):
                    for k in ks:
                        ready(r0 + k + 1)
                        row(slot_of(r0 + k), oh[:, k, :], ol[:, k, :], k == 0, k == KT - 1,
                            half if k == KT - 1 else None)

                pe.wait_ge(S[main, "ol"], PAIRS2)
                rows(0, 1)
                memory_turn(ph, 0)
                rows(2)
                memory_out(ph, 0)
                rows(3)
                pe.wait_ge(S[ph, "ol"], 1)
                memory_scores(ph, 1)
                rows(4, 5)
                memory_turn(ph, 1)
                rows(6)
                memory_out(ph, 1)
                pe.wait_ge(S[ph, "ol"], 2)
                rows(7)

            pe.wait_ge(S["p3", "fill"], PAIRS2)
            memory_scores("pm3", 0)
            finish("pm3", "p3", B_ROWS0, S["n2", "half"])
            for n in range(2):
                ready(B_KM + n + 1)
                memory_keys(B_KM + n, bank[n])
            turn_x("n2")

            def ffn(ph, b0, nm):
                ready(b0 + 1)
                stationary(slot_of(b0), bank[0][:, 0:T], xm, xml, x_ready(nm))
                ready(b0 + 2)
                stationary(slot_of(b0 + 1), bank[1][:, 0:T], xm, xml)
                open_banks(ph)

                with pe.Fori(0, FT - 1) as i:
                    ready(i * RING + (b0 + 3))
                    pe.wait_ge(S[ph, "free_a"], i + 1)
                    stationary(slot_of(b0 + 2), bank[0][:, 0:T], xm, xml)
                    ready(i * RING + (b0 + 4))
                    pe.wait_ge(S[ph, "ml"], i + 1)
                    row(slot_of(b0 + 3), mh, ml, False, False)
                    ready(i * RING + (b0 + 5))
                    stationary(slot_of(b0 + 4), bank[1][:, 0:T], xm, xml)
                ready(b0 + 3 * FT)
                pe.wait_ge(S[ph, "ml"], FT)
                row(slot_of(b0 + 3 * FT - 1), mh, ml, False, True, S["n3", "half"])

            pe.wait_ge(kv_free, 2)
            ffn("f0", B_FFN0, "n2")
            for n in range(2):
                ready(B_VM + n + 1)
                moving(slot_of(B_VM + n), bank[n], memh, meml)
            turn_x("n3")

            fa, fd = S["p5", "free_act"], S["p5", "free_dve"]
            pe.wait_ge(kv_free, 4)

            def moba_turn(i):
                for h in range(2):
                    pe.wait_ge(S["p5", "prob"], i * 4 + (2 * h + 2))
                    turn_p(bank[5 + h], pr[:, 0, h, :], S["p5", "turned"])

            def moba_out(i):
                pe.wait_ge(S["p5", "pt_act"], i + 1)
                pe.wait_ge(S["p5", "pt_dve"], i + 1)
                pv(0, v_s[:, :, 0:DH], pt[:, 0, 0, :], True, True)
                pv(1, v_s[:, :, DH:P], pt[:, 0, 1, :], True, True).then_inc(S["p5", "o"], 1)

            def moba(i):
                b = B_MOBA
                ready(i * RING + (b + 1))
                if not isinstance(i, int):
                    pe.wait_ge(fa, i * 2)
                stationary(slot_of(b), bank[0][:, 0:T], xm, xml, x_ready("n3") if isinstance(i, int) else None)
                ready(i * RING + (b + 2))
                stationary(slot_of(b + 1), bank[1][:, 0:T], xm, xml)
                if not isinstance(i, int):
                    moba_turn(i - 1)
                ready(i * RING + (b + 3))
                if not isinstance(i, int):
                    pe.wait_ge(fd, i)
                moving(slot_of(b + 2), bank[2], xh, xl)
                if not isinstance(i, int):
                    moba_out(i - 1)
                pe.wait_ge(fa, i * 2 + 2)
                for h in range(2):
                    scores(bank[3 + h], q_s, k_s, h, S["p5", "s"])

            moba(0)
            with pe.Fori(1, PAIRS2) as i:
                moba(i)
            b = B_ROWS1 - 2
            for n in range(2):
                ready(b + n + 1)
                stationary(slot_of(b + n), bank[n][:, 0:T], xm, xml)
            moba_turn(PAIRS2 - 1)
            pe.wait_ge(fa, 2 * PAIRS2 + 2)
            memory_scores("pm5", 0)
            pe.wait_ge(fd, PAIRS2)
            moba_out(PAIRS2 - 1)
            finish("pm5", "p5", B_ROWS1, S["n4", "half"])
            turn_x("n4")
            ffn("f1", B_FFN1, "n4")


def _columns(w, c0, width=P):
    k = w.shape[0] // P
    part = w.reshape(k, P, -1)[:, :, c0:c0 + width]
    return part.transpose(1, 0, 2)


def _stream(v):
    blocks = []

    def add(x):
        blocks.append(np.ascontiguousarray(x).reshape(P, KT * P))

    w_in = v["w_in"][0]
    order = [4, 5, 6, 0, 2, 1, 3, 7, 8, 9]
    for i in range(PAIRS1):
        for s in order:
            add(_columns(w_in, s * D + i * P))
    wc, wa, wo = v["w_out_conv"][0], v["w_out_attn"][0], v["w_o"][0]

    def skewed(n, first, second, rows):
        add(_columns(first, 0))
        add(_columns(second, 0))
        for j in range(1, n):
            add(_columns(first, j * P))
            add(rows[(j - 1) * P:j * P])
            add(_columns(second, j * P))
        add(rows[(n - 1) * P:n * P])

    skewed(KT, wc, wa, wo)
    aw = v["a_w_in_2"][0]
    q_w, hd = PAIRS2 * P, DH
    kc, vcmp, ks, vs, kw, vw, g, qm = (q_w, q_w + hd, q_w + 2 * hd, q_w + 3 * hd, q_w + 4 * hd,
                                       q_w + 5 * hd, q_w + 6 * hd, q_w + 6 * hd + 36)

    def beside(a, b):
        return np.concatenate([_columns(aw, a, hd), _columns(aw, b, hd)], axis=2)

    add(beside(kc, vcmp))
    add(beside(ks, kw))
    add(beside(vs, vw))
    add(np.pad(_columns(aw, g, 36), ((0, 0), (0, 0), (0, P - 36))))
    for w1 in (v["a_cmp_w1_k_2"][0], v["a_cmp_w1_v_2"][0]):
        for hf in range(2):
            t = _columns(w1, hf * P)
            add(t[:, 0:8])
            add(t[:, 8:16])
    kv_a, kv_b = v["a_w_mem_kv_2"][0], v["b_w_mem_kv_2"][0]
    fill = [_columns(aw, qm), _columns(aw, qm + P)] + [_columns(kv_a, n * P) for n in range(4)]
    add(_columns(aw, 0))
    for i in range(1, PAIRS2):
        add(_columns(aw, i * P))
        add(fill[i - 1])
    add(fill[PAIRS2 - 1])
    for k in range(KT):
        add(v["a_w_out_2"][0][k * P:(k + 1) * P])
    for n in range(2):
        add(_columns(kv_b, n * P))

    def ffn(layer):
        w, half_w = v["ffn_w_in_2"][layer], FT * P
        skewed(FT, w[:, :half_w], w[:, half_w:], v["ffn_w_out_2"][layer])

    ffn(0)
    for n in range(2, 4):
        add(_columns(kv_b, n * P))
    kv, bw = v["shared_w_kv_2"], v["b_w_in_2"][0]
    for i in range(PAIRS2):
        add(_columns(bw, i * P))
        add(_columns(kv, i * P))
        add(_columns(kv, PAIRS2 * P + i * P))
    for i in range(2):
        add(_columns(bw, (PAIRS2 + i) * P))
    for k in range(KT):
        add(v["b_w_out_2"][0][k * P:(k + 1) * P])
    ffn(1)
    assert len(blocks) == N_BLOCKS, len(blocks)
    return np.stack(blocks)


def _alibi():
    delta = P + np.arange(P)[:, None] - np.arange(T)[None, :]
    count = ((delta <= 128).astype(np.float64) + (delta % 4 == 0) + (delta % 16 == 0))
    ok = (delta >= 0) & (count > 0)
    out = np.empty((2 * PAIRS1, P, T), np.float32)
    for h in range(2 * PAIRS1):
        slope = 2.0 ** (-8.0 * (h + 1) / (2 * PAIRS1))
        out[h] = np.where(ok, slope * delta - np.log(np.maximum(count, 1)), MASKED)
    return np.ascontiguousarray(out.reshape(PAIRS1, 2, P, T).transpose(0, 2, 1, 3)).reshape(PAIRS1, P, 2 * T)


def _distance_hot():
    delta = T - 1 - np.arange(RELW)
    n = np.maximum(delta, 0)
    nf = np.maximum(n, 1).astype(np.float32)
    large = 16 + (np.log(nf / np.float32(16)) / np.float32(np.log(8.0)) * np.float32(16)).astype(np.int32)
    bucket = np.where(n < 16, n, np.minimum(large, 31))
    hot = np.zeros((33, RELW), np.float32)
    for m in range(RELW):
        if delta[m] >= 0:
            hot[bucket[m], m] = -1.0
        else:
            hot[32, m] = 1.0
    return hot


def _tiles(x):
    y = x.reshape(x.shape[:-1] + (x.shape[-1] // P, P))
    return np.ascontiguousarray(np.moveaxis(y, -1, 0))


def kernel(**inputs):
    from concourse import bacc
    from concourse.bass_utils import run_bass_kernel_spmd

    v = {k: np.asarray(x) for k, x in inputs.items()}
    gains = [v["norm_g"][0], v["final_g"], v["ln1_g_2"][0], v["ln1_b_2"][0], v["ln2_g_2"][0], v["ln2_b_2"][0],
             v["ln1_g_2"][1], v["ln1_b_2"][1], v["ln2_g_2"][1], v["ln2_b_2"][1]]
    conv = np.concatenate([v["conv_w"][0], v["conv_w"][0][0:1]])
    conv_f = np.stack([np.concatenate([v["ffn_conv_w_2"][n], v["ffn_conv_b_2"][n][None]]) for n in range(2)])
    pe_kv = np.stack([v["a_cmp_pe_k_2"][0], v["a_cmp_pe_v_2"][0]])
    w2 = np.stack([v["a_cmp_w2_k_2"][0], v["a_cmp_w2_v_2"][0]])
    arrays = {
        "x": v["x"],
        "stream": _stream(v),
        "gains_t": _tiles(np.stack(gains)),
        "conv_t": np.ascontiguousarray(_tiles(conv).transpose(0, 2, 1)),
        "conv_f_t": np.ascontiguousarray(_tiles(conv_f).transpose(0, 1, 3, 2)),
        "b_merge_t": _tiles(v["b_merge"][0].reshape(2, D)),
        "pe_t": np.ascontiguousarray(pe_kv.reshape(2, 16, 2, DH).transpose(2, 3, 0, 1)).reshape(P, 2, 16),
        "w2_t": np.ascontiguousarray(w2.reshape(2, 2, P, DH).transpose(2, 0, 1, 3)),
        "mem_t": np.ascontiguousarray(v["mem_2"][0].T.reshape(KT, P, T).transpose(1, 0, 2)),
        "rel_bias_2": v["rel_bias_2"],
        "distance_hot": _distance_hot(),
        "alibi": _alibi(),
        "final_g": v["final_g"],
        "ln1_g_2": v["ln1_g_2"], "ln1_b_2": v["ln1_b_2"],
        "ln2_g_2": v["ln2_g_2"], "ln2_b_2": v["ln2_b_2"],
    }
    nc = bacc.Bacc("TRN2", target_bir_lowering=False, num_devices=1)
    a = {n: nc.dram_tensor(f"in_{n}", x.shape, mybir.dt.from_np(x.dtype), kind="ExternalInput").ap()
         for n, x in arrays.items()}
    a["out"] = nc.dram_tensor("out", (1, T, D), F32, kind="ExternalOutput").ap()
    build_program(nc, a)
    r = run_bass_kernel_spmd(nc, [{f"in_{n}": x for n, x in arrays.items()}], core_ids=[0])
    return r.results[0]["out"]
```

```python
from contextlib import ExitStack

import numpy as np

import concourse.bass as bass
from concourse import mybir

F32 = mybir.dt.float32
F32R = mybir.dt.float32r
BF16 = mybir.dt.bfloat16
ALU = mybir.AluOpType
ACT = mybir.ActivationFunctionType
AX = mybir.AxisListType

P = 128
T = 256
NT = T // P
D = 1024
KT = D // P
DH = 64
PAIRS1 = 8
PAIRS2 = 6
NCMP = 15
CMP_STRIDE, CMP_LEN = 16, 32
FT = 2816 // P
EPS_RMS, EPS_LN = 1e-6, 1e-5
ALPHA = 4.0 ** 0.25
TINY = 1e-30
MASKED = 1e30
NO_KEY = 1e20
BIASW = 384
RELW = 512
CAUSAL = P + T

RING = 3
PER1 = 9
B_FIRST = KT
B_MIX = B_FIRST + PAIRS1 * PER1
B_KM0 = B_MIX + 3 * KT
B_NSA = B_KM0 + 2
NSA_FRONT = 12
B_PAIRS = B_NSA + NSA_FRONT
B_ROWS0 = B_PAIRS + PAIRS2 + 4
B_KM = B_ROWS0 + KT
B_FFN0 = B_KM + 2
B_VM = B_FFN0 + 3 * FT
B_MOBA = B_VM + 2
B_QK = B_MOBA + PAIRS2
B_ROWS1 = B_QK + 2 * PAIRS2 + 2
B_FFN1 = B_ROWS1 + KT
N_BLOCKS = B_FFN1 + 3 * FT


QUERY_BLOCK = (0, 1, 3, 5, 6, 7)
FILL_BLOCK = (2, 4, 8, 9)
PAIR_BANK = (5, 6, 4, 5, 6, 6, 6, 6, 6, 6)
WARM_UP = 12


def slot_of(b):
    return b % RING


class Chain:

    def __init__(self, engine, sem, per=0):
        self.engine, self.sem, self.per, self.n, self.i = engine, sem, per, 0, 0

    def begin(self, i):
        self.i, self.n = i, 0

    def link(self, instruction):
        self.n += 1
        instruction.then_inc(self.sem, 1)
        self.engine.wait_ge(self.sem, self.i * self.per + self.n if self.per else self.n)

    def end(self):
        assert self.n == self.per, self.n


def build_program(nc, a):
    ctx = ExitStack()
    with ctx:
        def sb(name, shape, dt=F32):
            return ctx.enter_context(nc.sbuf_tensor("sb_" + name, shape, dt))

        def sem(name):
            return ctx.enter_context(nc.semaphore(name))

        bank = [ctx.enter_context(nc.psum_tensor(f"bank{n}", [P, 512], F32)) for n in range(4)]
        ysum = [ctx.enter_context(nc.psum_tensor(f"ysum{t}", [P, D], F32)) for t in range(NT)]
        bank += [ysum[t][:, n * 512:(n + 1) * 512] for t in range(NT) for n in range(2)]
        rel_rows = nc.dram_tensor("rel_rows", (2 * PAIRS2, P, RELW), F32, kind="Internal").ap()

        raw = [sb(f"raw{n}", [P, KT, P]) for n in range(RING)]
        wh = [sb(f"wh{n}", [P, KT, P], F32R) for n in range(RING)]
        wl = [sb(f"wl{n}", [P, KT, P], F32R) for n in range(RING)]
        x_tok = sb("x_tok", [P, NT, D])
        z = sb("z", [P, NT, D])
        xh = sb("xh", [P, KT, T], F32R)
        xl = sb("xl", [P, KT, T], F32R)
        gb = sb("gb", [P, 2, D])
        gbt = sb("gbt", [P, 10, KT])
        mixh = sb("mixh", [P, 2, KT, T], F32R)
        mixl = sb("mixl", [P, 2, KT, T], F32R)
        gates = sb("gates", [P, 2, KT, T])
        oh, ol = mixh[:, 0], mixl[:, 0]
        memf = sb("memf", [P, KT, T])
        memh = sb("memh", [P, KT, T], F32R)
        meml = sb("meml", [P, KT, T], F32R)
        qall = gates[:, 1]
        mh = sb("mh", [P, T], F32R)
        ml = sb("ml", [P, T], F32R)
        bias = sb("bias", [P, 2, BIASW])
        q_s = sb("q_s", [P, T])
        k_s = sb("k_s", [P, T])
        v_s = sb("v_s", [P, NT, P])
        ks2 = sb("ks2", [P, T])
        kw2 = sb("kw2", [P, T])
        kc2 = sb("kc2", [P, 16])
        vc = sb("vc", [16, DH])
        g_nsa = sb("g_nsa", [P, NT, 36])
        km = sb("km", [P, 2, T])
        vm = sb("vm", [P, NT, T])
        blkh = sb("blkh", [P, 2, 16, 16], F32R)
        blkl = sb("blkl", [P, 2, 16, 16], F32R)
        hid = sb("hid", [P, 2, 2, 16])
        w2 = sb("w2", [P, 2, 2, DH])
        pe_kv = sb("pe_kv", [P, 2, 16])
        sc = sb("sc", [P, 2, 2, 512])
        pr = sb("pr", [P, 2, 2, 512])
        pt = sb("pt", [P, 2, 2, 512])
        scc = sb("scc", [P, 2, NT, 16])
        prc = [sb(f"prc{n}", [P, 2, NT, 16]) for n in range(2)]
        ptc = sb("ptc", [16, 2, T])
        mx = sb("mx", [P, 12])
        den = sb("den", [P, 12])
        deng = sb("deng", [P, 12])
        rden = sb("rden", [P, 12])
        rg = sb("rg", [P, 12])
        t_a = sb("t_a", [P, T])
        t_b = sb("t_b", [P, T])
        t_c = sb("t_c", [P, T])
        t_d = sb("t_d", [P, T])
        t_e = sb("t_e", [P, T])
        t_f = sb("t_f", [P, T])
        t_g = sb("t_g", [P, T])
        ident = sb("ident", [P, P])
        zeros = sb("zeros", [P, 512], BF16)
        relb = sb("relb", [33, 2 * PAIRS2])
        relf = sb("relf", [2 * PAIRS2, RELW])
        convw = sb("convw", [P, KT, 4])
        convf = sb("convf", [P, 2, FT, 4])
        bm = sb("bm", [P, 2, KT])
        bmh = sb("bmh", [P, 2, KT])
        st = sb("st", [P, 16])
        half = sb("half", [P, 1])
        xf = pt[:, :, :, :].rearrange("p b a (s t) -> p (b a s) t", s=2)
        blk = pt[:, 0, 0, :].rearrange("p (s l n) -> p s l n", s=2, l=16)
        onehot = sc[0:33, 0, 0, :]
        hid_rows = sc[0:16, 1, 1, :]
        prs = [pr, z[:, :, :].rearrange("p b (h c) -> p b h c", h=2)]
        v_all = z
        sq = pr[:, 0, :, :].rearrange("p h c -> p (h c)")

        landed = [sem(f"landed{n}") for n in range(RING)]
        split_h, split_l, used = sem("split_h"), sem("split_l"), sem("used")
        gains_in, kv_free = sem("gains_in"), sem("kv_free")
        mem_hl = sem("mem_split")
        consts_in, ident_up, set_up = sem("consts_in"), sem("ident_up"), sem("set_up")
        dch, ach, pch = sem("dve_chain"), sem("act_chain"), sem("pool_chain")
        dch1, dch2 = sem("dve_c1"), sem("dve_c2")
        dchf = [sem("dve_cf0"), sem("dve_cf1")]
        rel_ps, rel_sb, rel_out = sem("rel_ps"), sem("rel_sb"), sem("rel_out")
        mem_in, mem_h, mem_l = sem("mem_in"), sem("mem_h"), sem("mem_l")
        out_done, seen = sem("out_done"), sem("scores_seen")
        S = {}
        norms = ["n0", "n1", "n2", "n3", "n4", "n5"]
        per_norm = {"sum": 2, "mean": 2, "var": 2, "rstd": 2, "z": 2, "x": 2, "half": 1, "off": 2,
                    "turned": KT, "xf": 6, "xf_act": 2, "xh": KT, "xl_dve": 4, "xl_pool": 4}
        first_norm = {"sum": 1, "mean": 2, "x": 1, "half": 1, "off": 5}
        for what in per_norm:
            one = sem(f"norm_{what}")
            for nm in norms:
                S[nm, what] = one
        x_in, gb_in = [sem(f"x_in{t}") for t in range(NT)], sem("gb_in")

        def turned_x(nm, k):
            bk = bank[(0 if nm in ("n0", "n3") else 4) + k // 2]
            return bk[:, (k % 2) * T:(k % 2 + 1) * T]

        def norm_wait(engine, nm, what, count):
            before = norms.index(nm) - first_norm.get(what, 0)
            engine.wait_ge(S[nm, what], before * per_norm[what] + count)

        for ph in ("p1", "p3", "p5", "pm3", "pm5"):
            for what in ("s", "max", "exp", "prob", "turned", "pt_act", "pt_dve", "o", "oh", "ol"):
                S[ph, what] = sem(f"{ph}_{what}")
        for ph in ("p1", "p3", "p5"):
            for what in ("bias_in", "free_act", "free_dve"):
                S[ph, what] = sem(f"{ph}_{what}")
        for what in ("xc", "tz", "yc", "yc_h", "ta", "ya", "ya_h"):
            S["p1", what] = sem(f"p1_{what}")
        for ph in ("p2", "f0", "f1"):
            for what in ("free_a", "free_b", "m", "mh", "ml", "base", "g"):
                S[ph, what] = sem(f"{ph}_{what}")
        v_pair = sem("v_pair")
        v_up = [sem("v1_up"), sem("v2_up")]
        for what in ("blk", "blkh", "blkl", "hid_out", "hid_in", "hid", "w2", "cmp", "q", "gate", "gate_in",
                     "fill", "parts", "rg", "prob_pool"):
            S["p3", what] = sem(f"p3_{what}")

        block = ctx.enter_context(nc.Block())

        def s384(t):
            return slice(0, P) if t == 0 else slice(P, CAUSAL)

        @block.sync
        def _(sp):
            def load(b, slot):
                sp.dma_start(raw[slot][:, :, :], a["stream"][bass.ds(b, 1)].rearrange(
                    "a p (k c) -> p (a k) c", k=KT)).then_inc(landed[slot], 16)

            for t in range(NT):
                sp.dma_start(x_tok[:, t, :], a["x"][0, t * P:(t + 1) * P, :]).then_inc(x_in[t], 16)
            sp.dma_start(gbt[:, :, :], a["gains_t"]).then_inc(gains_in, 16)
            for b in range(RING):
                load(b, slot_of(b))
            sp.dma_start(convw[:, :, :], a["conv_t"]).then_inc(consts_in, 16)
            sp.dma_start(bm[:, :, :], a["b_merge_t"]).then_inc(consts_in, 16)
            sp.dma_start(onehot[:, :], a["distance_hot"]).then_inc(consts_in, 16)
            sp.dma_start(relb[0:32, :], a["rel_bias_2"]).then_inc(consts_in, 16)
            sp.dma_start(convf[:, :, :, :], a["conv_f_t"]).then_inc(consts_in, 16)
            sp.dma_start(pe_kv[:, :, :], a["pe_t"]).then_inc(consts_in, 16)
            sp.dma_start(w2[:, :, :, :], a["w2_t"]).then_inc(consts_in, 16)
            with sp.Fori(1, N_BLOCKS // RING) as i:
                for n in range(RING):
                    sp.wait_ge(split_l, i * RING + (n - RING + 1))
                    load(i * RING + n, n)
            for b in range(N_BLOCKS // RING * RING, N_BLOCKS):
                sp.wait_ge(split_l, b - RING + 1)
                load(b, slot_of(b))
            for t in range(NT):
                norm_wait(sp, "n5", "z", t + 1)
                sp.dma_start(a["out"][0, t * P:(t + 1) * P, :], x_tok[:, t, :]).then_inc(out_done, 16)
            sp.wait_ge(out_done, 16 * NT)

        @block.gpsimd
        def _(pool):
            chain = Chain(pool, pch)
            pool.memset(half[:, :], -0.5).then_inc(set_up, 1)
            chain.link(pool.memset(ident[:, :], 0.0))
            pool.affine_select(out=ident[:, :], in_=ident[:, :], compare_op=ALU.not_equal, fill=1.0,
                               base=0, pattern=[[-1, P]], channel_multiplier=1).then_inc(ident_up, 1)
            pool.memset(zeros[:, :], 0.0).then_inc(set_up, 1)
            pool.wait_ge(set_up, 5)

            def rstd(nm, t, eps):
                norm_wait(pool, nm, "var", t + 1)
                chain.link(pool.tensor_scalar(st[:, 8 + t:9 + t], st[:, 6 + t:7 + t], 1.0 / D, eps,
                                              ALU.mult, ALU.add))
                pool.tensor_tensor(st[:, 10 + t:11 + t], st[:, 8 + t:9 + t], half[:, :],
                                   ALU.pow).then_inc(S[nm, "rstd"], 1)

            def load_gb(nm, gain, shift):
                pool.dma_start(gb[:, 0, :], gain.partition_broadcast(P)).then_inc(gb_in, 16)
                if shift is not None:
                    pool.dma_start(gb[:, 1, :], shift.partition_broadcast(P)).then_inc(gb_in, 16)

            def tail(nm, shift):
                pool.wait_ge(gb_in, 16 + 32 * (norms.index(nm) - 1))
                for t in range(NT):
                    norm_wait(pool, nm, "z", t + 1)
                    last = pool.tensor_tensor(x_tok[:, t, :], z[:, t, :], gb[:, 0, :], ALU.mult)
                    if shift:
                        chain.link(last)
                        last = pool.tensor_tensor(x_tok[:, t, :], x_tok[:, t, :], gb[:, 1, :], ALU.add)
                    last.then_inc(S[nm, "x"], 1)

            def low_odd(nm):
                for k in range(1, KT, 2):
                    norm_wait(pool, nm, "xh", k + 1)
                    pool.tensor_tensor(xl[:, k, :], xf[:, k, :], xh[:, k, :].bitcast(F32), ALU.subtract
                                       ).then_inc(S[nm, "xl_pool"], 1)

            def alibi(i):
                if not isinstance(i, int):
                    pool.wait_ge(S["p1", "max"], i * 4)
                pool.dma_start(bias[:, :, 0:T], a["alibi"][bass.ds(i, 1)].rearrange(
                    "a p (h c) -> p (a h) c", h=2)).then_inc(S["p1", "bias_in"], 16)

            for t in range(NT):
                rstd("n0", t, EPS_RMS)
            alibi(0)
            low_odd("n0")
            load_gb("n1", a["final_g"], None)
            pool.wait_ge(rel_sb, 1)
            pool.dma_start(rel_rows, relf[:, :].unsqueeze(1).to_broadcast([2 * PAIRS2, P, RELW])
                           ).then_inc(rel_out, 16)

            pool.dma_start(memf[:, :, :], a["mem_t"]).then_inc(mem_in, 16)
            def pick_values(i):
                if not isinstance(i, int):
                    pool.wait_ge(S["p1", "o"], i)
                pool.tensor_copy(v_s[:, :, :], v_all[:, :, bass.ds(i * P, P)]).then_inc(v_pair, 1)

            pool.wait_ge(v_up[0], 2)
            pick_values(0)
            with pool.Fori(1, PAIRS1) as i:
                alibi(i)
                pick_values(i)
            pool.wait_ge(rel_out, 16)

            def relative(ph, i, per):
                if not isinstance(i, int) or i > 0:
                    pool.wait_ge(S[ph, "max"], i * per)
                src = bass.AP(rel_rows.tensor, 0, [[RELW - 1, P], [P * RELW, 2 * PAIRS2], [1, BIASW]])
                pool.dma_start(bias[:, :, :], src_pair(src, i)).then_inc(S[ph, "bias_in"], 16)

            def src_pair(src, i):
                base = bass.AP(rel_rows.tensor, P - 1,
                               [[RELW - 1, P], [P * RELW, 2 * PAIRS2], [1, BIASW]])
                return base[:, bass.ds(i * 2, 2), :]

            pool.wait_ge(S["p1", "max"], 4 * PAIRS1)
            relative("p3", 0, 12)
            pool.wait_ge(mem_h, 2)
            pool.tensor_tensor(meml[:, :, :], memf[:, :, :], memh[:, :, :].bitcast(F32), ALU.subtract
                               ).then_inc(mem_l, 1)
            for t in range(NT):
                rstd("n1", t, EPS_RMS)
            low_odd("n1")
            tail("n1", False)
            norm_wait(pool, "n1", "x", 2)
            load_gb("n2", a["ln1_g_2"][0], a["ln1_b_2"][0])
            for i in range(PAIRS2):
                if i + 1 < PAIRS2:
                    relative("p3", i + 1, 12)
                pool.wait_ge(S["p3", "rg"], 3 * i + 2)
                for h in range(2):
                    for t in range(NT):
                        c = 4 + 2 * h + t
                        p = prs[i % 2][:, 1, h, s384(t)]
                        pool.tensor_scalar(p, p, rg[:, c:c + 1], None, ALU.mult).then_inc(S["p3", "prob_pool"], 1)
                pool.wait_ge(S["p3", "rg"], 3 * i + 3)
                for h in range(2):
                    for t in range(NT):
                        c = 8 + 2 * h + t
                        p = prc[i % 2][:, h, t, 0:NCMP]
                        pool.tensor_scalar(p, p, rg[:, c:c + 1], None, ALU.mult).then_inc(S["p3", "prob_pool"], 1)
            for nm, nx, g, b, row in (("n2", "n3", "ln2_g_2", "ln2_b_2", 0),
                                      ("n3", "n4", "ln1_g_2", "ln1_b_2", 1),
                                      ("n4", "n5", "ln2_g_2", "ln2_b_2", 1)):
                for t in range(NT):
                    rstd(nm, t, EPS_LN)
                low_odd(nm)
                tail(nm, True)
                norm_wait(pool, nm, "x", 2)
                load_gb(nx, a[g][row], a[b][row])
                if nm == "n3":
                    pool.wait_ge(S["p3", "max"], 12 * PAIRS2)
                    relative("p5", 0, 4)
                    with pool.Fori(1, PAIRS2) as i:
                        relative("p5", i, 4)
            for t in range(NT):
                rstd("n5", t, EPS_LN)

        @block.scalar
        def _(act):
            chain = Chain(act, ach)

            def make_high(slot, loads):
                act.wait_ge(landed[slot], loads * 16)
                act.activation(wh[slot][:, :, :], raw[slot][:, :, :], ACT.Copy).then_inc(split_h, 1)

            def refill(i, b, per=RING):
                if isinstance(i, int) and b + per * i + RING >= N_BLOCKS:
                    return
                act.wait_ge(used, i * per + (b + 1))
                make_high(slot_of(b), i * (per // RING) + ((b + RING) // RING + 1))

            def norm_var(nm, centred):
                for t in range(NT):
                    norm_wait(act, nm, "mean" if centred else "sum", t + 1)
                    if t:
                        norm_wait(act, nm, "var", t)
                    act.activation(sq[:, :], (z if nm != "n0" else x_tok)[:, t, :], ACT.Square,
                                   bias=st[:, 4 + t:5 + t] if centred else 0.0,
                                   accum_out=st[:, 6 + t:7 + t]).then_inc(S[nm, "var"], 1)

            def norm_high(nm, g, b):
                def high(k):
                    if k < 6:
                        norm_wait(act, nm, "xf", k + 1)
                    else:
                        norm_wait(act, nm, "xf_act", k - 5)
                    act.activation(xh[:, k, :], xf[:, k, :], ACT.Copy).then_inc(S[nm, "xh"], 1)

                for k in range(4):
                    high(k)
                norm_wait(act, nm, "turned", KT)
                for k in (6, 7):
                    if k == 7:
                        high(4)
                    act.activation(xf[:, k, :], turned_x(nm, k), ACT.Identity,
                                   scale=gbt[:, g, k:k + 1], bias=0.0 if b is None else gbt[:, b, k:k + 1]
                                   ).then_inc(S[nm, "xf_act"], 1)
                for k in range(5, KT):
                    high(k)

            def exps(ph, i, branch, h, sizes, causal=True, to=pr):
                for t in range(NT):
                    c = branch * 4 + h * 2 + t
                    cols = s384(t) if causal else slice(t * T, (t + 1) * T)
                    src = sc[:, branch, h, cols] if causal else bank[h][:, cols]
                    act.activation(to[:, branch, h, cols], src, ACT.Exp, bias=mx[:, c:c + 1], scale=-1.0,
                                   accum_out=den[:, c:c + 1]).then_inc(S[ph, "exp"], 1)

            for t in range(NT):
                act.wait_ge(x_in[t], 16)
                act.activation(z[:, t, :], x_tok[:, t, :], ACT.Square,
                               accum_out=st[:, 6 + t:7 + t]).then_inc(S["n0", "var"], 1)
            for b in range(2):
                make_high(b, 1)
            act.wait_ge(gains_in, 16)
            norm_high("n0", 0, None)
            make_high(2, 1)
            act.wait_ge(consts_in, 16 * 7)
            act.activation(bmh[:, :, :], bm[:, :, :], ACT.Copy, scale=0.5).then_inc(ach, 1)
            chain.n += 1
            act.wait_ge(ach, chain.n)
            for k in range(KT - 1):
                refill(0, k)
            act.wait_ge(used, B_FIRST)
            act.activation(v_all[:, 1, :], ysum[1][:, :], ACT.Copy).then_inc(v_up[0], 1)
            refill(0, KT - 1)

            def first(i):
                def made(p):
                    act.wait_ge(used, i * PER1 + (B_FIRST + p + 1))

                def again(p):
                    refill(i, B_FIRST + p, PER1)

                made(0)
                act.activation(q_s[:, :], bank[0][:, 0:T], ACT.Copy, scale=-0.125
                               ).then_inc(S["p1", "free_act"], 1)
                again(0)
                made(1)
                act.activation(k_s[:, :], bank[1][:, 0:T], ACT.Copy).then_inc(S["p1", "free_act"], 1)
                again(1)
                made(2)
                act.activation(t_a[:, :], bank[2][:, 0:T], ACT.Copy).then_inc(S["p1", "free_act"], 1)
                act.wait_ge(S["p1", "free_act"], i * 5 + 8)
                act.sem_inc(S["p1", "xc"], 1)
                for h in range(2):
                    act.wait_ge(S["p1", "max"], i * 4 + (2 * h + 2))
                    exps("p1", i, 0, h, None)
                again(2)
                again(3)
                again(4)
                act.wait_ge(S["p1", "turned"], i * 2 + 1)
                act.activation(pt[:, 0, 0, 0:CAUSAL], bank[5][:, 0:CAUSAL], ACT.Copy
                               ).then_inc(S["p1", "pt_act"], 1)
                made(5)
                act.activation(t_c[:, :], bank[2][:, 0:T], ACT.Tanh, scale=0.5).then_inc(S["p1", "tz"], 1)
                again(5)
                made(6)
                act.activation(t_d[:, :], bank[0][:, 0:T], ACT.Tanh, scale=0.5).then_inc(S["p1", "ta"], 1)
                act.wait_ge(S["p1", "yc"], i + 1)
                act.activation(mixh[:, 0, bass.ds(i, 1), :], t_e[:, :].unsqueeze(1), ACT.Copy
                               ).then_inc(S["p1", "yc_h"], 1)
                again(6)
                made(7)
                act.activation(gates[:, 0, bass.ds(i, 1), :], bank[1][:, 0:T].unsqueeze(1), ACT.Tanh,
                               scale=0.5, bias=bmh[:, 0, bass.ds(i, 1)]).then_inc(S["p1", "free_act"], 1)
                again(7)
                act.wait_ge(S["p1", "ya"], i + 1)
                act.activation(mixh[:, 1, bass.ds(i, 1), :], t_g[:, :].unsqueeze(1), ACT.Copy
                               ).then_inc(S["p1", "ya_h"], 1)
                made(8)
                act.activation(gates[:, 1, bass.ds(i, 1), :], bank[2][:, 0:T].unsqueeze(1), ACT.Tanh,
                               scale=0.5, bias=bmh[:, 1, bass.ds(i, 1)]).then_inc(S["p1", "free_act"], 1)
                again(8)

            with act.Fori(0, PAIRS1 - 1) as i:
                first(i)
            first(PAIRS1 - 1)

            def merge(i, b):
                act.wait_ge(S["p2", "m"], i + 1)
                act.activation(mh[:, :], t_c[:, :], ACT.Copy, scale=0.5).then_inc(S["p2", "mh"], 1)

            refill(0, B_MIX)
            refill(0, B_MIX + 1)
            merge(0, None)
            act.wait_ge(mem_in, 16)
            for n in range(2):
                part = slice(n * KT // 2, (n + 1) * KT // 2)
                act.activation(memh[:, part, :], memf[:, part, :], ACT.Copy).then_inc(mem_h, 1)
            with act.Fori(0, KT - 1) as i:
                for n in range(3):
                    refill(i, B_MIX + 2 + n)
                merge(i + 1, None)

            def refills(b0, n):
                for b in range(b0, b0 + n):
                    refill(0, b)

            def memory_keys(b):
                act.wait_ge(used, b + 2)
                for n in range(2):
                    act.activation(km[:, n, :], bank[2 + n][:, 0:T], ACT.Copy).then_inc(kv_free, 1)

            norm_var("n1", False)
            refill(0, B_KM0 - 1)
            refill(0, B_KM0)
            norm_high("n1", 1, None)
            memory_keys(B_KM0)
            refill(0, B_KM0 + 1)

            def pt_evac(ph, want, dst, src):
                act.wait_ge(S[ph, "turned"], want)
                act.activation(dst, src, ACT.Copy).then_inc(S[ph, "pt_act"], 1)

            def o_high(ph, i, j, b):
                act.wait_ge(S[ph, "o"], i + 1)
                act.activation(oh[:, bass.ds(j, 1), :], bank[b][:, 0:T].unsqueeze(1), ACT.Copy
                               ).then_inc(S[ph, "oh"], 1)

            def memory_exps(ph, j):
                for h in range(2):
                    act.wait_ge(S[ph, "max"], 2 * j + h + 1)
                    exps(ph, j, 0, h, None, causal=False)

            def finish(ph, r0):
                if ph == "pm3":
                    pt_evac(ph, 1, pt[:, 0, 0, :], bank[2][:, :])
                refill(0, r0)
                refill(0, r0 + 1)
                if ph != "pm3":
                    pt_evac(ph, 1, pt[:, 0, 0, :], bank[2][:, :])
                refill(0, r0 + 2)
                o_high(ph, 0, PAIRS2, 2)
                memory_exps(ph, 1)
                refill(0, r0 + 3)
                refill(0, r0 + 4)
                pt_evac(ph, 3, pt[:, 0, 0, :], bank[2][:, :])
                refill(0, r0 + 5)
                o_high(ph, 1, PAIRS2 + 1, 2)
                refill(0, r0 + 6)

            b = B_NSA
            act.wait_ge(used, b + 1)
            refill(0, b)
            act.wait_ge(used, b + 2)
            act.activation(ks2[0:DH, :], bank[1][0:DH, 0:T], ACT.Copy).then_inc(S["p3", "free_act"], 1)
            act.activation(ks2[DH:P, :], bank[1][0:DH, 0:T], ACT.Copy).then_inc(S["p3", "free_act"], 1)
            act.activation(kw2[0:DH, :], bank[1][DH:P, 0:T], ACT.Copy).then_inc(S["p3", "free_act"], 1)
            act.activation(kw2[DH:P, :], bank[1][DH:P, 0:T], ACT.Copy).then_inc(S["p3", "free_act"], 1)
            act.wait_ge(S["p3", "blk"], 1)
            act.activation(blkh[:, :, :, :], blk[:, :, :, :], ACT.Copy).then_inc(S["p3", "blkh"], 1)
            refill(0, b + 1)
            refill(0, b + 2)
            act.wait_ge(S["p3", "gate_in"], 1)
            act.activation(t_c[:, 72:144], t_c[:, 0:72], ACT.Tanh, scale=0.5).then_inc(S["p3", "free_act"], 1)
            refills(b + 3, 9)

            def queries(i):
                n = QUERY_BLOCK[i]
                act.wait_ge(used, B_PAIRS + n + 1)
                act.activation(qall[:, i, :], bank[PAIR_BANK[n]][:, 0:T], ACT.Copy, scale=-0.125
                               ).then_inc(S["p3", "q"], 1)
                refill(0, B_PAIRS + n)

            queries(0)
            act.wait_ge(S["p3", "hid_in"], 1)
            act.activation(hid[:, :, :, :], bank[3][:, 0:64].rearrange("p (s h n) -> p s h n", s=2, h=2),
                           ACT.Gelu_apprx_tanh).then_inc(S["p3", "hid"], 1)
            queries(1)
            act.wait_ge(S["p3", "w2"], 1)
            act.activation(kc2[0:DH, :], bank[3][0:DH, 128:144], ACT.Copy).then_inc(S["p3", "cmp"], 1)
            act.activation(kc2[DH:P, :], bank[3][0:DH, 128:144], ACT.Copy).then_inc(S["p3", "cmp"], 1)
            act.activation(vc[:, :], bank[3][0:16, 192:256], ACT.Copy).then_inc(S["p3", "cmp"], 1)
            refill(0, B_PAIRS + FILL_BLOCK[0])

            def branch_exps(i, br):
                for h in range(2):
                    act.wait_ge(S["p3", "max"], i * 12 + (br * 4 + 2 * h + 2))
                    exps("p3", i, br, h, None, to=prs[i % 2])

            def compressed_exps(i):
                act.wait_ge(S["p3", "max"], i * 12 + 12)
                for h in range(2):
                    for t in range(NT):
                        c = 8 + 2 * h + t
                        act.activation(prc[i % 2][:, h, t, 0:NCMP], scc[:, h, t, 0:NCMP], ACT.Exp,
                                       bias=mx[:, c:c + 1], scale=-1.0, accum_out=den[:, c:c + 1]
                                       ).then_inc(S["p3", "exp"], 1)

            branch_exps(0, 0)
            branch_exps(0, 1)
            compressed_exps(0)
            queries(2)
            refill(0, B_PAIRS + FILL_BLOCK[1])
            norm_wait(act, "n1", "x", 2)

            def nsa(i):
                if i + 1 < PAIRS2:
                    branch_exps(i + 1, 0)
                else:
                    memory_exps("pm3", 0)
                pt_evac("p3", i * 5 + 1, pt[:, 0, 0, 0:CAUSAL], bank[4][:, 0:CAUSAL])
                pt_evac("p3", i * 5 + 2, pt[:, 0, 1, 0:CAUSAL], bank[5][:, 0:CAUSAL])
                if i + 1 < PAIRS2:
                    branch_exps(i + 1, 1)
                    compressed_exps(i + 1)
                if i + 3 < PAIRS2:
                    queries(i + 3)
                elif i + 1 < PAIRS2:
                    refill(0, B_PAIRS + FILL_BLOCK[i - 1])
                o_high("p3", i, i, 7)

            for i in range(PAIRS2):
                nsa(i)
            finish("pm3", B_ROWS0)
            norm_var("n2", True)
            refill(0, B_KM - 1)
            refill(0, B_KM)
            norm_high("n2", 2, 3)
            memory_keys(B_KM)
            refill(0, B_KM + 1)

            def ffn(ph, layer, b0):
                def base(i):
                    act.activation(t_a[:, :], bank[0][:, 0:T], ACT.Identity,
                                   bias=convf[:, layer, bass.ds(i, 1), 3], scale=convf[:, layer, bass.ds(i, 1), 2]
                                   ).then_inc(S[ph, "base"], 1)

                def gelu(i):
                    act.wait_ge(S[ph, "free_a"], i + 1)
                    act.activation(t_b[:, :], t_a[:, :], ACT.Gelu_apprx_tanh).then_inc(S[ph, "g"], 1)

                def high(i):
                    act.wait_ge(S[ph, "m"], i + 1)
                    act.activation(mh[:, :], t_c[:, :], ACT.Copy).then_inc(S[ph, "mh"], 1)

                act.wait_ge(used, b0 + 1)
                base(0)
                refill(0, b0)
                gelu(0)
                refill(0, b0 + 1)
                high(0)

                def body(i):
                    bb = b0 + 2
                    act.wait_ge(used, i * RING + (bb + 1))
                    base(i + 1)
                    refill(i, bb)
                    gelu(i + 1)
                    refill(i, bb + 1)
                    act.wait_ge(used, i * RING + (bb + 3))
                    high(i + 1)
                    refill(i, bb + 2)

                with act.Fori(0, FT - 2) as i:
                    body(i)
                body(FT - 2)

            ffn("f0", 0, B_FFN0)
            norm_var("n3", True)
            refill(0, B_VM - 1)
            refill(0, B_VM)
            norm_high("n3", 4, 5)
            act.wait_ge(used, B_VM + 2)
            act.activation(vm[:, :, :], bank[4][:, :].rearrange("p (t c) -> p t c", t=NT), ACT.Copy
                           ).then_inc(kv_free, 1)
            refill(0, B_VM + 1)

            refills(B_MOBA, PAIRS2 - 1)
            act.wait_ge(used, B_QK)
            norm_wait(act, "n3", "x", 2)
            act.activation(v_all[:, 1, 0:512], bank[6][:, :], ACT.Copy).then_inc(v_up[1], 1)
            refill(0, B_QK - 1)

            def moba(i):
                b = B_QK + 2 * i
                act.wait_ge(used, b + 1)
                act.activation(q_s[:, :], bank[0][:, 0:T], ACT.Copy, scale=-0.125
                               ).then_inc(S["p5", "free_act"], 1)
                refill(0, b)
                act.wait_ge(used, b + 2)
                act.activation(k_s[:, :], bank[1][:, 0:T], ACT.Copy).then_inc(S["p5", "free_act"], 1)
                if i:
                    pt_evac("p5", 2 * i - 1, pt[:, 0, 0, 0:CAUSAL], bank[5][:, 0:CAUSAL])
                for h in range(2):
                    act.wait_ge(S["p5", "max"], i * 4 + (2 * h + 2))
                    exps("p5", i, 0, h, None)
                if i:
                    o_high("p5", i - 1, i - 1, 7)
                refill(0, b + 1)

            for i in range(PAIRS2):
                moba(i)
            b = B_ROWS1 - 2
            for n in range(2):
                act.wait_ge(used, b + 1 + n)
                act.activation(qall[:, PAIRS2 + n, :], bank[n][:, 0:T], ACT.Copy, scale=-0.125
                               ).then_inc(S["p5", "free_act"], 1)
                refill(0, b + n)
            pt_evac("p5", 2 * PAIRS2 - 1, pt[:, 0, 0, 0:CAUSAL], bank[5][:, 0:CAUSAL])
            memory_exps("pm5", 0)
            o_high("p5", PAIRS2 - 1, PAIRS2 - 1, 7)
            finish("pm5", B_ROWS1)
            norm_var("n4", True)
            norm_high("n4", 6, 7)
            refill(0, B_FFN1 - 1)
            ffn("f1", 1, B_FFN1)
            norm_var("n5", True)

        @block.vector
        def _(dve):
            chain = Chain(dve, dch)

            def make_low(slot, count):
                dve.wait_ge(split_h, count)
                dve.tensor_tensor(wl[slot][:, :, :], raw[slot][:, :, :], wh[slot][:, :, :].bitcast(F32),
                                  ALU.subtract).then_inc(split_l, 1)

            def refill(i, b, per=RING):
                if isinstance(i, int) and b + per * i + RING >= N_BLOCKS:
                    return
                make_low(slot_of(b), i * per + (b + RING + 1))

            def low(dst, src, high, s):
                dve.tensor_tensor(dst, src, high, ALU.subtract).then_inc(s, 1)

            def norm_x(nm, g, b, between=None):
                def fetch(k):
                    norm_wait(dve, nm, "turned", k // 2 * 2 + 2)
                    ps = turned_x(nm, k)
                    if b is None:
                        dve.tensor_scalar(xf[:, k, :], ps, gbt[:, g, k:k + 1], None, ALU.mult
                                          ).then_inc(S[nm, "xf"], 1)
                    else:
                        dve.tensor_scalar(xf[:, k, :], ps, gbt[:, g, k:k + 1], gbt[:, b, k:k + 1],
                                          ALU.mult, ALU.add).then_inc(S[nm, "xf"], 1)

                def low_even(k):
                    norm_wait(dve, nm, "xh", k + 1)
                    low(xl[:, k, :], xf[:, k, :], xh[:, k, :].bitcast(F32), S[nm, "xl_dve"])

                for k in range(0, 6, 2):
                    fetch(k)
                    fetch(k + 1)
                    low_even(k)
                    if k == 0 and between is not None:
                        between()
                low_even(6)

            def norm_sum(nm, last_block, alpha, centred, x_from, fill=()):
                fill = list(fill)
                if x_from:
                    norm_wait(dve, x_from, "x", 2)
                for t in range(NT):
                    if t == 0:
                        norm_wait(dve, nm, "half", 1)
                    else:
                        dve.wait_ge(used, last_block + 1)
                    ins = dve.scalar_tensor_tensor(out=z[:, t, :], in0=x_tok[:, t, :], scalar=alpha,
                                                   in1=ysum[t][:, :], op0=ALU.mult, op1=ALU.add,
                                                   accum_out=st[:, t:t + 1])
                    if centred:
                        chain.link(ins)
                        dve.tensor_scalar(st[:, 4 + t:5 + t], st[:, t:t + 1], -1.0 / D, None,
                                          ALU.mult).then_inc(S[nm, "mean"], 1)
                    else:
                        ins.then_inc(S[nm, "sum"], 1)
                if nm == "n5":
                    dve.wait_ge(gb_in, 16 + 32 * 4)
                    for t in range(NT):
                        norm_wait(dve, nm, "mean", t + 1)
                        dve.scalar_tensor_tensor(out=x_tok[:, t, :], in0=z[:, t, :], scalar=st[:, 4 + t:5 + t],
                                                 in1=gb[:, 0, :], op0=ALU.add, op1=ALU.mult
                                                 ).then_inc(S[nm, "off"], 1)
                    for t in range(NT):
                        norm_wait(dve, nm, "off", t + 1)
                        norm_wait(dve, nm, "rstd", t + 1)
                        dve.scalar_tensor_tensor(out=x_tok[:, t, :], in0=x_tok[:, t, :],
                                                 scalar=st[:, 10 + t:11 + t], in1=gb[:, 1, :],
                                                 op0=ALU.mult, op1=ALU.add).then_inc(S[nm, "z"], 1)
                    return
                for t in range(NT):
                    norm_wait(dve, nm, "rstd", t + 1)
                    if centred:
                        norm_wait(dve, nm, "mean", t + 1)
                        dve.tensor_scalar(z[:, t, :], z[:, t, :], st[:, 4 + t:5 + t],
                                          st[:, 10 + t:11 + t], ALU.add, ALU.mult).then_inc(S[nm, "z"], 1)
                    else:
                        norm_wait(dve, nm, "sum", t + 1)
                        dve.tensor_scalar(z[:, t, :], z[:, t, :], st[:, 10 + t:11 + t], None,
                                          ALU.mult).then_inc(S[nm, "z"], 1)
                    if t == NT - 1:
                        for b in fill:
                            refill(0, b)

            def score_min(ph, branch, h, src, guard):
                dve.sem_inc(seen, 1)
                for t in range(NT):
                    c = branch * 4 + h * 2 + t
                    keys = slice(P, T) if t == 0 else slice(0, T)
                    dve.tensor_tensor_reduce(sc[:, branch, h, s384(t)], src[:, s384(t)], bias[:, h, keys],
                                             1.0, guard, ALU.add, ALU.min, mx[:, c:c + 1]
                                             ).then_inc(S[ph, "max"], 1)

            def scale_probs(ph, branch, h, factor, causal=True, p=pr):
                for t in range(NT):
                    c = branch * 4 + h * 2 + t
                    cols = s384(t) if causal else slice(t * T, (t + 1) * T)
                    dve.tensor_scalar(p[:, branch, h, cols], p[:, branch, h, cols],
                                      factor[:, c:c + 1], None, ALU.mult).then_inc(S[ph, "prob"], 1)

            def o_low(ph, i, j, b):
                dve.wait_ge(S[ph, "oh"], i + 1)
                low(ol[:, bass.ds(j, 1), :], bank[b][:, 0:T].unsqueeze(1), oh[:, bass.ds(j, 1), :].bitcast(F32),
                    S[ph, "ol"])

            dve.memset(mx[:, :], 0.0).then_inc(set_up, 1)
            dve.memset(relb[32:33, :], MASKED).then_inc(set_up, 1)
            dve.memset(t_g[:, :], 0.0).then_inc(set_up, 1)
            dve.memset(t_f[:, :], 0.0).then_inc(S["p1", "free_dve"], 5)
            dve.memset(t_e[:, :], 0.0).then_inc(S["p1", "free_act"], 5)
            for t in range(NT):
                norm_wait(dve, "n0", "rstd", t + 1)
                dve.tensor_scalar(z[:, t, :], x_tok[:, t, :], st[:, 10 + t:11 + t], None,
                                  ALU.mult).then_inc(S["n0", "z"], 1)
            dve.wait_ge(gains_in, 16)
            make_low(0, 1)
            norm_x("n0", 0, None, lambda: make_low(1, 2))
            make_low(2, 3)
            for k in range(KT - 1):
                refill(0, k)
            dve.wait_ge(used, B_FIRST)
            dve.tensor_copy(v_all[:, 0, :], ysum[0][:, :]).then_inc(v_up[0], 1)
            dve.wait_ge(rel_ps, 1)
            dve.tensor_copy(relf[:, :], bank[3][0:2 * PAIRS2, :]).then_inc(rel_sb, 1)
            refill(0, KT - 1)

            c1 = Chain(dve, dch1, 6)

            def first(i):
                def made(p):
                    dve.wait_ge(used, i * PER1 + (B_FIRST + p + 1))

                def again(p):
                    refill(i, B_FIRST + p, PER1)

                c1.begin(i)
                again(0)
                again(1)
                dve.wait_ge(S["p1", "bias_in"], i * 16 + 16)
                for h in range(2):
                    dve.wait_ge(S["p1", "s"], i * 2 + (h + 1))
                    score_min("p1", 0, h, bank[3 + h], 3e38)
                made(3)
                dve.wait_ge(S["p1", "xc"], i + 1)
                dve.tensor_tensor(t_b[:, :], bank[0][:, 0:T], t_a[:, :], ALU.mult
                                  ).then_inc(S["p1", "free_dve"], 1)
                again(2)
                dve.wait_ge(S["p1", "exp"], i * 4 + 4)
                c1.link(dve.reciprocal(rden[:, 0:4], den[:, 0:4]))
                for h in range(2):
                    scale_probs("p1", 0, h, rden)
                again(3)
                dve.wait_ge(S["p1", "free_dve"], i * 4 + 6)
                c1.link(dve.tensor_scalar(t_f[:, :], t_b[:, :], convw[:, bass.ds(i, 1), 2], None, ALU.mult))
                c1.link(dve.scalar_tensor_tensor(out=t_f[:, 1:T], in0=t_b[:, 0:T - 1],
                                                 scalar=convw[:, bass.ds(i, 1), 1], in1=t_f[:, 1:T],
                                                 op0=ALU.mult, op1=ALU.add))
                c1.link(dve.scalar_tensor_tensor(out=t_f[:, 2:T], in0=t_b[:, 0:T - 2],
                                                 scalar=convw[:, bass.ds(i, 1), 0], in1=t_f[:, 2:T],
                                                 op0=ALU.mult, op1=ALU.add))
                made(4)
                dve.tensor_tensor(t_b[:, :], bank[1][:, 0:T], t_f[:, :], ALU.mult
                                  ).then_inc(S["p1", "free_dve"], 1)
                again(4)
                dve.wait_ge(S["p1", "turned"], i * 2 + 2)
                dve.tensor_copy(pt[:, 0, 1, 0:CAUSAL], bank[6][:, 0:CAUSAL]).then_inc(S["p1", "pt_dve"], 1)
                dve.wait_ge(S["p1", "free_dve"], i * 4 + 7)
                dve.wait_ge(S["p1", "tz"], i + 1)
                dve.scalar_tensor_tensor(out=t_f[:, :], in0=t_c[:, :], scalar=1.0, in1=bank[2][:, 0:T],
                                         op0=ALU.add, op1=ALU.mult).then_inc(S["p1", "free_dve"], 1)
                dve.wait_ge(S["p1", "free_dve"], i * 4 + 8)
                dve.scalar_tensor_tensor(out=t_e[:, :], in0=t_f[:, :], scalar=0.5, in1=t_b[:, :],
                                         op0=ALU.mult, op1=ALU.mult).then_inc(S["p1", "yc"], 1)
                again(5)
                dve.wait_ge(S["p1", "yc"], i + 1)
                dve.wait_ge(S["p1", "ta"], i + 1)
                dve.scalar_tensor_tensor(out=t_f[:, :], in0=t_d[:, :], scalar=1.0, in1=bank[0][:, 0:T],
                                         op0=ALU.add, op1=ALU.mult).then_inc(S["p1", "free_dve"], 1)
                dve.wait_ge(S["p1", "yc_h"], i + 1)
                c1.link(dve.tensor_tensor(mixl[:, 0, bass.ds(i, 1), :], t_e[:, :].unsqueeze(1),
                                          mixh[:, 0, bass.ds(i, 1), :].bitcast(F32), ALU.subtract))
                again(6)
                dve.wait_ge(S["p1", "o"], i + 1)
                dve.wait_ge(S["p1", "free_dve"], i * 4 + 9)
                dve.scalar_tensor_tensor(out=t_g[:, :], in0=bank[7][:, 0:T], scalar=0.5, in1=t_f[:, :],
                                         op0=ALU.mult, op1=ALU.mult).then_inc(S["p1", "ya"], 1)
                again(7)
                dve.wait_ge(S["p1", "ya_h"], i + 1)
                c1.link(dve.tensor_tensor(mixl[:, 1, bass.ds(i, 1), :], t_g[:, :].unsqueeze(1),
                                          mixh[:, 1, bass.ds(i, 1), :].bitcast(F32), ALU.subtract))
                again(8)
                c1.end()

            with dve.Fori(0, PAIRS1 - 1) as i:
                first(i)
            first(PAIRS1 - 1)

            c2 = Chain(dve, dch2, 2)

            def part_c(i, b):
                dve.wait_ge(used, b)
                if isinstance(i, int):
                    dve.wait_ge(S["p1", "free_act"], 5 * PAIRS1 + 5)
                dve.scalar_tensor_tensor(out=t_a[:, :].unsqueeze(1), in0=gates[:, 0, bass.ds(i, 1), :], scalar=1.0,
                                         in1=bank[0][:, 0:T].unsqueeze(1), op0=ALU.add, op1=ALU.mult
                                         ).then_inc(S["p2", "free_a"], 1)

            def part_a(i, b):
                dve.wait_ge(used, b)
                c2.begin(i)
                c2.link(dve.scalar_tensor_tensor(out=t_b[:, :].unsqueeze(1), in0=gates[:, 1, bass.ds(i, 1), :],
                                                 scalar=1.0, in1=bank[1][:, 0:T].unsqueeze(1),
                                                 op0=ALU.add, op1=ALU.mult))
                dve.wait_ge(S["p2", "free_a"], i + 1)
                c2.link(dve.tensor_tensor(t_c[:, :], t_a[:, :], t_b[:, :], ALU.add))
                c2.end()
                dve.sem_inc(S["p2", "m"], 1)
                dve.wait_ge(S["p2", "mh"], i + 1)
                dve.scalar_tensor_tensor(out=ml[:, :], in0=t_c[:, :], scalar=0.5, in1=mh[:, :].bitcast(F32),
                                         op0=ALU.mult, op1=ALU.subtract).then_inc(S["p2", "ml"], 1)

            part_c(0, B_MIX + 1)
            refill(0, B_MIX)
            part_a(0, B_MIX + 2)
            refill(0, B_MIX + 1)
            with dve.Fori(0, KT - 1) as i:
                part_c(i + 1, i * RING + (B_MIX + 3))
                refill(i, B_MIX + 2)
                refill(i, B_MIX + 3)
                part_a(i + 1, i * RING + (B_MIX + 5))
                refill(i, B_MIX + 4)

            norm_sum("n1", B_KM0 - 1, 1.0, False, None, fill=[B_KM0 - 1, B_KM0])
            norm_x("n1", 1, None)
            refill(0, B_KM0 + 1)

            def memory_softmax(ph, j):
                for h in range(2):
                    dve.wait_ge(S[ph, "s"], 2 * j + h + 1)
                    dve.tensor_reduce(mx[:, 2 * h:2 * h + 2],
                                      bank[h][:, :].rearrange("p (t c) -> p t c", t=NT), AX.X, ALU.min
                                      ).then_inc(S[ph, "max"], 1)

            def memory_probs(ph, j):
                dve.wait_ge(S[ph, "exp"], 4 * j + 4)
                chain.link(dve.reciprocal(rden[:, 0:4], den[:, 0:4]))
                for h in range(2):
                    scale_probs(ph, 0, h, rden, causal=False)

            def finish(ph, r0):
                def transposed(j):
                    dve.wait_ge(S[ph, "turned"], 2 * j + 2)
                    dve.tensor_copy(pt[:, 0, 1, :], bank[3][:, :]).then_inc(S[ph, "pt_dve"], 1)

                if ph == "pm3":
                    transposed(0)
                refill(0, r0)
                refill(0, r0 + 1)
                if ph != "pm3":
                    transposed(0)
                refill(0, r0 + 2)
                o_low(ph, 0, PAIRS2, 2)
                memory_softmax(ph, 1)
                memory_probs(ph, 1)
                refill(0, r0 + 3)
                refill(0, r0 + 4)
                transposed(1)
                refill(0, r0 + 5)
                o_low(ph, 1, PAIRS2 + 1, 2)
                refill(0, r0 + 6)

            b = B_NSA
            dve.wait_ge(used, b + 1)
            chain.link(dve.memset(blk[:, :, :, :], 0.0))
            for s in range(2):
                for par in range(2):
                    src = bank[0][s * DH:(s + 1) * DH, 0:T].rearrange("p (n l) -> p l n", l=16)
                    for lo in range(2):
                        dst = blk[par * DH:(par + 1) * DH, s, 8 * lo:8 * lo + 8, 0:NCMP]
                        taps = pe_kv[par * DH:(par + 1) * DH, s, 8 * lo:8 * lo + 8].unsqueeze(2)
                        ins = dve.tensor_tensor(dst, src[:, par:16:2, lo:lo + NCMP],
                                                taps.to_broadcast([DH, 8, NCMP]), ALU.add)
                        if (s, par, lo) != (1, 1, 1):
                            ins.then_inc(S["p3", "parts"], 1)
            ins.then_inc(S["p3", "blk"], 1)
            refill(0, b)
            dve.wait_ge(S["p3", "blkh"], 1)
            low(blkl[:, :, :, :], blk[:, :, :, :], blkh[:, :, :, :].bitcast(F32), S["p3", "blkl"])
            refill(0, b + 1)
            refill(0, b + 2)
            dve.wait_ge(used, b + 4)
            vg = bank[2][:, :].rearrange("p (t c) -> p t c", t=NT)
            dve.tensor_copy(t_c[:, 0:72].rearrange("p (t g) -> p t g", t=NT), vg[:, :, P:P + 36]
                            ).then_inc(S["p3", "gate_in"], 1)
            dve.tensor_copy(v_s[:, :, :], vg[:, :, 0:P]).then_inc(S["p3", "free_dve"], 1)
            dve.wait_ge(S["p3", "free_act"], 5)
            dve.tensor_scalar(g_nsa[:, :, :], t_c[:, 72:144].rearrange("p (t g) -> p t g", t=NT), 0.5, 0.5,
                              ALU.mult, ALU.add).then_inc(S["p3", "gate"], 1)
            for n in range(3, NSA_FRONT):
                refill(0, b + n)
            dve.tensor_copy(hid_rows, bank[3][0:16, :]).then_inc(S["p3", "hid_out"], 1)
            dve.wait_ge(S["p3", "gate"], 1)

            def filler(i):
                n = FILL_BLOCK[i]
                bk = bank[PAIR_BANK[n]]
                dve.wait_ge(used, B_PAIRS + n + 1)
                if i < 2:
                    dve.tensor_scalar(qall[:, PAIRS2 + i, :], bk[:, 0:T], -0.125, None, ALU.mult
                                      ).then_inc(S["p3", "fill"], 1)
                elif i == 3:
                    dve.tensor_copy(vm[:, :, :], bk[:, :].rearrange("p (t c) -> p t c", t=NT)
                                    ).then_inc(S["p3", "fill"], 1)
                refill(0, B_PAIRS + n)

            def branch_mins(i):
                dve.wait_ge(S["p3", "bias_in"], i * 16 + 16)
                for br in range(2):
                    for h in range(2):
                        dve.wait_ge(S["p3", "s"], i * 4 + (2 * br + h + 1))
                        score_min("p3", br, h, bank[2 * br + h], NO_KEY)
                for h in range(2):
                    for t in range(NT):
                        c = 8 + 2 * h + t
                        first_key = (P if t == 0 else 0) + CMP_LEN - 1
                        dve.tensor_tensor_reduce(
                            scc[:, h, t, 0:NCMP], bank[h][:, CAUSAL + 16 * t:CAUSAL + 16 * t + NCMP],
                            bias[:, h, first_key:first_key + CMP_STRIDE * (NCMP - 1) + 1:CMP_STRIDE],
                            1.0, NO_KEY, ALU.add, ALU.min, mx[:, c:c + 1]).then_inc(S["p3", "max"], 1)

            def branch_probs(i, n):
                gate = g_nsa[:, :, i * 6:i * 6 + 6].rearrange("p t (h r) -> p r h t", r=3)
                c = slice(4 * n, 4 * n + 4)
                dve.wait_ge(S["p3", "exp"], i * 12 + 4 * n + 4)
                chain.link(dve.tensor_scalar(deng[:, c], den[:, c], TINY, None, ALU.max))
                chain.link(dve.reciprocal(rden[:, c], deng[:, c]))
                if i and n:
                    dve.wait_ge(S["p3", "prob_pool"], 8 * (i - 1) + 4 * n)
                dve.tensor_tensor(rg[:, c].rearrange("p (h t) -> p h t", h=2),
                                  rden[:, c].rearrange("p (h t) -> p h t", h=2),
                                  gate[:, (1, 2, 0)[n]], ALU.mult).then_inc(S["p3", "rg"], 1)
                if n == 0:
                    dve.wait_ge(S["p3", "rg"], 3 * i + 1)
                    for h in range(2):
                        scale_probs("p3", 0, h, rg, p=prs[i % 2])

            refill(0, B_PAIRS + QUERY_BLOCK[0])
            refill(0, B_PAIRS + QUERY_BLOCK[1])
            filler(0)
            branch_mins(0)
            for n in range(2):
                branch_probs(0, n)
            refill(0, B_PAIRS + QUERY_BLOCK[2])
            filler(1)
            branch_probs(0, 2)

            def nsa(i):
                if i + 1 < PAIRS2:
                    branch_mins(i + 1)
                    for n in range(2):
                        branch_probs(i + 1, n)
                else:
                    memory_softmax("pm3", 0)
                for h in range(2):
                    dve.wait_ge(S["p3", "turned"], i * 5 + (3 + h))
                    dve.tensor_copy(pt[:, 1, h, 0:CAUSAL], bank[4 + h][:, 0:CAUSAL]
                                    ).then_inc(S["p3", "pt_dve"], 1)
                dve.wait_ge(S["p3", "turned"], i * 5 + 5)
                dve.tensor_copy(ptc[0:NCMP, :, :], bank[4][0:NCMP, :].rearrange("p (h t) -> p h t", h=2)
                                ).then_inc(S["p3", "pt_dve"], 1)
                if i + 1 < PAIRS2:
                    branch_probs(i + 1, 2)
                else:
                    memory_probs("pm3", 0)
                if i + 3 < PAIRS2:
                    refill(0, B_PAIRS + QUERY_BLOCK[i + 3])
                elif i + 1 < PAIRS2:
                    filler(i - 1)
                o_low("p3", i, i, 7)

            for i in range(PAIRS2):
                nsa(i)
            finish("pm3", B_ROWS0)
            norm_sum("n2", B_KM - 1, ALPHA, True, "n1", fill=[B_KM - 1, B_KM])
            norm_x("n2", 2, 3)
            refill(0, B_KM + 1)

            def ffn(ph, layer, b0):
                cf = Chain(dve, dchf[layer], 1)

                def taps(i):
                    cf.begin(i)
                    dve.wait_ge(S[ph, "base"], i + 1)
                    cf.link(dve.scalar_tensor_tensor(out=t_a[:, 1:T], in0=bank[0][:, 0:T - 1],
                                                     scalar=convf[:, layer, bass.ds(i, 1), 1], in1=t_a[:, 1:T],
                                                     op0=ALU.mult, op1=ALU.add))
                    dve.scalar_tensor_tensor(out=t_a[:, 2:T], in0=bank[0][:, 0:T - 2],
                                             scalar=convf[:, layer, bass.ds(i, 1), 0], in1=t_a[:, 2:T],
                                             op0=ALU.mult, op1=ALU.add).then_inc(S[ph, "free_a"], 1)
                    cf.end()

                def gated(i, b):
                    dve.wait_ge(used, b)
                    dve.wait_ge(S[ph, "g"], i + 1)
                    dve.tensor_tensor(t_c[:, :], bank[1][:, 0:T], t_b[:, :], ALU.mult).then_inc(S[ph, "m"], 1)
                    dve.wait_ge(S[ph, "mh"], i + 1)
                    low(ml[:, :], t_c[:, :], mh[:, :].bitcast(F32), S[ph, "ml"])

                taps(0)
                refill(0, b0)
                gated(0, b0 + 2)
                refill(0, b0 + 1)

                def body(i):
                    taps(i + 1)
                    refill(i, b0 + 2)
                    refill(i, b0 + 3)
                    gated(i + 1, i * RING + (b0 + 5))
                    refill(i, b0 + 4)

                with dve.Fori(0, FT - 2) as i:
                    body(i)
                body(FT - 2)

            ffn("f0", 0, B_FFN0)
            norm_sum("n3", B_VM - 1, ALPHA, True, "n2", fill=[B_VM - 1, B_VM])
            norm_x("n3", 4, 5)
            refill(0, B_VM + 1)

            for n in range(PAIRS2 - 1):
                refill(0, B_MOBA + n)
            dve.wait_ge(used, B_QK)
            norm_wait(dve, "n3", "x", 2)
            dve.tensor_copy(v_all[:, 0, 0:512], bank[5][:, :]).then_inc(v_up[1], 1)
            dve.tensor_copy(v_all[:, :, 512:PAIRS2 * P], bank[7][:, :].rearrange("p (t c) -> p t c", t=NT)
                            ).then_inc(v_up[1], 1)
            refill(0, B_QK - 1)

            def moba(i):
                b = B_QK + 2 * i
                refill(0, b)
                if i:
                    dve.wait_ge(S["p5", "turned"], 2 * i)
                    dve.tensor_copy(pt[:, 0, 1, 0:CAUSAL], bank[6][:, 0:CAUSAL]).then_inc(S["p5", "pt_dve"], 1)
                dve.wait_ge(S["p5", "bias_in"], i * 16 + 16)
                for h in range(2):
                    dve.wait_ge(S["p5", "s"], i * 2 + (h + 1))
                    score_min("p5", 0, h, bank[3 + h], NO_KEY)
                if i:
                    o_low("p5", i - 1, i - 1, 7)
                refill(0, b + 1)
                dve.wait_ge(S["p5", "exp"], i * 4 + 4)
                chain.link(dve.tensor_scalar(deng[:, 0:4], den[:, 0:4], TINY, None, ALU.max))
                chain.link(dve.reciprocal(rden[:, 0:4], deng[:, 0:4]))
                for h in range(2):
                    scale_probs("p5", 0, h, rden)

            for i in range(PAIRS2):
                moba(i)
            refill(0, B_ROWS1 - 2)
            refill(0, B_ROWS1 - 1)
            dve.wait_ge(S["p5", "turned"], 2 * PAIRS2)
            dve.tensor_copy(pt[:, 0, 1, 0:CAUSAL], bank[6][:, 0:CAUSAL]).then_inc(S["p5", "pt_dve"], 1)
            memory_softmax("pm5", 0)
            o_low("p5", PAIRS2 - 1, PAIRS2 - 1, 7)
            memory_probs("pm5", 0)
            finish("pm5", B_ROWS1)
            norm_sum("n4", B_FFN1 - 1, ALPHA, True, "n3")
            norm_x("n4", 6, 7)
            refill(0, B_FFN1 - 1)
            ffn("f1", 1, B_FFN1)
            norm_sum("n5", N_BLOCKS - 1, ALPHA, True, "n4")

        @block.tensor
        def _(pe):
            def stationary(slot, out, mov_h, mov_l):
                for k in range(KT):
                    pe.matmul(out, wh[slot][:, k, :], mov_h(k), start=k == 0, stop=False)
                    pe.matmul(out, wh[slot][:, k, :], mov_l(k), start=False, stop=False)
                    last = pe.matmul(out, wl[slot][:, k, :], mov_h(k), start=False, stop=k == KT - 1)
                last.then_inc(used, 1)

            def two_stationary(b, nm):
                ready(b + 2)
                for k in range(KT):
                    x_ready(nm)(k)
                    for n in range(2):
                        out, s = bank[n][:, 0:T], slot_of(b + n)
                        pe.matmul(out, wh[s][:, k, :], xh[:, k, :], start=k == 0, stop=False)
                        pe.matmul(out, wh[s][:, k, :], xl[:, k, :], start=False, stop=False)
                        last = pe.matmul(out, wl[s][:, k, :], xh[:, k, :], start=False, stop=k == KT - 1)
                        if k == KT - 1:
                            last.then_inc(used, 1)

            def wide(slot, part, bk, sh, sl, each=None):
                for t in range(NT):
                    out = bk[:, t * T:(t + 1) * T]
                    for j in range(KT // 2):
                        k = part * KT // 2 + j
                        th, tl = sh[:, k, t * P:(t + 1) * P], sl[:, k, t * P:(t + 1) * P]
                        hw = wh[slot][:, 2 * j:2 * j + 2, :].rearrange("p k c -> p (k c)")
                        lw = wl[slot][:, 2 * j:2 * j + 2, :].rearrange("p k c -> p (k c)")
                        pe.matmul(out, th, hw, start=k == 0 and t == 0, stop=False)
                        pe.matmul(out, th, lw, start=False, stop=False)
                        last = pe.matmul(out, tl, hw, start=False, stop=k == KT - 1 and t == NT - 1)
                last.then_inc(used, 1)

            def x_ready(nm):
                def wait(k):
                    norm_wait(pe, nm, "xl_pool" if k % 2 else "xl_dve", k // 2 + 1)
                return wait

            def row(slot, th, tl, start, stop, half=None):
                for t in range(NT):
                    for n in range(2):
                        out = bank[4 + 2 * t + n][:, :]
                        hw = wh[slot][:, 4 * n:4 * n + 4, :].rearrange("p k c -> p (k c)")
                        lw = wl[slot][:, 4 * n:4 * n + 4, :].rearrange("p k c -> p (k c)")
                        pe.matmul(out, th[:, t * P:(t + 1) * P], hw, start=start, stop=False)
                        pe.matmul(out, th[:, t * P:(t + 1) * P], lw, start=False, stop=False)
                        last = pe.matmul(out, tl[:, t * P:(t + 1) * P], hw, start=False, stop=stop)
                    if t == 0 and half is not None:
                        last.then_inc(half, 1)
                last.then_inc(used, 1)

            def ready(b):
                pe.wait_ge(split_l, b)

            def xm(k):
                return xh[:, k, :]

            def xml(k):
                return xl[:, k, :]

            def turn_x(nm, t):
                norm_wait(pe, nm, "z", t + 1)
                for k in range(KT):
                    ins = pe.transpose(turned_x(nm, k)[:, t * P:(t + 1) * P], z[:, t, k * P:(k + 1) * P], ident[:, :])
                    if t == NT - 1:
                        ins.then_inc(S[nm, "turned"], 1)

            def scores(out, q, k, h, s=None, keep=False):
                r = slice(h * DH, (h + 1) * DH)
                for t in range(NT):
                    last = pe.matmul(out[:, s384(t)], q[r, t * P:(t + 1) * P], k[r, 0:(t + 1) * P],
                                     start=True, stop=True)
                if s is not None:
                    last.then_inc(s, 1)

            def turn_p(out, p, s):
                for c in range(3):
                    last = pe.transpose(out[:, c * P:(c + 1) * P], p[:, c * P:(c + 1) * P], ident[:, :])
                last.then_inc(s, 1)

            def pv(h, v, p, start, stop):
                r = slice(h * DH, (h + 1) * DH)
                pe.matmul(bank[7][r, 0:T], v(0), p[:, 0:T], start=start, stop=False)
                return pe.matmul(bank[7][r, P:T], v(1), p[:, T:CAUSAL], start=False, stop=stop)

            def values(i, h):
                return lambda t: v_all[:, t, i * P + h * DH:i * P + (h + 1) * DH]

            pe.wait_ge(set_up, 5)
            for n in range(WARM_UP):
                pe.matmul(bank[4][:, :], zeros[:, 0:P], zeros[:, :], start=True, stop=True)
            pe.wait_ge(ident_up, 1)
            turn_x("n0", 0)
            turn_x("n0", 1)
            for n in range(WARM_UP // 3):
                pe.matmul(bank[4][:, :], zeros[:, 0:P], zeros[:, :], start=True, stop=True)
            for k in range(KT):
                ready(k + 1)
                x_ready("n0")(k)
                row(slot_of(k), xh[:, k, :], xl[:, k, :], k == 0, k == KT - 1)
            pe.wait_ge(consts_in, 16 * 7)
            pe.wait_ge(set_up, 5)
            pe.matmul(bank[3][0:2 * PAIRS2, :], relb[:, :], onehot[:, :], start=True, stop=True
                      ).then_inc(rel_ps, 1)

            def first(i):
                fa, fd = S["p1", "free_act"], S["p1", "free_dve"]
                plan = [("q", fd, 4, 5), ("k", fa, 5, 4), ("xc", fa, 5, 5), ("cg", fa, 5, 6), ("bg", fa, 5, 7),
                        ("zc", fa, 5, 8), ("za", fd, 4, 6), ("gc", fd, 4, 7), ("ga", fd, 4, 8)]
                for p, (kind, free, per, count) in enumerate(plan):
                    ready(i * PER1 + (B_FIRST + p + 1))
                    pe.wait_ge(free, i * per + count)
                    stationary(slot_of(B_FIRST + p), bank[p % 3][:, 0:T], xm, xml)
                    if kind == "xc":
                        pe.wait_ge(fa, i * 5 + 7)
                        pe.wait_ge(v_up[0], 2)
                        pe.wait_ge(rel_sb, 1)
                        for h in range(2):
                            scores(bank[3 + h], q_s, k_s, h, S["p1", "s"])
                    if kind == "zc":
                        for h in range(2):
                            pe.wait_ge(S["p1", "prob"], i * 4 + (2 * h + 2))
                            turn_p(bank[5 + h], pr[:, 0, h, :], S["p1", "turned"])
                    if kind == "gc":
                        pe.wait_ge(S["p1", "pt_act"], i + 1)
                        pe.wait_ge(S["p1", "pt_dve"], i + 1)
                        pe.wait_ge(v_pair, i + 1)
                        pv(0, lambda t: v_s[:, t, 0:DH], pt[:, 0, 0, :], True, True)
                        pv(1, lambda t: v_s[:, t, DH:P], pt[:, 0, 1, :], True, True).then_inc(S["p1", "o"], 1)

            with pe.Fori(0, PAIRS1 - 1) as i:
                first(i)
            first(PAIRS1 - 1)

            def open_banks(ph):
                for n in range(4):
                    pe.matmul(bank[4 + n][:, :], zeros[:, 0:P], zeros[:, :], start=True, stop=False)

            def mix(which, slot, bk):
                stationary(slot, bk[:, 0:T], lambda k: mixh[:, which, k, :], lambda k: mixl[:, which, k, :])

            pe.wait_ge(dch1, 6 * PAIRS1)
            pe.wait_ge(S["p1", "free_act"], 5 + 5 * PAIRS1)
            open_banks("p2")
            ready(B_MIX + 1)
            mix(0, slot_of(B_MIX), bank[0])
            ready(B_MIX + 2)
            mix(1, slot_of(B_MIX + 1), bank[1])
            with pe.Fori(0, KT - 1) as i:
                ready(i * RING + (B_MIX + 3))
                pe.wait_ge(S["p2", "free_a"], i + 1)
                mix(0, slot_of(B_MIX + 2), bank[0])
                ready(i * RING + (B_MIX + 4))
                pe.wait_ge(S["p2", "ml"], i + 1)
                row(slot_of(B_MIX + 3), mh, ml, False, False)
                ready(i * RING + (B_MIX + 5))
                mix(1, slot_of(B_MIX + 4), bank[1])
            ready(B_KM0)
            pe.wait_ge(S["p2", "ml"], KT)
            row(slot_of(B_KM0 - 1), mh, ml, False, True, S["n1", "half"])

            def memory_keys(b, nm):
                for n in range(2):
                    ready(b + n + 1)
                    stationary(slot_of(b + n), bank[2 + n][:, 0:T], lambda k: memh[:, k, :], lambda k: meml[:, k, :])
                    turn_x(nm, n)

            pe.wait_ge(mem_l, 1)
            memory_keys(B_KM0, "n1")

            b = B_NSA
            fa, fd = S["p3", "free_act"], S["p3", "free_dve"]
            two_stationary(b, "n1")
            pe.wait_ge(kv_free, 2)
            for n in range(2):
                ready(b + n + 3)
                wide(slot_of(b + n + 2), n, bank[2], xh, xl)
            pe.wait_ge(S["p3", "blkl"], 1)
            for s in range(2):
                out = bank[3][0:16, s * T:(s + 1) * T]
                for q in range(4):
                    n = 4 + 4 * s + q
                    ready(b + n + 1)
                    sl = slot_of(b + n)
                    for j in range(4):
                        l2 = 4 * q + j
                        hw = wh[sl][:, 2 * j:2 * j + 2, :].rearrange("p k c -> p (k c)")
                        lw = wl[sl][:, 2 * j:2 * j + 2, :].rearrange("p k c -> p (k c)")
                        pe.matmul(out, blkh[:, s, l2, :], hw, start=l2 == 0, stop=False)
                        pe.matmul(out, blkh[:, s, l2, :], lw, start=False, stop=False)
                        last = pe.matmul(out, blkl[:, s, l2, :], hw, start=False, stop=l2 == 15)
                    last.then_inc(used, 1)

            def pair_block(n):
                ready(B_PAIRS + n + 1)
                bk = bank[PAIR_BANK[n]]
                if n >= 8:
                    wide(slot_of(B_PAIRS + n), n - 8, bk, memh, meml)
                else:
                    stationary(slot_of(B_PAIRS + n), bk[:, 0:T], xm, xml)

            pair_block(QUERY_BLOCK[0])
            pe.wait_ge(S["p3", "hid_out"], 1)
            for s in range(2):
                for hf in range(2):
                    n = 2 * s + hf
                    last = pe.transpose(bank[3][:, n * 16:(n + 1) * 16], hid_rows[:, n * P:(n + 1) * P],
                                        ident[0:16, 0:16])
            last.then_inc(S["p3", "hid_in"], 1)
            pair_block(QUERY_BLOCK[1])
            pe.wait_ge(S["p3", "hid"], 1)
            for hf in range(2):
                pe.matmul(bank[3][0:DH, 128:144], w2[:, 0, hf, :], hid[:, 0, hf, :],
                          start=hf == 0, stop=hf == 1)
            for hf in range(2):
                last = pe.matmul(bank[3][0:16, 192:256], hid[:, 1, hf, :], w2[:, 1, hf, :],
                                 start=hf == 0, stop=hf == 1)
            last.then_inc(S["p3", "w2"], 1)
            pair_block(FILL_BLOCK[0])
            pe.wait_ge(fa, 5)
            pe.wait_ge(fd, 1)
            pe.wait_ge(S["p3", "cmp"], 3)

            def pair_scores(i):
                q = qall[:, i, :]
                pe.wait_ge(S["p3", "q"], i + 1)
                if i:
                    pe.wait_ge(S["p3", "max"], 12 * i)
                for br, keys in enumerate((ks2, kw2)):
                    for h in range(2):
                        if br == 0:
                            r = slice(h * DH, (h + 1) * DH)
                            for t in range(NT):
                                pe.matmul(bank[h][:, CAUSAL + 16 * t:CAUSAL + 16 * t + NCMP],
                                          q[r, t * P:(t + 1) * P], kc2[r, 0:NCMP], start=True, stop=True)
                        scores(bank[2 * br + h], q, keys, h, S["p3", "s"])

            def pair_turn(i, br):
                for h in range(2):
                    if br:
                        pe.wait_ge(S["p3", "prob_pool"], i * 8 + (2 * h + 2))
                    else:
                        pe.wait_ge(S["p3", "prob"], i * 4 + (2 * h + 2))
                    turn_p(bank[4 + h], prs[i % 2][:, br, h, :], S["p3", "turned"])

            pair_scores(0)
            pair_block(QUERY_BLOCK[2])
            pe.wait_ge(S["p3", "q"], 2)
            pair_block(FILL_BLOCK[1])

            def memory_scores(ph, j):
                for h in range(2):
                    r = slice(h * DH, (h + 1) * DH)
                    for t in range(NT):
                        last = pe.matmul(bank[h][:, t * T:(t + 1) * T],
                                         qall[r, PAIRS2 + j, t * P:(t + 1) * P], km[r, j, :],
                                         start=True, stop=True)
                    last.then_inc(S[ph, "s"], 1)

            def nsa(i):
                if i + 1 < PAIRS2:
                    pair_scores(i + 1)
                else:
                    pe.wait_ge(S["p3", "max"], 12 * PAIRS2)
                    pe.wait_ge(S["p3", "fill"], 1)
                    memory_scores("pm3", 0)
                if i == 0:
                    pe.wait_ge(S["p3", "fill"], 1)
                    pe.wait_ge(S["p3", "q"], 3)
                pair_turn(i, 0)
                if i == 0:
                    pe.wait_ge(S["p3", "fill"], 2)
                    pair_block(QUERY_BLOCK[3])
                elif i < PAIRS2 - 1:
                    pe.wait_ge(S["p3", "q"], min(i + 3, PAIRS2))
                    pair_block(QUERY_BLOCK[i + 3] if i + 3 < PAIRS2 else FILL_BLOCK[i - 1])
                pe.wait_ge(S["p3", "pt_act"], i * 2 + 2)
                pair_turn(i, 1)
                pe.wait_ge(S["p3", "prob_pool"], i * 8 + 8)
                pe.wait_ge(S["p3", "pt_dve"], i * 3 + 1)
                for h in range(2):
                    for t in range(NT):
                        last = pe.matmul(bank[4][0:NCMP, h * T + t * P:h * T + (t + 1) * P],
                                         prc[i % 2][:, h, t, 0:NCMP], ident[:, :], start=True, stop=True)
                last.then_inc(S["p3", "turned"], 1)
                if i:
                    pe.wait_ge(S["p3", "ol"], i)
                for h in range(2):
                    pv(h, lambda t: v_s[:, t, 0:DH], pt[:, 0, h, :], True, False)
                    if h == 0:
                        pe.wait_ge(S["p3", "pt_dve"], i * 3 + 3)
                    pv(h, lambda t: v_s[:, t, DH:P], pt[:, 1, h, :], False, False)
                    last = pe.matmul(bank[7][h * DH:(h + 1) * DH, 0:T], vc[0:NCMP, :], ptc[0:NCMP, h, :],
                                     start=False, stop=True)
                last.then_inc(S["p3", "o"], 1)

            for i in range(PAIRS2):
                nsa(i)

            def memory_turn(ph, j):
                for h in range(2):
                    pe.wait_ge(S[ph, "prob"], 4 * j + 2 * h + 2)
                    for kk in range(NT):
                        for t in range(NT):
                            last = pe.transpose(bank[2 + h][:, (kk * NT + t) * P:(kk * NT + t + 1) * P],
                                                pr[:, 0, h, t * T + kk * P:t * T + (kk + 1) * P], ident[:, :])
                    last.then_inc(S[ph, "turned"], 1)

            def memory_out(ph, j):
                for h in range(2):
                    pe.wait_ge(S[ph, "pt_act"], j + 1)
                    if h == 1:
                        pe.wait_ge(S[ph, "pt_dve"], j + 1)
                    for kk in range(NT):
                        last = pe.matmul(bank[2][h * DH:(h + 1) * DH, 0:T],
                                         vm[:, kk, j * P + h * DH:j * P + (h + 1) * DH],
                                         pt[:, 0, h, kk * T:(kk + 1) * T], start=kk == 0, stop=kk == 1)
                last.then_inc(S[ph, "o"], 1)

            def finish(ph, main, r0, half):
                def rows(*ks):
                    for k in ks:
                        ready(r0 + k + 1)
                        row(slot_of(r0 + k), oh[:, k, :], ol[:, k, :], k == 0, k == KT - 1,
                            half if k == KT - 1 else None)

                if ph == "pm3":
                    memory_turn(ph, 0)
                pe.wait_ge(S[main, "ol"], PAIRS2)
                rows(0, 1)
                if ph != "pm3":
                    memory_turn(ph, 0)
                rows(2)
                memory_out(ph, 0)
                memory_scores(ph, 1)
                rows(3, 4)
                pe.wait_ge(S[ph, "ol"], 1)
                memory_turn(ph, 1)
                rows(5)
                memory_out(ph, 1)
                rows(6)
                pe.wait_ge(S[ph, "ol"], 2)
                rows(7)

            pe.wait_ge(S["p3", "fill"], 3)
            finish("pm3", "p3", B_ROWS0, S["n2", "half"])
            memory_keys(B_KM, "n2")

            def ffn(ph, b0, nm):
                two_stationary(b0, nm)
                open_banks(ph)

                with pe.Fori(0, FT - 1) as i:
                    ready(i * RING + (b0 + 3))
                    pe.wait_ge(S[ph, "free_a"], i + 1)
                    stationary(slot_of(b0 + 2), bank[0][:, 0:T], xm, xml)
                    ready(i * RING + (b0 + 4))
                    pe.wait_ge(S[ph, "ml"], i + 1)
                    row(slot_of(b0 + 3), mh, ml, False, False)
                    ready(i * RING + (b0 + 5))
                    stationary(slot_of(b0 + 4), bank[1][:, 0:T], xm, xml)
                ready(b0 + 3 * FT)
                pe.wait_ge(S[ph, "ml"], FT)
                row(slot_of(b0 + 3 * FT - 1), mh, ml, False, True, S["n3", "half"])

            ffn("f0", B_FFN0, "n2")
            norm_wait(pe, "n3", "mean", 1)
            for n in range(2):
                ready(B_VM + n + 1)
                wide(slot_of(B_VM + n), n, bank[4], memh, meml)
                turn_x("n3", n)

            for n in range(4):
                b = B_MOBA + n
                ready(b + 1)
                for j in range(2):
                    k = 2 * n + j
                    x_ready("n3")(k)
                    hw = wh[slot_of(b)][:, 4 * j:4 * j + 4, :].rearrange("p k c -> p (k c)")
                    lw = wl[slot_of(b)][:, 4 * j:4 * j + 4, :].rearrange("p k c -> p (k c)")
                    for t in range(NT):
                        tok = slice(t * P, (t + 1) * P)
                        pe.matmul(bank[5 + t][:, :], xh[:, k, tok], hw, start=k == 0, stop=False)
                        pe.matmul(bank[5 + t][:, :], xh[:, k, tok], lw, start=False, stop=False)
                        last = pe.matmul(bank[5 + t][:, :], xl[:, k, tok], hw, start=False, stop=k == KT - 1)
                last.then_inc(used, 1)
            for n in range(2):
                b = B_MOBA + 4 + n
                ready(b + 1)
                wide(slot_of(b), n, bank[7], xh, xl)
            fa, fd = S["p5", "free_act"], S["p5", "free_dve"]

            def moba_turn(i):
                for h in range(2):
                    pe.wait_ge(S["p5", "prob"], i * 4 + (2 * h + 2))
                    turn_p(bank[5 + h], pr[:, 0, h, :], S["p5", "turned"])

            def moba_out(i):
                pe.wait_ge(S["p5", "pt_act"], i + 1)
                pe.wait_ge(S["p5", "pt_dve"], i + 1)
                if i:
                    pe.wait_ge(S["p5", "ol"], i)
                for h in range(2):
                    last = pv(h, values(i, h), pt[:, 0, h, :], True, True)
                last.then_inc(S["p5", "o"], 1)

            def moba(i):
                b = B_QK + 2 * i
                for n in range(2):
                    ready(b + n + 1)
                    if i:
                        pe.wait_ge(fa, 2 * i - 1 + n)
                    stationary(slot_of(b + n), bank[n][:, 0:T], xm, xml)
                if i:
                    moba_turn(i - 1)
                else:
                    pe.wait_ge(v_up[1], 3)
                    pe.wait_ge(kv_free, 5)
                pe.wait_ge(fa, 2 * i + 2)
                for h in range(2):
                    scores(bank[3 + h], q_s, k_s, h, S["p5", "s"])
                if i:
                    moba_out(i - 1)

            for i in range(PAIRS2):
                moba(i)
            b = B_ROWS1 - 2
            for n in range(2):
                ready(b + n + 1)
                stationary(slot_of(b + n), bank[n][:, 0:T], xm, xml)
            moba_turn(PAIRS2 - 1)
            pe.wait_ge(fa, 2 * PAIRS2 + 2)
            memory_scores("pm5", 0)
            moba_out(PAIRS2 - 1)
            finish("pm5", "p5", B_ROWS1, S["n4", "half"])
            for t in range(NT):
                turn_x("n4", t)
            ffn("f1", B_FFN1, "n4")


def _columns(w, c0, width=P):
    k = w.shape[0] // P
    part = w.reshape(k, P, -1)[:, :, c0:c0 + width]
    return part.transpose(1, 0, 2)


def _stream(v):
    blocks = []

    def add(x):
        blocks.append(np.ascontiguousarray(x).reshape(P, KT * P))

    w_in = v["w_in"][0]
    v1 = 6
    order = [4, 5, 0, 2, 1, 3, 7, 8, 9]
    for k in range(KT):
        add(w_in[k * P:(k + 1) * P, v1 * D:(v1 + 1) * D])
    for i in range(PAIRS1):
        for s in order:
            add(_columns(w_in, s * D + i * P))
    wc, wa, wo = v["w_out_conv"][0], v["w_out_attn"][0], v["w_o"][0]

    def skewed(n, first, second, rows):
        add(_columns(first, 0))
        add(_columns(second, 0))
        for j in range(1, n):
            add(_columns(first, j * P))
            add(rows[(j - 1) * P:j * P])
            add(_columns(second, j * P))
        add(rows[(n - 1) * P:n * P])

    skewed(KT, wc, wa, wo)
    aw = v["a_w_in_2"][0]
    q_w, hd = PAIRS2 * P, DH
    kc, vcmp, ks, vs, kw, vw, g, qm = (q_w, q_w + hd, q_w + 2 * hd, q_w + 3 * hd, q_w + 4 * hd,
                                       q_w + 5 * hd, q_w + 6 * hd, q_w + 6 * hd + 36)

    def beside(a, b):
        return np.concatenate([_columns(aw, a, hd), _columns(aw, b, hd)], axis=2)

    kv_a, kv_b = v["a_w_mem_kv_2"][0], v["b_w_mem_kv_2"][0]

    def wide(w):
        t = _columns(w, 0, T)
        return [t[:, n * 4:(n + 1) * 4] for n in range(t.shape[1] // 4)]

    for n in range(2):
        add(_columns(kv_a, n * P))
    add(beside(kc, vcmp))
    add(beside(ks, kw))
    for t in wide(np.concatenate([aw[:, vs:vs + hd], aw[:, vw:vw + hd], aw[:, g:g + 36],
                                  np.zeros((D, P - 36), aw.dtype)], axis=1)):
        add(t)
    for w1 in (v["a_cmp_w1_k_2"][0], v["a_cmp_w1_v_2"][0]):
        for t in wide(w1):
            add(t)
    fill = [_columns(aw, qm), _columns(aw, qm + P)] + wide(kv_a[:, T:2 * T])
    for n in range(len(PAIR_BANK)):
        add(fill[FILL_BLOCK.index(n)] if n in FILL_BLOCK else _columns(aw, QUERY_BLOCK.index(n) * P))
    for k in range(KT):
        add(v["a_w_out_2"][0][k * P:(k + 1) * P])
    for n in range(2):
        add(_columns(kv_b, n * P))

    def ffn(layer):
        w, half_w = v["ffn_w_in_2"][layer], FT * P
        skewed(FT, w[:, :half_w], w[:, half_w:], v["ffn_w_out_2"][layer])

    ffn(0)
    for t in wide(kv_b[:, T:2 * T]):
        add(t)
    kv, bw = v["shared_w_kv_2"], v["b_w_in_2"][0]
    t = _columns(kv, PAIRS2 * P, 512)
    for n in range(4):
        add(t[:, 2 * n:2 * n + 2])
    for t in wide(kv[:, PAIRS2 * P + 512:2 * PAIRS2 * P]):
        add(t)
    for i in range(PAIRS2):
        add(_columns(bw, i * P))
        add(_columns(kv, i * P))
    for i in range(2):
        add(_columns(bw, (PAIRS2 + i) * P))
    for k in range(KT):
        add(v["b_w_out_2"][0][k * P:(k + 1) * P])
    ffn(1)
    assert len(blocks) == N_BLOCKS, len(blocks)
    return np.stack(blocks)


def _alibi():
    delta = P + np.arange(P)[:, None] - np.arange(T)[None, :]
    count = ((delta <= 128).astype(np.float64) + (delta % 4 == 0) + (delta % 16 == 0))
    ok = (delta >= 0) & (count > 0)
    out = np.empty((2 * PAIRS1, P, T), np.float32)
    for h in range(2 * PAIRS1):
        slope = 2.0 ** (-8.0 * (h + 1) / (2 * PAIRS1))
        out[h] = np.where(ok, slope * delta - np.log(np.maximum(count, 1)), MASKED)
    return np.ascontiguousarray(out.reshape(PAIRS1, 2, P, T).transpose(0, 2, 1, 3)).reshape(PAIRS1, P, 2 * T)


def _distance_hot():
    delta = T - 1 - np.arange(RELW)
    n = np.maximum(delta, 0)
    nf = np.maximum(n, 1).astype(np.float32)
    large = 16 + (np.log(nf / np.float32(16)) / np.float32(np.log(8.0)) * np.float32(16)).astype(np.int32)
    bucket = np.where(n < 16, n, np.minimum(large, 31))
    hot = np.zeros((33, RELW), np.float32)
    for m in range(RELW):
        if delta[m] >= 0:
            hot[bucket[m], m] = -1.0
        else:
            hot[32, m] = 1.0
    return hot


def _tiles(x):
    y = x.reshape(x.shape[:-1] + (x.shape[-1] // P, P))
    return np.ascontiguousarray(np.moveaxis(y, -1, 0))


def kernel(**inputs):
    from concourse import bacc
    from concourse.bass_utils import run_bass_kernel_spmd

    v = {k: np.asarray(x) for k, x in inputs.items()}
    gains = [v["norm_g"][0], v["final_g"], v["ln1_g_2"][0], v["ln1_b_2"][0], v["ln2_g_2"][0], v["ln2_b_2"][0],
             v["ln1_g_2"][1], v["ln1_b_2"][1], v["ln2_g_2"][1], v["ln2_b_2"][1]]
    conv = np.concatenate([v["conv_w"][0], v["conv_w"][0][0:1]])
    conv_f = np.stack([np.concatenate([v["ffn_conv_w_2"][n], v["ffn_conv_b_2"][n][None]]) for n in range(2)])
    pe_kv = np.stack([v["a_cmp_pe_k_2"][0], v["a_cmp_pe_v_2"][0]])
    w2 = np.stack([v["a_cmp_w2_k_2"][0], v["a_cmp_w2_v_2"][0]])
    arrays = {
        "x": v["x"],
        "stream": _stream(v),
        "gains_t": _tiles(np.stack(gains)),
        "conv_t": np.ascontiguousarray(_tiles(conv).transpose(0, 2, 1)),
        "conv_f_t": np.ascontiguousarray(_tiles(conv_f).transpose(0, 1, 3, 2)),
        "b_merge_t": _tiles(v["b_merge"][0].reshape(2, D)),
        "pe_t": np.ascontiguousarray(pe_kv.reshape(2, 16, 2, DH).transpose(2, 3, 0, 1)).reshape(P, 2, 16),
        "w2_t": np.ascontiguousarray(w2.reshape(2, 2, P, DH).transpose(2, 0, 1, 3)),
        "mem_t": np.ascontiguousarray(v["mem_2"][0].T.reshape(KT, P, T).transpose(1, 0, 2)),
        "rel_bias_2": v["rel_bias_2"],
        "distance_hot": _distance_hot(),
        "alibi": _alibi(),
        "final_g": v["final_g"],
        "ln1_g_2": v["ln1_g_2"], "ln1_b_2": v["ln1_b_2"],
        "ln2_g_2": v["ln2_g_2"], "ln2_b_2": v["ln2_b_2"],
    }
    nc = bacc.Bacc("TRN2", target_bir_lowering=False, num_devices=1)
    a = {n: nc.dram_tensor(f"in_{n}", x.shape, mybir.dt.from_np(x.dtype), kind="ExternalInput").ap()
         for n, x in arrays.items()}
    a["out"] = nc.dram_tensor("out", (1, T, D), F32, kind="ExternalOutput").ap()
    build_program(nc, a)
    r = run_bass_kernel_spmd(nc, [{f"in_{n}": x for n, x in arrays.items()}], core_ids=[0])
    return r.results[0]["out"]
```

```python
from contextlib import ExitStack

import numpy as np

import concourse.bass as bass
from concourse import mybir

F32 = mybir.dt.float32
F32R = mybir.dt.float32r
BF16 = mybir.dt.bfloat16
ALU = mybir.AluOpType
ACT = mybir.ActivationFunctionType
AX = mybir.AxisListType

P = 128
T = 256
NT = T // P
D = 1024
KT = D // P
DH = 64
PAIRS1 = 8
PAIRS2 = 6
NCMP = 15
CMP_STRIDE, CMP_LEN = 16, 32
CMP = 16
FT = 2816 // P
EPS_RMS, EPS_LN = 1e-6, 1e-5
ALPHA = 4.0 ** 0.25
TINY = 1e-30
MASKED = 1e30
NO_KEY = 1e20
BIASW = 384
RELW = 512
CAUSAL = P + T

RING = 3
PER1 = 9
B_FIRST = KT
B_MIX = B_FIRST + PAIRS1 * PER1
B_KM0 = B_MIX + 3 * KT
B_NSA = B_KM0 + 2
B_CMP = B_NSA + 4
CMP_BLOCKS = 8
B_ROWS0 = B_CMP + CMP_BLOCKS + PAIRS2 + 4
B_KM = B_ROWS0 + KT
B_FFN0 = B_KM + 2
B_VM = B_FFN0 + 3 * FT
B_MOBA = B_VM + 2
B_QK = B_MOBA + PAIRS2
B_ROWS1 = B_QK + 2 * PAIRS2 + 2
B_FFN1 = B_ROWS1 + KT
N_BLOCKS = B_FFN1 + 3 * FT


QUERY_BLOCK = (0, 1, 3, 5, 6, 7)
FILL_BLOCK = (2, 4, 8, 9)
PAIR_BANK = (5, 6, 4, 5, 6, 4, 6, 6, 6, 6)

WARM_SETUP = 12
WARM_PAIR = 6
WARM_SCORES = 4


def cmp_block(n):
    return B_CMP + n + n // 2


def pair_at(n):
    return B_CMP + 3 * n + 2 if n < CMP_BLOCKS // 2 else B_CMP + CMP_BLOCKS + n


def slot_of(b):
    return b % RING


class Chain:

    def __init__(self, engine, sem, per=0):
        self.engine, self.sem, self.per, self.n, self.i = engine, sem, per, 0, 0

    def begin(self, i):
        self.i, self.n = i, 0

    def link(self, instruction):
        self.n += 1
        instruction.then_inc(self.sem, 1)
        self.engine.wait_ge(self.sem, self.i * self.per + self.n if self.per else self.n)

    def end(self):
        assert self.n == self.per, self.n


def build_program(nc, a):
    ctx = ExitStack()
    with ctx:
        def sb(name, shape, dt=F32):
            return ctx.enter_context(nc.sbuf_tensor("sb_" + name, shape, dt))

        def sem(name):
            return ctx.enter_context(nc.semaphore(name))

        bank = [ctx.enter_context(nc.psum_tensor(f"bank{n}", [P, 512], F32)) for n in range(4)]
        ysum = [ctx.enter_context(nc.psum_tensor(f"ysum{t}", [P, D], F32)) for t in range(NT)]
        bank += [ysum[t][:, n * 512:(n + 1) * 512] for t in range(NT) for n in range(2)]
        rel_rows = nc.dram_tensor("rel_rows", (2 * PAIRS2, P, RELW), F32, kind="Internal").ap()

        raw = [sb(f"raw{n}", [P, KT, P]) for n in range(RING)]
        wh = [sb(f"wh{n}", [P, KT, P], F32R) for n in range(RING)]
        wl = [sb(f"wl{n}", [P, KT, P], F32R) for n in range(RING)]
        x_tok = sb("x_tok", [P, NT, D])
        z = sb("z", [P, NT, D])
        xh = sb("xh", [P, KT, T], F32R)
        xl = sb("xl", [P, KT, T], F32R)
        gb = sb("gb", [P, 2, D])
        gbt = sb("gbt", [P, 10, KT])
        mixh = sb("mixh", [P, 2, KT, T], F32R)
        mixl = sb("mixl", [P, 2, KT, T], F32R)
        gates = sb("gates", [P, 2, KT, T])
        oh, ol = mixh[:, 0], mixl[:, 0]
        memf = sb("memf", [P, KT, T])
        memh = sb("memh", [P, KT, T], F32R)
        meml = sb("meml", [P, KT, T], F32R)
        qall = gates[:, 1]
        mh = sb("mh", [P, 2, T], F32R)
        ml = sb("ml", [P, 2, T], F32R)
        bias = sb("bias", [P, 2, BIASW])
        q_s = sb("q_s", [P, T])
        k_s = sb("k_s", [P, T])
        v_s = sb("v_s", [P, NT, P])
        ks2 = sb("ks2", [P, CMP + T])
        kw2 = sb("kw2", [P, T])
        vc = sb("vc", [16, DH])
        g_nsa = sb("g_nsa", [P, NT, 36])
        km = sb("km", [P, 2, T])
        vm = sb("vm", [P, NT, T])
        blkh = sb("blkh", [P, 2, 16, 16], F32R)
        blkl = sb("blkl", [P, 2, 16, 16], F32R)
        hid = sb("hid", [P, 2, 2, 16])
        w2 = sb("w2", [P, 2, 2, DH])
        pe_kv = sb("pe_kv", [P, 2, 16])
        sc = sb("sc", [P, 2, 2, 512])
        pr = sb("pr", [P, 2, 2, 512])
        pt = sb("pt", [P, 2, 2, 512])
        scc = sb("scc", [P, 2, NT, 16])
        prc = [sb(f"prc{n}", [P, 2, NT, 16]) for n in range(2)]
        ptc = sb("ptc", [16, 2, T])
        mx = sb("mx", [P, 12])
        den = sb("den", [P, 12])
        deng = sb("deng", [P, 12])
        rden = sb("rden", [P, 12])
        rg = sb("rg", [P, 12])
        t_a = sb("t_a", [P, T])
        t_b = sb("t_b", [P, T])
        t_c = sb("t_c", [P, T])
        t_d = sb("t_d", [P, T])
        t_e = sb("t_e", [P, T])
        t_f = sb("t_f", [P, T])
        t_g = sb("t_g", [P, T])
        ident = sb("ident", [P, P])
        zeros = sb("zeros", [P, 512], BF16)
        relb = sb("relb", [33, 2 * PAIRS2])
        convw = sb("convw", [P, KT, 4])
        convf = sb("convf", [P, 2, FT, 4])
        bm = sb("bm", [P, 2, KT])
        bmh = sb("bmh", [P, 2, KT])
        st = sb("st", [P, 16])
        half = sb("half", [P, 1])
        xf = pt[:, :, :, :].rearrange("p b a (s t) -> p (b a s) t", s=2)
        blk = pt[:, 0, 0, :].rearrange("p (s l n) -> p s l n", s=2, l=16)
        onehot = sc[0:33, 0, 0, :]
        relf = ptc[0:2 * PAIRS2, :, :].rearrange("p h c -> p (h c)")
        hid_rows = sc[0:16, 1, 1, :]
        prs = [pr, z[:, :, :].rearrange("p b (h c) -> p b h c", h=2)]
        v_all = z
        sq = pr[:, 0, :, :].rearrange("p h c -> p (h c)")

        landed = [sem(f"landed{n}") for n in range(RING)]
        split_h, split_l, used = sem("split_h"), sem("split_l"), sem("used")
        gains_in, kv_free = sem("gains_in"), sem("kv_free")
        consts_in, ident_up, set_up = sem("consts_in"), sem("ident_up"), sem("set_up")
        dch, ach, pch = sem("dve_chain"), sem("act_chain"), sem("pool_chain")
        dch1, dch2 = sem("dve_pairs"), sem("dve_merge")
        dchf = [sem("dve_ffn0"), sem("dve_ffn1")]
        rel_ps, rel_sb, rel_out = sem("rel_ps"), sem("rel_sb"), sem("rel_out")
        mem_in, mem_h, mem_l = sem("mem_in"), sem("mem_h"), sem("mem_l")
        out_done, seen = sem("out_done"), sem("scores_seen")
        S = {}
        norms = ["n0", "n1", "n2", "n3", "n4", "n5"]
        per_norm = {"sum": 2, "mean": 2, "var": 2, "rstd": 2, "z": 2, "x": 2, "half": 1, "off": 2,
                    "turned": KT, "xf": 6, "xf_act": 2, "xh": KT, "xl_dve": 4, "xl_pool": 4}
        first_norm = {"sum": 1, "mean": 2, "x": 1, "half": 1, "off": 5}
        for what in per_norm:
            one = sem(f"norm_{what}")
            for nm in norms:
                S[nm, what] = one
        x_in, gb_in = [sem(f"x_in{t}") for t in range(NT)], sem("gb_in")

        def turned_x(nm, k):
            bk = bank[(0 if nm in ("n0", "n3") else 4) + k // 2]
            return bk[:, (k % 2) * T:(k % 2 + 1) * T]

        def norm_wait(engine, nm, what, count):
            before = norms.index(nm) - first_norm.get(what, 0)
            engine.wait_ge(S[nm, what], before * per_norm[what] + count)

        for ph in ("p1", "p3", "p5", "pm3", "pm5"):
            for what in ("s", "max", "exp", "prob", "turned", "pt_act", "pt_dve", "o", "oh", "ol"):
                S[ph, what] = sem(f"{ph}_{what}")
        for ph in ("p1", "p3", "p5"):
            for what in ("bias_in", "free_act", "free_dve"):
                S[ph, what] = sem(f"{ph}_{what}")
        for what in ("xc", "tz", "yc", "yc_h", "ta", "ya", "ya_h"):
            S["p1", what] = sem(f"p1_{what}")
        for ph in ("p2", "f0", "f1"):
            for what in ("free_a", "m", "mh", "ml", "base", "g"):
                S[ph, what] = sem(f"{ph}_{what}")
        v_pair = sem("v_pair")
        v_up = [sem("v1_up"), sem("v2_up")]
        for what in ("blk", "blkh", "blkl", "hid_out", "hid_in", "hid", "w2", "cmp", "q", "gate", "gate_in",
                     "fill", "parts", "rg", "prob_pool"):
            S["p3", what] = sem(f"p3_{what}")

        block = ctx.enter_context(nc.Block())

        def s384(t):
            return slice(0, P) if t == 0 else slice(P, CAUSAL)

        @block.sync
        def _(sp):
            def load(b, slot):
                sp.dma_start(raw[slot][:, :, :], a["stream"][bass.ds(b, 1)].rearrange(
                    "a p (k c) -> p (a k) c", k=KT)).then_inc(landed[slot], 16)

            for t in range(NT):
                sp.dma_start(x_tok[:, t, :], a["x"][0, t * P:(t + 1) * P, :]).then_inc(x_in[t], 16)
            sp.dma_start(gbt[:, :, :], a["gains_t"]).then_inc(gains_in, 16)
            for b in range(RING):
                load(b, slot_of(b))
            sp.dma_start(convw[:, :, :], a["conv_t"]).then_inc(consts_in, 16)
            sp.dma_start(bm[:, :, :], a["b_merge_t"]).then_inc(consts_in, 16)
            sp.dma_start(onehot[:, :], a["distance_hot"]).then_inc(consts_in, 16)
            sp.dma_start(relb[0:32, :], a["rel_bias_2"]).then_inc(consts_in, 16)
            sp.dma_start(convf[:, :, :, :], a["conv_f_t"]).then_inc(consts_in, 16)
            sp.dma_start(pe_kv[:, :, :], a["pe_t"]).then_inc(consts_in, 16)
            sp.dma_start(w2[:, :, :, :], a["w2_t"]).then_inc(consts_in, 16)
            with sp.Fori(1, N_BLOCKS // RING) as i:
                for n in range(RING):
                    sp.wait_ge(split_l, i * RING + (n - RING + 1))
                    load(i * RING + n, n)
            for b in range(N_BLOCKS // RING * RING, N_BLOCKS):
                sp.wait_ge(split_l, b - RING + 1)
                load(b, slot_of(b))
            for t in range(NT):
                norm_wait(sp, "n5", "z", t + 1)
                sp.dma_start(a["out"][0, t * P:(t + 1) * P, :], x_tok[:, t, :]).then_inc(out_done, 16)
            sp.wait_ge(out_done, 16 * NT)

        @block.gpsimd
        def _(pool):
            chain = Chain(pool, pch)
            pool.memset(half[:, :], -0.5).then_inc(set_up, 1)
            chain.link(pool.memset(ident[:, :], 0.0))
            pool.affine_select(out=ident[:, :], in_=ident[:, :], compare_op=ALU.not_equal, fill=1.0,
                               base=0, pattern=[[-1, P]], channel_multiplier=1).then_inc(ident_up, 1)
            pool.memset(zeros[:, :], 0.0).then_inc(set_up, 1)
            pool.wait_ge(set_up, 5)

            def rstd(nm, t, eps):
                norm_wait(pool, nm, "var", t + 1)
                chain.link(pool.tensor_scalar(st[:, 8 + t:9 + t], st[:, 6 + t:7 + t], 1.0 / D, eps,
                                              ALU.mult, ALU.add))
                pool.tensor_tensor(st[:, 10 + t:11 + t], st[:, 8 + t:9 + t], half[:, :],
                                   ALU.pow).then_inc(S[nm, "rstd"], 1)

            def load_gb(gain, shift):
                pool.dma_start(gb[:, 0, :], gain.partition_broadcast(P)).then_inc(gb_in, 16)
                if shift is not None:
                    pool.dma_start(gb[:, 1, :], shift.partition_broadcast(P)).then_inc(gb_in, 16)

            def tail(nm, shift):
                pool.wait_ge(gb_in, 16 + 32 * (norms.index(nm) - 1))
                for t in range(NT):
                    norm_wait(pool, nm, "z", t + 1)
                    last = pool.tensor_tensor(x_tok[:, t, :], z[:, t, :], gb[:, 0, :], ALU.mult)
                    if shift:
                        chain.link(last)
                        last = pool.tensor_tensor(x_tok[:, t, :], x_tok[:, t, :], gb[:, 1, :], ALU.add)
                    last.then_inc(S[nm, "x"], 1)

            def low_odd(nm):
                for k in range(1, KT, 2):
                    norm_wait(pool, nm, "xh", k + 1)
                    pool.tensor_tensor(xl[:, k, :], xf[:, k, :], xh[:, k, :].bitcast(F32), ALU.subtract
                                       ).then_inc(S[nm, "xl_pool"], 1)

            def alibi(i):
                if not isinstance(i, int) or i:
                    pool.wait_ge(S["p1", "max"], i * 4)
                pool.dma_start(bias[:, :, 0:T], a["alibi"][bass.ds(i, 1)].rearrange(
                    "a p (h c) -> p (a h) c", h=2)).then_inc(S["p1", "bias_in"], 16)

            for t in range(NT):
                rstd("n0", t, EPS_RMS)
            alibi(0)
            low_odd("n0")
            load_gb(a["final_g"], None)
            def relative_rows(n):
                heads = slice(4 * n, 4 * n + 4)
                pool.dma_start(rel_rows[heads], relf[heads, :].unsqueeze(1).to_broadcast([4, P, RELW])
                               ).then_inc(rel_out, 16)

            def pick_values(i):
                if not isinstance(i, int) or i:
                    pool.wait_ge(S["p1", "o"], i)
                pool.tensor_copy(v_s[:, :, :], v_all[:, :, bass.ds(i * P, P)]).then_inc(v_pair, 1)

            pool.wait_ge(v_up[0], 2)
            pick_values(0)
            pool.wait_ge(rel_sb, 1)
            for i in range(1, 4):
                alibi(i)
                pick_values(i)
                relative_rows(i - 1)
            with pool.Fori(4, PAIRS1) as i:
                alibi(i)
                pick_values(i)
            pool.dma_start(memf[:, :, :], a["mem_t"]).then_inc(mem_in, 16)
            pool.wait_ge(rel_out, 3 * 16)

            def relative(ph, i, per):
                if not isinstance(i, int) or i > 0:
                    pool.wait_ge(S[ph, "max"], i * per)
                pool.dma_start(bias[:, :, :], skewed_rows(i)).then_inc(S[ph, "bias_in"], 16)

            def skewed_rows(i):
                base = bass.AP(rel_rows.tensor, P - 1,
                               [[RELW - 1, P], [P * RELW, 2 * PAIRS2], [1, BIASW]])
                return base[:, bass.ds(i * 2, 2), :]

            pool.wait_ge(S["p1", "max"], 4 * PAIRS1)
            relative("p3", 0, 12)
            pool.wait_ge(mem_h, 2)
            pool.tensor_tensor(meml[:, :, :], memf[:, :, :], memh[:, :, :].bitcast(F32), ALU.subtract
                               ).then_inc(mem_l, 1)
            for t in range(NT):
                rstd("n1", t, EPS_RMS)
            low_odd("n1")
            tail("n1", False)
            norm_wait(pool, "n1", "x", 2)
            load_gb(a["ln1_g_2"][0], a["ln1_b_2"][0])
            for i in range(PAIRS2):
                if i + 1 < PAIRS2:
                    relative("p3", i + 1, 12)
                pool.wait_ge(S["p3", "rg"], 3 * i + 2)
                for h in range(2):
                    for t in range(NT):
                        c = 4 + 2 * h + t
                        p = prs[i % 2][:, 1, h, s384(t)]
                        pool.tensor_scalar(p, p, rg[:, c:c + 1], None, ALU.mult).then_inc(S["p3", "prob_pool"], 1)
                pool.wait_ge(S["p3", "rg"], 3 * i + 3)
                for h in range(2):
                    for t in range(NT):
                        c = 8 + 2 * h + t
                        p = prc[i % 2][:, h, t, 0:NCMP]
                        pool.tensor_scalar(p, p, rg[:, c:c + 1], None, ALU.mult).then_inc(S["p3", "prob_pool"], 1)
            for nm, g, b, row in (("n2", "ln2_g_2", "ln2_b_2", 0),
                                  ("n3", "ln1_g_2", "ln1_b_2", 1),
                                  ("n4", "ln2_g_2", "ln2_b_2", 1)):
                for t in range(NT):
                    rstd(nm, t, EPS_LN)
                low_odd(nm)
                tail(nm, True)
                norm_wait(pool, nm, "x", 2)
                load_gb(a[g][row], a[b][row])
                if nm == "n3":
                    pool.wait_ge(S["p3", "max"], 12 * PAIRS2)
                    relative("p5", 0, 4)
                    with pool.Fori(1, PAIRS2) as i:
                        relative("p5", i, 4)
            for t in range(NT):
                rstd("n5", t, EPS_LN)

        @block.scalar
        def _(act):
            chain = Chain(act, ach)

            def make_high(slot, loads):
                act.wait_ge(landed[slot], loads * 16)
                act.activation(wh[slot][:, :, :], raw[slot][:, :, :], ACT.Copy).then_inc(split_h, 1)

            def refill(i, b, per=RING):
                if isinstance(i, int) and b + per * i + RING >= N_BLOCKS:
                    return
                act.wait_ge(used, i * per + (b + 1))
                make_high(slot_of(b), i * (per // RING) + ((b + RING) // RING + 1))

            def norm_var(nm, centred):
                for t in range(NT):
                    norm_wait(act, nm, "mean" if centred else "sum", t + 1)
                    if t:
                        norm_wait(act, nm, "var", t)
                    act.activation(sq[:, :], (z if nm != "n0" else x_tok)[:, t, :], ACT.Square,
                                   bias=st[:, 4 + t:5 + t] if centred else 0.0,
                                   accum_out=st[:, 6 + t:7 + t]).then_inc(S[nm, "var"], 1)

            def norm_high(nm, g, b):
                def high(k):
                    if k < 6:
                        norm_wait(act, nm, "xf", k + 1)
                    else:
                        norm_wait(act, nm, "xf_act", k - 5)
                    act.activation(xh[:, k, :], xf[:, k, :], ACT.Copy).then_inc(S[nm, "xh"], 1)

                for k in range(4):
                    high(k)
                norm_wait(act, nm, "turned", KT)
                for k in (6, 7):
                    if k == 7:
                        high(4)
                    act.activation(xf[:, k, :], turned_x(nm, k), ACT.Identity,
                                   scale=gbt[:, g, k:k + 1], bias=0.0 if b is None else gbt[:, b, k:k + 1]
                                   ).then_inc(S[nm, "xf_act"], 1)
                for k in range(5, KT):
                    high(k)

            def exps(ph, branch, h, causal=True, to=pr):
                for t in range(NT):
                    c = branch * 4 + h * 2 + t
                    cols = s384(t) if causal else slice(t * T, (t + 1) * T)
                    src = sc[:, branch, h, cols] if causal else bank[h][:, cols]
                    act.activation(to[:, branch, h, cols], src, ACT.Exp, bias=mx[:, c:c + 1], scale=-1.0,
                                   accum_out=den[:, c:c + 1]).then_inc(S[ph, "exp"], 1)

            for t in range(NT):
                act.wait_ge(x_in[t], 16)
                act.activation(z[:, t, :], x_tok[:, t, :], ACT.Square,
                               accum_out=st[:, 6 + t:7 + t]).then_inc(S["n0", "var"], 1)
            for b in range(2):
                make_high(b, 1)
            act.wait_ge(gains_in, 16)
            norm_high("n0", 0, None)
            make_high(2, 1)
            act.wait_ge(consts_in, 16 * 7)
            act.activation(bmh[:, :, :], bm[:, :, :], ACT.Copy, scale=0.5).then_inc(ach, 1)
            chain.n += 1
            act.wait_ge(ach, chain.n)
            for k in range(KT - 1):
                refill(0, k)
            act.wait_ge(used, B_FIRST)
            act.activation(v_all[:, 1, :], ysum[1][:, :], ACT.Copy).then_inc(v_up[0], 1)
            refill(0, KT - 1)

            def first(i):
                def made(p):
                    act.wait_ge(used, i * PER1 + (B_FIRST + p + 1))

                def again(p):
                    refill(i, B_FIRST + p, PER1)

                made(0)
                act.activation(q_s[:, :], bank[0][:, 0:T], ACT.Copy, scale=-0.125
                               ).then_inc(S["p1", "free_act"], 1)
                again(0)
                made(1)
                act.activation(k_s[:, :], bank[1][:, 0:T], ACT.Copy).then_inc(S["p1", "free_act"], 1)
                again(1)
                made(2)
                act.activation(t_a[:, :], bank[2][:, 0:T], ACT.Copy).then_inc(S["p1", "free_act"], 1)
                act.wait_ge(S["p1", "free_act"], i * 5 + 8)
                act.sem_inc(S["p1", "xc"], 1)
                for h in range(2):
                    act.wait_ge(S["p1", "max"], i * 4 + (2 * h + 2))
                    exps("p1", 0, h)
                again(2)
                again(3)
                again(4)
                act.wait_ge(S["p1", "turned"], i * 2 + 1)
                act.activation(pt[:, 0, 0, 0:CAUSAL], bank[5][:, 0:CAUSAL], ACT.Copy
                               ).then_inc(S["p1", "pt_act"], 1)
                made(5)
                act.activation(t_c[:, :], bank[2][:, 0:T], ACT.Tanh, scale=0.5).then_inc(S["p1", "tz"], 1)
                again(5)
                made(6)
                act.activation(t_d[:, :], bank[0][:, 0:T], ACT.Tanh, scale=0.5).then_inc(S["p1", "ta"], 1)
                act.wait_ge(S["p1", "yc"], i + 1)
                act.activation(mixh[:, 0, bass.ds(i, 1), :], t_e[:, :].unsqueeze(1), ACT.Copy
                               ).then_inc(S["p1", "yc_h"], 1)
                again(6)
                made(7)
                act.activation(gates[:, 0, bass.ds(i, 1), :], bank[1][:, 0:T].unsqueeze(1), ACT.Tanh,
                               scale=0.5, bias=bmh[:, 0, bass.ds(i, 1)]).then_inc(S["p1", "free_act"], 1)
                again(7)
                act.wait_ge(S["p1", "ya"], i + 1)
                act.activation(mixh[:, 1, bass.ds(i, 1), :], t_g[:, :].unsqueeze(1), ACT.Copy
                               ).then_inc(S["p1", "ya_h"], 1)
                made(8)
                act.activation(gates[:, 1, bass.ds(i, 1), :], bank[2][:, 0:T].unsqueeze(1), ACT.Tanh,
                               scale=0.5, bias=bmh[:, 1, bass.ds(i, 1)]).then_inc(S["p1", "free_act"], 1)
                again(8)

            with act.Fori(0, PAIRS1 - 1) as i:
                first(i)
            first(PAIRS1 - 1)

            def merge(i, buf=0):
                act.wait_ge(S["p2", "m"], i + 1)
                act.activation(mh[:, buf, :], t_c[:, :], ACT.Copy, scale=0.5).then_inc(S["p2", "mh"], 1)

            refill(0, B_MIX)
            refill(0, B_MIX + 1)
            merge(0)
            act.wait_ge(mem_in, 16)
            for n in range(2):
                part = slice(n * KT // 2, (n + 1) * KT // 2)
                act.activation(memh[:, part, :], memf[:, part, :], ACT.Copy).then_inc(mem_h, 1)
            with act.Fori(0, KT - 2) as i:
                for n in range(3):
                    refill(i, B_MIX + 2 + n)
                merge(i + 1)
            refill(KT - 2, B_MIX + 2)
            merge(KT - 1, 1)
            refill(KT - 2, B_MIX + 3)
            refill(KT - 2, B_MIX + 4)

            def refills(b0, n):
                for b in range(b0, b0 + n):
                    refill(0, b)

            def memory_keys(b):
                act.wait_ge(used, b + 2)
                for n in range(2):
                    act.activation(km[:, n, :], bank[2 + n][:, 0:T], ACT.Copy).then_inc(kv_free, 1)

            norm_var("n1", False)
            refill(0, B_KM0 - 1)
            refill(0, B_KM0)
            norm_high("n1", 1, None)
            memory_keys(B_KM0)
            refill(0, B_KM0 + 1)

            def pt_evac(ph, want, dst, src):
                act.wait_ge(S[ph, "turned"], want)
                act.activation(dst, src, ACT.Copy).then_inc(S[ph, "pt_act"], 1)

            def o_high(ph, i, j, b):
                act.wait_ge(S[ph, "o"], i + 1)
                act.activation(oh[:, bass.ds(j, 1), :], bank[b][:, 0:T].unsqueeze(1), ACT.Copy
                               ).then_inc(S[ph, "oh"], 1)

            def memory_exps(ph, j):
                for h in range(2):
                    act.wait_ge(S[ph, "max"], 2 * j + h + 1)
                    exps(ph, 0, h, causal=False)

            def finish(ph, r0):
                if ph == "pm3":
                    pt_evac(ph, 1, pt[:, 0, 0, :], bank[2][:, :])
                refill(0, r0)
                refill(0, r0 + 1)
                if ph != "pm3":
                    pt_evac(ph, 1, pt[:, 0, 0, :], bank[2][:, :])
                refill(0, r0 + 2)
                o_high(ph, 0, PAIRS2, 2)
                memory_exps(ph, 1)
                refill(0, r0 + 3)
                refill(0, r0 + 4)
                pt_evac(ph, 3, pt[:, 0, 0, :], bank[2][:, :])
                refill(0, r0 + 5)
                o_high(ph, 1, PAIRS2 + 1, 2)
                refill(0, r0 + 6)

            b = B_NSA
            act.wait_ge(used, b + 1)
            refill(0, b)
            act.wait_ge(used, b + 2)
            act.activation(ks2[0:DH, CMP:], bank[1][0:DH, 0:T], ACT.Copy).then_inc(S["p3", "free_act"], 1)
            act.activation(ks2[DH:P, CMP:], bank[1][0:DH, 0:T], ACT.Copy).then_inc(S["p3", "free_act"], 1)
            act.activation(kw2[0:DH, :], bank[1][DH:P, 0:T], ACT.Copy).then_inc(S["p3", "free_act"], 1)
            act.activation(kw2[DH:P, :], bank[1][DH:P, 0:T], ACT.Copy).then_inc(S["p3", "free_act"], 1)
            act.wait_ge(S["p3", "blk"], 1)
            act.activation(blkh[:, :, :, :], blk[:, :, :, :], ACT.Copy).then_inc(S["p3", "blkh"], 1)
            refill(0, b + 1)
            refill(0, b + 2)
            act.wait_ge(S["p3", "gate_in"], 1)
            act.activation(t_c[:, 72:144], t_c[:, 0:72], ACT.Tanh, scale=0.5).then_inc(S["p3", "free_act"], 1)
            refill(0, b + 3)

            def queries(i):
                n = QUERY_BLOCK[i]
                act.wait_ge(used, pair_at(n) + 1)
                act.activation(qall[:, i, :], bank[PAIR_BANK[n]][:, 0:T], ACT.Copy, scale=-0.125
                               ).then_inc(S["p3", "q"], 1)
                refill(0, pair_at(n))

            for n in range(4):
                refill(0, cmp_block(2 * n))
                refill(0, cmp_block(2 * n + 1))
                if n in QUERY_BLOCK:
                    queries(QUERY_BLOCK.index(n))
                else:
                    refill(0, pair_at(n))
            act.wait_ge(S["p3", "hid_in"], 1)
            act.activation(hid[:, :, :, :], bank[3][:, 0:64].rearrange("p (s h n) -> p s h n", s=2, h=2),
                           ACT.Gelu_apprx_tanh).then_inc(S["p3", "hid"], 1)
            refill(0, pair_at(4))
            act.wait_ge(S["p3", "w2"], 1)
            act.activation(ks2[0:DH, 0:CMP], bank[3][0:DH, 128:144], ACT.Copy).then_inc(S["p3", "cmp"], 1)
            act.activation(ks2[DH:P, 0:CMP], bank[3][0:DH, 128:144], ACT.Copy).then_inc(S["p3", "cmp"], 1)
            act.activation(vc[:, :], bank[3][0:16, 192:256], ACT.Copy).then_inc(S["p3", "cmp"], 1)

            def branch_exps(i, br, heads=(0, 1)):
                for h in heads:
                    act.wait_ge(S["p3", "max"], i * 12 + (br * 4 + 2 * h + 2))
                    exps("p3", br, h, to=prs[i % 2])

            def compressed_exps(i):
                act.wait_ge(S["p3", "max"], i * 12 + 12)
                for h in range(2):
                    for t in range(NT):
                        c = 8 + 2 * h + t
                        act.activation(prc[i % 2][:, h, t, 0:NCMP], scc[:, h, t, 0:NCMP], ACT.Exp,
                                       bias=mx[:, c:c + 1], scale=-1.0, accum_out=den[:, c:c + 1]
                                       ).then_inc(S["p3", "exp"], 1)

            branch_exps(0, 0)
            branch_exps(0, 1)
            compressed_exps(0)
            queries(3)
            norm_wait(act, "n1", "x", 2)

            def nsa(i):
                if i + 1 < PAIRS2:
                    branch_exps(i + 1, 0, (0,))
                pt_evac("p3", i * 5 + 1, pt[:, 0, 0, 0:CAUSAL], bank[4][:, 0:CAUSAL])
                if i + 1 < PAIRS2:
                    branch_exps(i + 1, 0, (1,))
                pt_evac("p3", i * 5 + 2, pt[:, 0, 1, 0:CAUSAL], bank[5][:, 0:CAUSAL])
                if i + 1 < PAIRS2:
                    branch_exps(i + 1, 1)
                    compressed_exps(i + 1)
                else:
                    memory_exps("pm3", 0)
                if i + 4 < PAIRS2:
                    queries(i + 4)
                elif i < 4:
                    refill(0, pair_at(6 + i))
                o_high("p3", i, i, 7)

            for i in range(PAIRS2):
                nsa(i)
            finish("pm3", B_ROWS0)
            norm_var("n2", True)
            refill(0, B_KM - 1)
            refill(0, B_KM)
            norm_high("n2", 2, 3)
            memory_keys(B_KM)
            refill(0, B_KM + 1)

            def ffn(ph, layer, b0):
                def base(i):
                    act.activation(t_a[:, :], bank[0][:, 0:T], ACT.Identity,
                                   bias=convf[:, layer, bass.ds(i, 1), 3], scale=convf[:, layer, bass.ds(i, 1), 2]
                                   ).then_inc(S[ph, "base"], 1)

                def gelu(i):
                    act.wait_ge(S[ph, "free_a"], i + 1)
                    act.activation(t_b[:, :], t_a[:, :], ACT.Gelu_apprx_tanh).then_inc(S[ph, "g"], 1)

                def high(i, buf=0):
                    act.wait_ge(S[ph, "m"], i + 1)
                    act.activation(mh[:, buf, :], t_c[:, :], ACT.Copy).then_inc(S[ph, "mh"], 1)

                act.wait_ge(used, b0 + 1)
                base(0)
                refill(0, b0)
                gelu(0)
                refill(0, b0 + 1)
                high(0)

                def body(i):
                    bb = b0 + 2
                    act.wait_ge(used, i * RING + (bb + 1))
                    base(i + 1)
                    refill(i, bb)
                    gelu(i + 1)
                    if isinstance(i, int):
                        high(i + 1, 1)
                        refill(i, bb + 1)
                    else:
                        refill(i, bb + 1)
                        act.wait_ge(used, i * RING + (bb + 3))
                        high(i + 1)
                    refill(i, bb + 2)

                with act.Fori(0, FT - 2) as i:
                    body(i)
                body(FT - 2)

            ffn("f0", 0, B_FFN0)
            norm_var("n3", True)
            refill(0, B_VM - 1)
            refill(0, B_VM)
            norm_high("n3", 4, 5)
            act.wait_ge(used, B_VM + 2)
            act.activation(vm[:, :, :], bank[4][:, :].rearrange("p (t c) -> p t c", t=NT), ACT.Copy
                           ).then_inc(kv_free, 1)
            refill(0, B_VM + 1)

            refills(B_MOBA, PAIRS2 - 1)
            act.wait_ge(used, B_QK)
            norm_wait(act, "n3", "x", 2)
            act.activation(v_all[:, 1, 0:512], bank[6][:, :], ACT.Copy).then_inc(v_up[1], 1)
            refill(0, B_QK - 1)

            def moba(i):
                b = B_QK + 2 * i
                act.wait_ge(used, b + 1)
                act.activation(q_s[:, :], bank[0][:, 0:T], ACT.Copy, scale=-0.125
                               ).then_inc(S["p5", "free_act"], 1)
                refill(0, b)
                act.wait_ge(used, b + 2)
                act.activation(k_s[:, :], bank[1][:, 0:T], ACT.Copy).then_inc(S["p5", "free_act"], 1)
                if i:
                    pt_evac("p5", 2 * i - 1, pt[:, 0, 0, 0:CAUSAL], bank[5][:, 0:CAUSAL])
                for h in range(2):
                    act.wait_ge(S["p5", "max"], i * 4 + (2 * h + 2))
                    exps("p5", 0, h)
                if i:
                    o_high("p5", i - 1, i - 1, 7)
                refill(0, b + 1)

            for i in range(PAIRS2):
                moba(i)
            b = B_ROWS1 - 2
            for n in range(2):
                act.wait_ge(used, b + 1 + n)
                act.activation(qall[:, PAIRS2 + n, :], bank[n][:, 0:T], ACT.Copy, scale=-0.125
                               ).then_inc(S["p5", "free_act"], 1)
                if n == 0:
                    refill(0, b)
            pt_evac("p5", 2 * PAIRS2 - 1, pt[:, 0, 0, 0:CAUSAL], bank[5][:, 0:CAUSAL])
            refill(0, b + 1)
            o_high("p5", PAIRS2 - 1, PAIRS2 - 1, 7)
            memory_exps("pm5", 0)
            finish("pm5", B_ROWS1)
            norm_var("n4", True)
            norm_high("n4", 6, 7)
            refill(0, B_FFN1 - 1)
            ffn("f1", 1, B_FFN1)
            norm_var("n5", True)

        @block.vector
        def _(dve):
            chain = Chain(dve, dch)

            def make_low(slot, count):
                dve.wait_ge(split_h, count)
                dve.tensor_tensor(wl[slot][:, :, :], raw[slot][:, :, :], wh[slot][:, :, :].bitcast(F32),
                                  ALU.subtract).then_inc(split_l, 1)

            def refill(i, b, per=RING):
                if isinstance(i, int) and b + per * i + RING >= N_BLOCKS:
                    return
                make_low(slot_of(b), i * per + (b + RING + 1))

            def low(dst, src, high, s):
                dve.tensor_tensor(dst, src, high, ALU.subtract).then_inc(s, 1)

            def norm_x(nm, g, b, between=None):
                def fetch(k):
                    norm_wait(dve, nm, "turned", k // 2 * 2 + 2)
                    ps = turned_x(nm, k)
                    if b is None:
                        dve.tensor_scalar(xf[:, k, :], ps, gbt[:, g, k:k + 1], None, ALU.mult
                                          ).then_inc(S[nm, "xf"], 1)
                    else:
                        dve.tensor_scalar(xf[:, k, :], ps, gbt[:, g, k:k + 1], gbt[:, b, k:k + 1],
                                          ALU.mult, ALU.add).then_inc(S[nm, "xf"], 1)

                def low_even(k):
                    norm_wait(dve, nm, "xh", k + 1)
                    low(xl[:, k, :], xf[:, k, :], xh[:, k, :].bitcast(F32), S[nm, "xl_dve"])

                for k in range(0, 6, 2):
                    fetch(k)
                    fetch(k + 1)
                    low_even(k)
                    if k == 0 and between is not None:
                        between()
                low_even(6)

            def norm_sum(nm, last_block, alpha, centred, x_from, fill=()):
                fill = list(fill)
                if x_from:
                    norm_wait(dve, x_from, "x", 2)
                for t in range(NT):
                    if t == 0:
                        norm_wait(dve, nm, "half", 1)
                    else:
                        dve.wait_ge(used, last_block + 1)
                    ins = dve.scalar_tensor_tensor(out=z[:, t, :], in0=x_tok[:, t, :], scalar=alpha,
                                                   in1=ysum[t][:, :], op0=ALU.mult, op1=ALU.add,
                                                   accum_out=st[:, t:t + 1])
                    if centred:
                        chain.link(ins)
                        dve.tensor_scalar(st[:, 4 + t:5 + t], st[:, t:t + 1], -1.0 / D, None,
                                          ALU.mult).then_inc(S[nm, "mean"], 1)
                    else:
                        ins.then_inc(S[nm, "sum"], 1)
                if nm == "n5":
                    dve.wait_ge(gb_in, 16 + 32 * 4)
                    for t in range(NT):
                        norm_wait(dve, nm, "mean", t + 1)
                        dve.scalar_tensor_tensor(out=x_tok[:, t, :], in0=z[:, t, :], scalar=st[:, 4 + t:5 + t],
                                                 in1=gb[:, 0, :], op0=ALU.add, op1=ALU.mult
                                                 ).then_inc(S[nm, "off"], 1)
                    for t in range(NT):
                        norm_wait(dve, nm, "off", t + 1)
                        norm_wait(dve, nm, "rstd", t + 1)
                        dve.scalar_tensor_tensor(out=x_tok[:, t, :], in0=x_tok[:, t, :],
                                                 scalar=st[:, 10 + t:11 + t], in1=gb[:, 1, :],
                                                 op0=ALU.mult, op1=ALU.add).then_inc(S[nm, "z"], 1)
                    return
                for t in range(NT):
                    norm_wait(dve, nm, "rstd", t + 1)
                    if centred:
                        norm_wait(dve, nm, "mean", t + 1)
                        dve.tensor_scalar(z[:, t, :], z[:, t, :], st[:, 4 + t:5 + t],
                                          st[:, 10 + t:11 + t], ALU.add, ALU.mult).then_inc(S[nm, "z"], 1)
                    else:
                        norm_wait(dve, nm, "sum", t + 1)
                        dve.tensor_scalar(z[:, t, :], z[:, t, :], st[:, 10 + t:11 + t], None,
                                          ALU.mult).then_inc(S[nm, "z"], 1)
                    if t == NT - 1:
                        for b in fill:
                            refill(0, b)

            def score_min(ph, branch, h, src, guard, lead=0):
                dve.sem_inc(seen, 1)
                for t in range(NT):
                    c = branch * 4 + h * 2 + t
                    keys = slice(P, T) if t == 0 else slice(0, T)
                    cols = slice(s384(t).start + lead * (t + 1), s384(t).stop + lead * (t + 1))
                    dve.tensor_tensor_reduce(sc[:, branch, h, s384(t)], src[:, cols], bias[:, h, keys],
                                             1.0, guard, ALU.add, ALU.min, mx[:, c:c + 1]
                                             ).then_inc(S[ph, "max"], 1)

            def scale_probs(ph, branch, h, factor, causal=True, p=pr):
                for t in range(NT):
                    c = branch * 4 + h * 2 + t
                    cols = s384(t) if causal else slice(t * T, (t + 1) * T)
                    dve.tensor_scalar(p[:, branch, h, cols], p[:, branch, h, cols],
                                      factor[:, c:c + 1], None, ALU.mult).then_inc(S[ph, "prob"], 1)

            def o_low(ph, i, j, b):
                dve.wait_ge(S[ph, "oh"], i + 1)
                low(ol[:, bass.ds(j, 1), :], bank[b][:, 0:T].unsqueeze(1), oh[:, bass.ds(j, 1), :].bitcast(F32),
                    S[ph, "ol"])

            dve.memset(mx[:, :], 0.0).then_inc(set_up, 1)
            dve.memset(relb[32:33, :], MASKED).then_inc(set_up, 1)
            dve.memset(t_g[:, :], 0.0).then_inc(set_up, 1)
            dve.memset(t_f[:, :], 0.0).then_inc(S["p1", "free_dve"], 5)
            dve.memset(t_e[:, :], 0.0).then_inc(S["p1", "free_act"], 5)
            for t in range(NT):
                norm_wait(dve, "n0", "rstd", t + 1)
                dve.tensor_scalar(z[:, t, :], x_tok[:, t, :], st[:, 10 + t:11 + t], None,
                                  ALU.mult).then_inc(S["n0", "z"], 1)
            dve.wait_ge(gains_in, 16)
            make_low(0, 1)
            norm_x("n0", 0, None, lambda: make_low(1, 2))
            make_low(2, 3)
            for k in range(KT - 1):
                refill(0, k)
            dve.wait_ge(used, B_FIRST)
            dve.tensor_copy(v_all[:, 0, :], ysum[0][:, :]).then_inc(v_up[0], 1)
            dve.wait_ge(rel_ps, 1)
            dve.tensor_copy(relf[:, :], bank[3][0:2 * PAIRS2, :]).then_inc(rel_sb, 1)
            refill(0, KT - 1)

            c1 = Chain(dve, dch1, 6)

            def first(i):
                def made(p):
                    dve.wait_ge(used, i * PER1 + (B_FIRST + p + 1))

                def again(p):
                    refill(i, B_FIRST + p, PER1)

                c1.begin(i)
                again(0)
                again(1)
                dve.wait_ge(S["p1", "bias_in"], i * 16 + 16)
                for h in range(2):
                    dve.wait_ge(S["p1", "s"], i * 2 + (h + 1))
                    score_min("p1", 0, h, bank[3 + h], 3e38)
                made(3)
                dve.wait_ge(S["p1", "xc"], i + 1)
                dve.tensor_tensor(t_b[:, :], bank[0][:, 0:T], t_a[:, :], ALU.mult
                                  ).then_inc(S["p1", "free_dve"], 1)
                again(2)
                dve.wait_ge(S["p1", "exp"], i * 4 + 4)
                c1.link(dve.reciprocal(rden[:, 0:4], den[:, 0:4]))
                for h in range(2):
                    scale_probs("p1", 0, h, rden)
                again(3)
                dve.wait_ge(S["p1", "free_dve"], i * 4 + 6)
                c1.link(dve.tensor_scalar(t_f[:, :], t_b[:, :], convw[:, bass.ds(i, 1), 2], None, ALU.mult))
                c1.link(dve.scalar_tensor_tensor(out=t_f[:, 1:T], in0=t_b[:, 0:T - 1],
                                                 scalar=convw[:, bass.ds(i, 1), 1], in1=t_f[:, 1:T],
                                                 op0=ALU.mult, op1=ALU.add))
                c1.link(dve.scalar_tensor_tensor(out=t_f[:, 2:T], in0=t_b[:, 0:T - 2],
                                                 scalar=convw[:, bass.ds(i, 1), 0], in1=t_f[:, 2:T],
                                                 op0=ALU.mult, op1=ALU.add))
                made(4)
                dve.tensor_tensor(t_b[:, :], bank[1][:, 0:T], t_f[:, :], ALU.mult
                                  ).then_inc(S["p1", "free_dve"], 1)
                again(4)
                dve.wait_ge(S["p1", "turned"], i * 2 + 2)
                dve.tensor_copy(pt[:, 0, 1, 0:CAUSAL], bank[6][:, 0:CAUSAL]).then_inc(S["p1", "pt_dve"], 1)
                dve.wait_ge(S["p1", "free_dve"], i * 4 + 7)
                dve.wait_ge(S["p1", "tz"], i + 1)
                dve.scalar_tensor_tensor(out=t_f[:, :], in0=t_c[:, :], scalar=1.0, in1=bank[2][:, 0:T],
                                         op0=ALU.add, op1=ALU.mult).then_inc(S["p1", "free_dve"], 1)
                dve.wait_ge(S["p1", "free_dve"], i * 4 + 8)
                dve.scalar_tensor_tensor(out=t_e[:, :], in0=t_f[:, :], scalar=0.5, in1=t_b[:, :],
                                         op0=ALU.mult, op1=ALU.mult).then_inc(S["p1", "yc"], 1)
                again(5)
                dve.wait_ge(S["p1", "yc"], i + 1)
                dve.wait_ge(S["p1", "ta"], i + 1)
                dve.scalar_tensor_tensor(out=t_f[:, :], in0=t_d[:, :], scalar=1.0, in1=bank[0][:, 0:T],
                                         op0=ALU.add, op1=ALU.mult).then_inc(S["p1", "free_dve"], 1)
                dve.wait_ge(S["p1", "yc_h"], i + 1)
                c1.link(dve.tensor_tensor(mixl[:, 0, bass.ds(i, 1), :], t_e[:, :].unsqueeze(1),
                                          mixh[:, 0, bass.ds(i, 1), :].bitcast(F32), ALU.subtract))
                again(6)
                dve.wait_ge(S["p1", "o"], i + 1)
                dve.wait_ge(S["p1", "free_dve"], i * 4 + 9)
                dve.scalar_tensor_tensor(out=t_g[:, :], in0=bank[7][:, 0:T], scalar=0.5, in1=t_f[:, :],
                                         op0=ALU.mult, op1=ALU.mult).then_inc(S["p1", "ya"], 1)
                again(7)
                dve.wait_ge(S["p1", "ya_h"], i + 1)
                c1.link(dve.tensor_tensor(mixl[:, 1, bass.ds(i, 1), :], t_g[:, :].unsqueeze(1),
                                          mixh[:, 1, bass.ds(i, 1), :].bitcast(F32), ALU.subtract))
                again(8)
                c1.end()

            with dve.Fori(0, PAIRS1 - 1) as i:
                first(i)
            first(PAIRS1 - 1)

            c2 = Chain(dve, dch2, 2)

            def part_c(i, b):
                dve.wait_ge(used, b)
                if isinstance(i, int):
                    dve.wait_ge(S["p1", "free_act"], 5 * PAIRS1 + 5)
                dve.scalar_tensor_tensor(out=t_a[:, :].unsqueeze(1), in0=gates[:, 0, bass.ds(i, 1), :], scalar=1.0,
                                         in1=bank[0][:, 0:T].unsqueeze(1), op0=ALU.add, op1=ALU.mult
                                         ).then_inc(S["p2", "free_a"], 1)

            def part_a(i, b, buf=0):
                dve.wait_ge(used, b)
                c2.begin(i)
                c2.link(dve.scalar_tensor_tensor(out=t_b[:, :].unsqueeze(1), in0=gates[:, 1, bass.ds(i, 1), :],
                                                 scalar=1.0, in1=bank[1][:, 0:T].unsqueeze(1),
                                                 op0=ALU.add, op1=ALU.mult))
                dve.wait_ge(S["p2", "free_a"], i + 1)
                c2.link(dve.tensor_tensor(t_c[:, :], t_a[:, :], t_b[:, :], ALU.add))
                c2.end()
                dve.sem_inc(S["p2", "m"], 1)
                dve.wait_ge(S["p2", "mh"], i + 1)
                dve.scalar_tensor_tensor(out=ml[:, buf, :], in0=t_c[:, :], scalar=0.5, in1=mh[:, buf, :].bitcast(F32),
                                         op0=ALU.mult, op1=ALU.subtract).then_inc(S["p2", "ml"], 1)

            part_c(0, B_MIX + 1)
            refill(0, B_MIX)
            part_a(0, B_MIX + 2)
            refill(0, B_MIX + 1)
            with dve.Fori(0, KT - 2) as i:
                part_c(i + 1, i * RING + (B_MIX + 3))
                refill(i, B_MIX + 2)
                refill(i, B_MIX + 3)
                part_a(i + 1, i * RING + (B_MIX + 5))
                refill(i, B_MIX + 4)
            part_c(KT - 1, B_KM0 - 3)
            refill(KT - 2, B_MIX + 2)
            part_a(KT - 1, B_KM0 - 2, 1)
            refill(KT - 2, B_MIX + 3)
            refill(KT - 2, B_MIX + 4)

            norm_sum("n1", B_KM0 - 1, 1.0, False, None, fill=[B_KM0 - 1, B_KM0])
            norm_x("n1", 1, None)
            refill(0, B_KM0 + 1)

            def memory_softmax(ph, j):
                for h in range(2):
                    dve.wait_ge(S[ph, "s"], 2 * j + h + 1)
                    dve.tensor_reduce(mx[:, 2 * h:2 * h + 2],
                                      bank[h][:, :].rearrange("p (t c) -> p t c", t=NT), AX.X, ALU.min
                                      ).then_inc(S[ph, "max"], 1)

            def memory_probs(ph, j):
                dve.wait_ge(S[ph, "exp"], 4 * j + 4)
                chain.link(dve.reciprocal(rden[:, 0:4], den[:, 0:4]))
                for h in range(2):
                    scale_probs(ph, 0, h, rden, causal=False)

            def finish(ph, r0):
                def transposed(j):
                    dve.wait_ge(S[ph, "turned"], 2 * j + 2)
                    dve.tensor_copy(pt[:, 0, 1, :], bank[3][:, :]).then_inc(S[ph, "pt_dve"], 1)

                if ph == "pm3":
                    transposed(0)
                refill(0, r0)
                refill(0, r0 + 1)
                if ph != "pm3":
                    transposed(0)
                refill(0, r0 + 2)
                o_low(ph, 0, PAIRS2, 2)
                memory_softmax(ph, 1)
                memory_probs(ph, 1)
                refill(0, r0 + 3)
                refill(0, r0 + 4)
                transposed(1)
                refill(0, r0 + 5)
                o_low(ph, 1, PAIRS2 + 1, 2)
                refill(0, r0 + 6)

            b = B_NSA
            dve.wait_ge(used, b + 1)
            chain.link(dve.memset(blk[:, :, :, :], 0.0))
            for s in range(2):
                for par in range(2):
                    src = bank[0][s * DH:(s + 1) * DH, 0:T].rearrange("p (n l) -> p l n", l=16)
                    for lo in range(2):
                        dst = blk[par * DH:(par + 1) * DH, s, 8 * lo:8 * lo + 8, 0:NCMP]
                        taps = pe_kv[par * DH:(par + 1) * DH, s, 8 * lo:8 * lo + 8].unsqueeze(2)
                        ins = dve.tensor_tensor(dst, src[:, par:16:2, lo:lo + NCMP],
                                                taps.to_broadcast([DH, 8, NCMP]), ALU.add)
                        if (s, par, lo) != (1, 1, 1):
                            ins.then_inc(S["p3", "parts"], 1)
            ins.then_inc(S["p3", "blk"], 1)
            refill(0, b)
            dve.wait_ge(S["p3", "blkh"], 1)
            low(blkl[:, :, :, :], blk[:, :, :, :], blkh[:, :, :, :].bitcast(F32), S["p3", "blkl"])
            refill(0, b + 1)
            refill(0, b + 2)
            dve.wait_ge(used, b + 4)
            vg = bank[2][:, :].rearrange("p (t c) -> p t c", t=NT)
            dve.tensor_copy(t_c[:, 0:72].rearrange("p (t g) -> p t g", t=NT), vg[:, :, P:P + 36]
                            ).then_inc(S["p3", "gate_in"], 1)
            dve.tensor_copy(v_s[:, :, :], vg[:, :, 0:P]).then_inc(S["p3", "free_dve"], 1)
            dve.wait_ge(S["p3", "free_act"], 5)
            dve.tensor_scalar(g_nsa[:, :, :], t_c[:, 72:144].rearrange("p (t g) -> p t g", t=NT), 0.5, 0.5,
                              ALU.mult, ALU.add).then_inc(S["p3", "gate"], 1)
            refill(0, b + 3)

            def filler(i):
                n = FILL_BLOCK[i]
                bk = bank[PAIR_BANK[n]]
                dve.wait_ge(used, pair_at(n) + 1)
                if i < 2:
                    dve.tensor_scalar(qall[:, PAIRS2 + i, :], bk[:, 0:T], -0.125, None, ALU.mult
                                      ).then_inc(S["p3", "fill"], 1)
                elif i == 3:
                    dve.tensor_copy(vm[:, :, :], bk[:, :].rearrange("p (t c) -> p t c", t=NT)
                                    ).then_inc(S["p3", "fill"], 1)
                refill(0, pair_at(n))

            def branch_mins(i):
                dve.wait_ge(S["p3", "bias_in"], i * 16 + 16)
                for br in range(2):
                    for h in range(2):
                        dve.wait_ge(S["p3", "s"], i * 4 + (2 * br + h + 1))
                        score_min("p3", br, h, bank[2 * br + h], NO_KEY, CMP if br == 0 else 0)
                for h in range(2):
                    for t in range(NT):
                        c = 8 + 2 * h + t
                        first_key = (P if t == 0 else 0) + CMP_LEN - 1
                        dve.tensor_tensor_reduce(
                            scc[:, h, t, 0:NCMP], bank[h][:, (CMP + P) * t:(CMP + P) * t + NCMP],
                            bias[:, h, first_key:first_key + CMP_STRIDE * (NCMP - 1) + 1:CMP_STRIDE],
                            1.0, NO_KEY, ALU.add, ALU.min, mx[:, c:c + 1]).then_inc(S["p3", "max"], 1)

            def branch_probs(i, n):
                gate = g_nsa[:, :, i * 6:i * 6 + 6].rearrange("p t (h r) -> p r h t", r=3)
                c = slice(4 * n, 4 * n + 4)
                dve.wait_ge(S["p3", "exp"], i * 12 + 4 * n + 4)
                chain.link(dve.tensor_scalar(deng[:, c], den[:, c], TINY, None, ALU.max))
                chain.link(dve.reciprocal(rden[:, c], deng[:, c]))
                if i and n:
                    dve.wait_ge(S["p3", "prob_pool"], 8 * (i - 1) + 4 * n)
                dve.tensor_tensor(rg[:, c].rearrange("p (h t) -> p h t", h=2),
                                  rden[:, c].rearrange("p (h t) -> p h t", h=2),
                                  gate[:, (1, 2, 0)[n]], ALU.mult).then_inc(S["p3", "rg"], 1)
                if n == 0:
                    dve.wait_ge(S["p3", "rg"], 3 * i + 1)
                    for h in range(2):
                        scale_probs("p3", 0, h, rg, p=prs[i % 2])

            for n in range(4):
                refill(0, cmp_block(2 * n))
                if n == 3:
                    dve.wait_ge(used, cmp_block(2 * n + 1) + 1)
                    dve.tensor_copy(hid_rows, bank[3][0:16, :]).then_inc(S["p3", "hid_out"], 1)
                refill(0, cmp_block(2 * n + 1))
                if n == FILL_BLOCK[0]:
                    filler(0)
                else:
                    refill(0, pair_at(n))
            filler(1)
            dve.wait_ge(S["p3", "gate"], 1)
            branch_mins(0)
            for n in range(2):
                branch_probs(0, n)
            refill(0, pair_at(QUERY_BLOCK[3]))
            branch_probs(0, 2)

            def nsa(i):
                if i + 1 < PAIRS2:
                    branch_mins(i + 1)
                    branch_probs(i + 1, 0)
                else:
                    memory_softmax("pm3", 0)
                for h in range(2):
                    dve.wait_ge(S["p3", "turned"], i * 5 + (3 + h))
                    dve.tensor_copy(pt[:, 1, h, 0:CAUSAL], bank[4 + h][:, 0:CAUSAL]
                                    ).then_inc(S["p3", "pt_dve"], 1)
                if i + 1 < PAIRS2:
                    branch_probs(i + 1, 1)
                dve.wait_ge(S["p3", "turned"], i * 5 + 5)
                dve.tensor_copy(ptc[0:NCMP, :, :], bank[4][0:NCMP, :].rearrange("p (h t) -> p h t", h=2)
                                ).then_inc(S["p3", "pt_dve"], 1)
                if i + 1 < PAIRS2:
                    branch_probs(i + 1, 2)
                else:
                    memory_probs("pm3", 0)
                if i + 4 < PAIRS2:
                    refill(0, pair_at(QUERY_BLOCK[i + 4]))
                elif i < 4:
                    filler(i)
                o_low("p3", i, i, 7)

            for i in range(PAIRS2):
                nsa(i)
            finish("pm3", B_ROWS0)
            norm_sum("n2", B_KM - 1, ALPHA, True, "n1", fill=[B_KM - 1, B_KM])
            norm_x("n2", 2, 3)
            refill(0, B_KM + 1)

            def ffn(ph, layer, b0):
                cf = Chain(dve, dchf[layer], 1)

                def taps(i):
                    cf.begin(i)
                    dve.wait_ge(S[ph, "base"], i + 1)
                    cf.link(dve.scalar_tensor_tensor(out=t_a[:, 1:T], in0=bank[0][:, 0:T - 1],
                                                     scalar=convf[:, layer, bass.ds(i, 1), 1], in1=t_a[:, 1:T],
                                                     op0=ALU.mult, op1=ALU.add))
                    dve.scalar_tensor_tensor(out=t_a[:, 2:T], in0=bank[0][:, 0:T - 2],
                                             scalar=convf[:, layer, bass.ds(i, 1), 0], in1=t_a[:, 2:T],
                                             op0=ALU.mult, op1=ALU.add).then_inc(S[ph, "free_a"], 1)
                    cf.end()

                def gated(i, b, buf=0):
                    dve.wait_ge(used, b)
                    dve.wait_ge(S[ph, "g"], i + 1)
                    dve.tensor_tensor(t_c[:, :], bank[1][:, 0:T], t_b[:, :], ALU.mult).then_inc(S[ph, "m"], 1)
                    dve.wait_ge(S[ph, "mh"], i + 1)
                    low(ml[:, buf, :], t_c[:, :], mh[:, buf, :].bitcast(F32), S[ph, "ml"])

                taps(0)
                refill(0, b0)
                gated(0, b0 + 2)
                refill(0, b0 + 1)

                def body(i):
                    taps(i + 1)
                    refill(i, b0 + 2)
                    if isinstance(i, int):
                        gated(i + 1, i * RING + (b0 + 4), 1)
                        refill(i, b0 + 3)
                    else:
                        refill(i, b0 + 3)
                        gated(i + 1, i * RING + (b0 + 5))
                    refill(i, b0 + 4)

                with dve.Fori(0, FT - 2) as i:
                    body(i)
                body(FT - 2)

            ffn("f0", 0, B_FFN0)
            norm_sum("n3", B_VM - 1, ALPHA, True, "n2", fill=[B_VM - 1, B_VM])
            norm_x("n3", 4, 5)
            refill(0, B_VM + 1)

            for n in range(PAIRS2 - 1):
                refill(0, B_MOBA + n)
            dve.wait_ge(used, B_QK)
            norm_wait(dve, "n3", "x", 2)
            dve.tensor_copy(v_all[:, 0, 0:512], bank[5][:, :]).then_inc(v_up[1], 1)
            dve.tensor_copy(v_all[:, :, 512:PAIRS2 * P], bank[7][:, :].rearrange("p (t c) -> p t c", t=NT)
                            ).then_inc(v_up[1], 1)
            refill(0, B_QK - 1)

            def moba(i):
                b = B_QK + 2 * i
                refill(0, b)
                if i:
                    dve.wait_ge(S["p5", "turned"], 2 * i)
                    dve.tensor_copy(pt[:, 0, 1, 0:CAUSAL], bank[6][:, 0:CAUSAL]).then_inc(S["p5", "pt_dve"], 1)
                dve.wait_ge(S["p5", "bias_in"], i * 16 + 16)
                for h in range(2):
                    dve.wait_ge(S["p5", "s"], i * 2 + (h + 1))
                    score_min("p5", 0, h, bank[3 + h], NO_KEY)
                if i:
                    o_low("p5", i - 1, i - 1, 7)
                refill(0, b + 1)
                dve.wait_ge(S["p5", "exp"], i * 4 + 4)
                chain.link(dve.tensor_scalar(deng[:, 0:4], den[:, 0:4], TINY, None, ALU.max))
                chain.link(dve.reciprocal(rden[:, 0:4], deng[:, 0:4]))
                for h in range(2):
                    scale_probs("p5", 0, h, rden)

            for i in range(PAIRS2):
                moba(i)
            refill(0, B_ROWS1 - 2)
            dve.wait_ge(S["p5", "turned"], 2 * PAIRS2)
            dve.tensor_copy(pt[:, 0, 1, 0:CAUSAL], bank[6][:, 0:CAUSAL]).then_inc(S["p5", "pt_dve"], 1)
            memory_softmax("pm5", 0)
            refill(0, B_ROWS1 - 1)
            o_low("p5", PAIRS2 - 1, PAIRS2 - 1, 7)
            memory_probs("pm5", 0)
            finish("pm5", B_ROWS1)
            norm_sum("n4", B_FFN1 - 1, ALPHA, True, "n3")
            norm_x("n4", 6, 7)
            refill(0, B_FFN1 - 1)
            ffn("f1", 1, B_FFN1)
            norm_sum("n5", N_BLOCKS - 1, ALPHA, True, "n4")

        @block.tensor
        def _(pe):
            def stationary(slot, out, mov_h, mov_l):
                for k in range(KT):
                    pe.matmul(out, wh[slot][:, k, :], mov_h(k), start=k == 0, stop=False)
                    pe.matmul(out, wh[slot][:, k, :], mov_l(k), start=False, stop=False)
                    last = pe.matmul(out, wl[slot][:, k, :], mov_h(k), start=False, stop=k == KT - 1)
                last.then_inc(used, 1)

            def two_stationary(b, nm):
                ready(b + 2)
                for k in range(KT):
                    x_ready(nm)(k)
                    for n in range(2):
                        out, s = bank[n][:, 0:T], slot_of(b + n)
                        pe.matmul(out, wh[s][:, k, :], xh[:, k, :], start=k == 0, stop=False)
                        pe.matmul(out, wh[s][:, k, :], xl[:, k, :], start=False, stop=False)
                        last = pe.matmul(out, wl[s][:, k, :], xh[:, k, :], start=False, stop=k == KT - 1)
                        if k == KT - 1:
                            last.then_inc(used, 1)

            def wide(slot, part, bk, sh, sl):
                for t in range(NT):
                    out = bk[:, t * T:(t + 1) * T]
                    for j in range(KT // 2):
                        k = part * KT // 2 + j
                        th, tl = sh[:, k, t * P:(t + 1) * P], sl[:, k, t * P:(t + 1) * P]
                        hw = wh[slot][:, 2 * j:2 * j + 2, :].rearrange("p k c -> p (k c)")
                        lw = wl[slot][:, 2 * j:2 * j + 2, :].rearrange("p k c -> p (k c)")
                        pe.matmul(out, th, hw, start=k == 0 and t == 0, stop=False)
                        pe.matmul(out, th, lw, start=False, stop=False)
                        last = pe.matmul(out, tl, hw, start=False, stop=k == KT - 1 and t == NT - 1)
                last.then_inc(used, 1)

            def x_ready(nm):
                def wait(k):
                    norm_wait(pe, nm, "xl_pool" if k % 2 else "xl_dve", k // 2 + 1)
                return wait

            def row(slot, th, tl, start, stop, half=None, bank7_read=None):
                for t in range(NT):
                    for n in range(2):
                        out = bank[4 + 2 * t + n][:, :]
                        if bank7_read is not None and t == n == 1:
                            pe.wait_ge(*bank7_read)
                        hw = wh[slot][:, 4 * n:4 * n + 4, :].rearrange("p k c -> p (k c)")
                        lw = wl[slot][:, 4 * n:4 * n + 4, :].rearrange("p k c -> p (k c)")
                        pe.matmul(out, th[:, t * P:(t + 1) * P], hw, start=start, stop=False)
                        pe.matmul(out, th[:, t * P:(t + 1) * P], lw, start=False, stop=False)
                        last = pe.matmul(out, tl[:, t * P:(t + 1) * P], hw, start=False, stop=stop)
                    if t == 0 and half is not None:
                        last.then_inc(half, 1)
                last.then_inc(used, 1)

            def ready(b):
                pe.wait_ge(split_l, b)

            def xm(k):
                return xh[:, k, :]

            def xml(k):
                return xl[:, k, :]

            def turn_x(nm, t):
                norm_wait(pe, nm, "z", t + 1)
                for k in range(KT):
                    ins = pe.transpose(turned_x(nm, k)[:, t * P:(t + 1) * P], z[:, t, k * P:(k + 1) * P], ident[:, :])
                    if t == NT - 1:
                        ins.then_inc(S[nm, "turned"], 1)

            def scores(outs, q, k, s, lead=0):
                for t in range(NT):
                    cols = slice(s384(t).start + lead * t, s384(t).stop + lead * (t + 1))
                    for h in range(2):
                        r = slice(h * DH, (h + 1) * DH)
                        last = pe.matmul(outs[h][:, cols], q[r, t * P:(t + 1) * P], k[r, 0:lead + (t + 1) * P],
                                         start=True, stop=True)
                        if t == NT - 1:
                            last.then_inc(s, 1)

            def turn_p(out, p, s):
                for c in range(3):
                    last = pe.transpose(out[:, c * P:(c + 1) * P], p[:, c * P:(c + 1) * P], ident[:, :])
                last.then_inc(s, 1)

            def pv(h, v, p, start, stop):
                r = slice(h * DH, (h + 1) * DH)
                pe.matmul(bank[7][r, 0:T], v(0), p[:, 0:T], start=start, stop=False)
                return pe.matmul(bank[7][r, P:T], v(1), p[:, T:CAUSAL], start=False, stop=stop)

            def values(i, h):
                return lambda t: v_all[:, t, i * P + h * DH:i * P + (h + 1) * DH]

            def warm_up(count, bk=bank[3]):
                for _ in range(count):
                    pe.matmul(bk[:, :], zeros[:, 0:P], zeros[:, :], start=True, stop=True)

            pe.wait_ge(set_up, 5)
            warm_up(WARM_SETUP)
            pe.wait_ge(ident_up, 1)
            turn_x("n0", 0)
            turn_x("n0", 1)
            for k in range(KT):
                ready(k + 1)
                x_ready("n0")(k)
                row(slot_of(k), xh[:, k, :], xl[:, k, :], k == 0, k == KT - 1)
            pe.wait_ge(consts_in, 16 * 7)
            pe.wait_ge(set_up, 5)
            pe.matmul(bank[3][0:2 * PAIRS2, :], relb[:, :], onehot[:, :], start=True, stop=True
                      ).then_inc(rel_ps, 1)

            def first(i):
                fa, fd = S["p1", "free_act"], S["p1", "free_dve"]
                plan = [("q", fd, 4, 5), ("k", fa, 5, 4), ("xc", fa, 5, 5), ("cg", fa, 5, 6), ("bg", fa, 5, 7),
                        ("zc", fa, 5, 8), ("za", fd, 4, 6), ("gc", fd, 4, 7), ("ga", fd, 4, 8)]
                for p, (kind, free, per, count) in enumerate(plan):
                    ready(i * PER1 + (B_FIRST + p + 1))
                    pe.wait_ge(free, i * per + count)
                    stationary(slot_of(B_FIRST + p), bank[p % 3][:, 0:T], xm, xml)
                    if kind == "xc":
                        pe.wait_ge(fa, i * 5 + 7)
                        pe.wait_ge(v_up[0], 2)
                        pe.wait_ge(rel_sb, 1)
                        scores(bank[3:5], q_s, k_s, S["p1", "s"])
                    if kind == "zc":
                        for h in range(2):
                            pe.wait_ge(S["p1", "prob"], i * 4 + (2 * h + 2))
                            turn_p(bank[5 + h], pr[:, 0, h, :], S["p1", "turned"])
                    if kind == "gc":
                        pe.wait_ge(S["p1", "pt_act"], i + 1)
                        pe.wait_ge(S["p1", "pt_dve"], i + 1)
                        pe.wait_ge(v_pair, i + 1)
                        pv(0, lambda t: v_s[:, t, 0:DH], pt[:, 0, 0, :], True, True)
                        pv(1, lambda t: v_s[:, t, DH:P], pt[:, 0, 1, :], True, True).then_inc(S["p1", "o"], 1)

            with pe.Fori(0, PAIRS1 - 1) as i:
                first(i)
            first(PAIRS1 - 1)

            def open_banks():
                for n in range(4):
                    pe.matmul(bank[4 + n][:, :], zeros[:, 0:P], zeros[:, :], start=True, stop=False)

            def mix(which, slot, bk):
                stationary(slot, bk[:, 0:T], lambda k: mixh[:, which, k, :], lambda k: mixl[:, which, k, :])

            pe.wait_ge(dch1, 6 * PAIRS1)
            pe.wait_ge(S["p1", "free_act"], 5 + 5 * PAIRS1)
            open_banks()
            ready(B_MIX + 1)
            mix(0, slot_of(B_MIX), bank[0])
            ready(B_MIX + 2)
            mix(1, slot_of(B_MIX + 1), bank[1])
            with pe.Fori(0, KT - 2) as i:
                ready(i * RING + (B_MIX + 3))
                pe.wait_ge(S["p2", "free_a"], i + 1)
                mix(0, slot_of(B_MIX + 2), bank[0])
                ready(i * RING + (B_MIX + 4))
                pe.wait_ge(S["p2", "ml"], i + 1)
                row(slot_of(B_MIX + 3), mh[:, 0, :], ml[:, 0, :], False, False)
                ready(i * RING + (B_MIX + 5))
                mix(1, slot_of(B_MIX + 4), bank[1])
            ready(B_KM0 - 3)
            pe.wait_ge(S["p2", "free_a"], KT - 1)
            mix(0, slot_of(B_KM0 - 4), bank[0])
            ready(B_KM0 - 2)
            pe.wait_ge(S["p2", "ml"], KT - 1)
            mix(1, slot_of(B_KM0 - 3), bank[1])
            ready(B_KM0 - 1)
            row(slot_of(B_KM0 - 2), mh[:, 0, :], ml[:, 0, :], False, False)
            ready(B_KM0)
            pe.wait_ge(S["p2", "ml"], KT)
            row(slot_of(B_KM0 - 1), mh[:, 1, :], ml[:, 1, :], False, True, S["n1", "half"])

            def memory_keys(b, nm):
                for n in range(2):
                    ready(b + n + 1)
                    stationary(slot_of(b + n), bank[2 + n][:, 0:T], lambda k: memh[:, k, :], lambda k: meml[:, k, :])
                    turn_x(nm, n)

            pe.wait_ge(mem_l, 1)
            memory_keys(B_KM0, "n1")

            b = B_NSA
            fa, fd = S["p3", "free_act"], S["p3", "free_dve"]
            two_stationary(b, "n1")
            pe.wait_ge(kv_free, 2)
            for n in range(2):
                ready(b + n + 3)
                wide(slot_of(b + n + 2), n, bank[2], xh, xl)
            pe.wait_ge(S["p3", "blkl"], 1)

            def compress(n):
                s, q = n // 4, n % 4
                out = bank[3][0:16, s * T:(s + 1) * T]
                ready(cmp_block(n) + 1)
                sl = slot_of(cmp_block(n))
                for j in range(4):
                    l2 = 4 * q + j
                    hw = wh[sl][:, 2 * j:2 * j + 2, :].rearrange("p k c -> p (k c)")
                    lw = wl[sl][:, 2 * j:2 * j + 2, :].rearrange("p k c -> p (k c)")
                    pe.matmul(out, blkh[:, s, l2, :], hw, start=l2 == 0, stop=False)
                    pe.matmul(out, blkh[:, s, l2, :], lw, start=False, stop=False)
                    last = pe.matmul(out, blkl[:, s, l2, :], hw, start=False, stop=l2 == 15)
                last.then_inc(used, 1)

            def pair_block(n):
                ready(pair_at(n) + 1)
                bk = bank[PAIR_BANK[n]]
                if n >= 8:
                    wide(slot_of(pair_at(n)), n - 8, bk, memh, meml)
                else:
                    stationary(slot_of(pair_at(n)), bk[:, 0:T], xm, xml)

            for n in range(4):
                compress(2 * n)
                compress(2 * n + 1)
                if n == 3:
                    pe.wait_ge(S["p3", "q"], 1)
                pair_block(n)
            pe.wait_ge(S["p3", "hid_out"], 1)
            for s in range(2):
                for hf in range(2):
                    n = 2 * s + hf
                    last = pe.transpose(bank[3][:, n * 16:(n + 1) * 16], hid_rows[:, n * P:(n + 1) * P],
                                        ident[0:16, 0:16])
            last.then_inc(S["p3", "hid_in"], 1)
            pe.wait_ge(S["p3", "q"], 2)
            pair_block(4)
            pe.wait_ge(S["p3", "hid"], 1)
            for hf in range(2):
                pe.matmul(bank[3][0:DH, 128:144], w2[:, 0, hf, :], hid[:, 0, hf, :],
                          start=hf == 0, stop=hf == 1)
            for hf in range(2):
                last = pe.matmul(bank[3][0:16, 192:256], hid[:, 1, hf, :], w2[:, 1, hf, :],
                                 start=hf == 0, stop=hf == 1)
            last.then_inc(S["p3", "w2"], 1)
            warm_up(WARM_SCORES, bank[7])
            pe.wait_ge(fa, 5)
            pe.wait_ge(fd, 1)
            pe.wait_ge(S["p3", "cmp"], 3)

            def pair_scores(i):
                q = qall[:, i, :]
                pe.wait_ge(S["p3", "q"], i + 1)
                if i:
                    pe.wait_ge(S["p3", "max"], 12 * i)
                for br, keys in enumerate((ks2, kw2)):
                    scores(bank[2 * br:2 * br + 2], q, keys, S["p3", "s"], 0 if br else CMP)

            def pair_turn(i, br):
                for h in range(2):
                    if br:
                        pe.wait_ge(S["p3", "prob_pool"], i * 8 + (2 * h + 2))
                    else:
                        pe.wait_ge(S["p3", "prob"], i * 4 + (2 * h + 2))
                    turn_p(bank[4 + h], prs[i % 2][:, br, h, :], S["p3", "turned"])

            pair_scores(0)
            pe.wait_ge(S["p3", "fill"], 1)
            pair_block(5)

            def memory_scores(ph, j):
                for t in range(NT):
                    for h in range(2):
                        r = slice(h * DH, (h + 1) * DH)
                        last = pe.matmul(bank[h][:, t * T:(t + 1) * T],
                                         qall[r, PAIRS2 + j, t * P:(t + 1) * P], km[r, j, :],
                                         start=True, stop=True)
                        if t == NT - 1:
                            last.then_inc(S[ph, "s"], 1)

            def nsa(i):
                if i + 1 < PAIRS2:
                    pair_scores(i + 1)
                else:
                    pe.wait_ge(S["p3", "max"], 12 * PAIRS2)
                    pe.wait_ge(S["p3", "fill"], 1)
                    memory_scores("pm3", 0)
                if i == 0:
                    pe.wait_ge(S["p3", "q"], 4)
                pair_turn(i, 0)
                if i == 0:
                    pe.wait_ge(S["p3", "fill"], 2)
                elif i < 3:
                    pe.wait_ge(S["p3", "q"], i + 4)
                if i < 4:
                    pair_block(6 + i)
                else:
                    pe.wait_ge(S["p3", "fill"], 3)
                    warm_up(WARM_PAIR, bank[6])
                pe.wait_ge(S["p3", "pt_act"], i * 2 + 2)
                pair_turn(i, 1)
                if i == 0:
                    warm_up(WARM_PAIR, bank[7])
                pe.wait_ge(S["p3", "prob_pool"], i * 8 + 8)
                pe.wait_ge(S["p3", "pt_dve"], i * 3 + 1)
                for h in range(2):
                    for t in range(NT):
                        last = pe.transpose(bank[4][0:NCMP, h * T + t * P:h * T + (t + 1) * P],
                                            prc[i % 2][:, h, t, 0:NCMP], ident[:, :])
                last.then_inc(S["p3", "turned"], 1)
                if i:
                    pe.wait_ge(S["p3", "ol"], i)
                for h in range(2):
                    pv(h, lambda t: v_s[:, t, 0:DH], pt[:, 0, h, :], True, False)
                pe.wait_ge(S["p3", "pt_dve"], i * 3 + 3)
                for h in range(2):
                    pe.matmul(bank[7][h * DH:(h + 1) * DH, 0:T], vc[0:NCMP, :], ptc[0:NCMP, h, :],
                              start=False, stop=False)
                for h in range(2):
                    last = pv(h, lambda t: v_s[:, t, DH:P], pt[:, 1, h, :], False, True)
                last.then_inc(S["p3", "o"], 1)

            for i in range(PAIRS2):
                nsa(i)

            def memory_turn(ph, j):
                for h in range(2):
                    pe.wait_ge(S[ph, "prob"], 4 * j + 2 * h + 2)
                    for kk in range(NT):
                        for t in range(NT):
                            last = pe.transpose(bank[2 + h][:, (kk * NT + t) * P:(kk * NT + t + 1) * P],
                                                pr[:, 0, h, t * T + kk * P:t * T + (kk + 1) * P], ident[:, :])
                    last.then_inc(S[ph, "turned"], 1)

            def memory_out(ph, j):
                for h in range(2):
                    pe.wait_ge(S[ph, "pt_act"], j + 1)
                    if h == 1:
                        pe.wait_ge(S[ph, "pt_dve"], j + 1)
                    for kk in range(NT):
                        last = pe.matmul(bank[2][h * DH:(h + 1) * DH, 0:T],
                                         vm[:, kk, j * P + h * DH:j * P + (h + 1) * DH],
                                         pt[:, 0, h, kk * T:(kk + 1) * T], start=kk == 0, stop=kk == 1)
                last.then_inc(S[ph, "o"], 1)

            def finish(ph, main, r0, half):
                def rows(*ks):
                    for k in ks:
                        ready(r0 + k + 1)
                        row(slot_of(r0 + k), oh[:, k, :], ol[:, k, :], k == 0, k == KT - 1,
                            half if k == KT - 1 else None, (S[main, "ol"], PAIRS2) if k == 0 else None)

                if ph == "pm3":
                    warm_up(WARM_PAIR, bank[6])
                    memory_turn(ph, 0)
                rows(0, 1)
                if ph != "pm3":
                    memory_turn(ph, 0)
                rows(2)
                memory_out(ph, 0)
                memory_scores(ph, 1)
                rows(3, 4)
                pe.wait_ge(S[ph, "ol"], 1)
                memory_turn(ph, 1)
                rows(5)
                memory_out(ph, 1)
                rows(6)
                pe.wait_ge(S[ph, "ol"], 2)
                rows(7)

            pe.wait_ge(S["p3", "fill"], 3)
            finish("pm3", "p3", B_ROWS0, S["n2", "half"])
            memory_keys(B_KM, "n2")

            def ffn(ph, b0, nm):
                two_stationary(b0, nm)
                open_banks()

                with pe.Fori(0, FT - 2) as i:
                    ready(i * RING + (b0 + 3))
                    pe.wait_ge(S[ph, "free_a"], i + 1)
                    stationary(slot_of(b0 + 2), bank[0][:, 0:T], xm, xml)
                    ready(i * RING + (b0 + 4))
                    pe.wait_ge(S[ph, "ml"], i + 1)
                    row(slot_of(b0 + 3), mh[:, 0, :], ml[:, 0, :], False, False)
                    ready(i * RING + (b0 + 5))
                    stationary(slot_of(b0 + 4), bank[1][:, 0:T], xm, xml)
                b = b0 + 3 * FT - 4
                ready(b + 1)
                pe.wait_ge(S[ph, "free_a"], FT - 1)
                stationary(slot_of(b), bank[0][:, 0:T], xm, xml)
                ready(b + 2)
                pe.wait_ge(S[ph, "ml"], FT - 1)
                stationary(slot_of(b + 1), bank[1][:, 0:T], xm, xml)
                ready(b + 3)
                row(slot_of(b + 2), mh[:, 0, :], ml[:, 0, :], False, False)
                ready(b + 4)
                pe.wait_ge(S[ph, "ml"], FT)
                row(slot_of(b + 3), mh[:, 1, :], ml[:, 1, :], False, True, S["n3", "half"])

            ffn("f0", B_FFN0, "n2")
            norm_wait(pe, "n3", "mean", 1)
            for n in range(2):
                ready(B_VM + n + 1)
                wide(slot_of(B_VM + n), n, bank[4], memh, meml)
                turn_x("n3", n)

            for n in range(4):
                b = B_MOBA + n
                ready(b + 1)
                for j in range(2):
                    k = 2 * n + j
                    x_ready("n3")(k)
                    hw = wh[slot_of(b)][:, 4 * j:4 * j + 4, :].rearrange("p k c -> p (k c)")
                    lw = wl[slot_of(b)][:, 4 * j:4 * j + 4, :].rearrange("p k c -> p (k c)")
                    for t in range(NT):
                        tok = slice(t * P, (t + 1) * P)
                        pe.matmul(bank[5 + t][:, :], xh[:, k, tok], hw, start=k == 0, stop=False)
                        pe.matmul(bank[5 + t][:, :], xh[:, k, tok], lw, start=False, stop=False)
                        last = pe.matmul(bank[5 + t][:, :], xl[:, k, tok], hw, start=False, stop=k == KT - 1)
                last.then_inc(used, 1)
            for n in range(2):
                b = B_MOBA + 4 + n
                ready(b + 1)
                wide(slot_of(b), n, bank[7], xh, xl)
            fa, fd = S["p5", "free_act"], S["p5", "free_dve"]

            def moba_turn(i):
                for h in range(2):
                    pe.wait_ge(S["p5", "prob"], i * 4 + (2 * h + 2))
                    turn_p(bank[5 + h], pr[:, 0, h, :], S["p5", "turned"])

            def moba_out(i):
                pe.wait_ge(S["p5", "pt_act"], i + 1)
                pe.wait_ge(S["p5", "pt_dve"], i + 1)
                if i:
                    pe.wait_ge(S["p5", "ol"], i)
                for h in range(2):
                    last = pv(h, values(i, h), pt[:, 0, h, :], True, True)
                last.then_inc(S["p5", "o"], 1)

            def moba(i):
                b = B_QK + 2 * i
                for n in range(2):
                    ready(b + n + 1)
                    if i:
                        pe.wait_ge(fa, 2 * i - 1 + n)
                    stationary(slot_of(b + n), bank[n][:, 0:T], xm, xml)
                if i:
                    moba_turn(i - 1)
                else:
                    pe.wait_ge(v_up[1], 3)
                    pe.wait_ge(kv_free, 5)
                pe.wait_ge(fa, 2 * i + 2)
                scores(bank[3:5], q_s, k_s, S["p5", "s"])
                if i:
                    moba_out(i - 1)

            for i in range(PAIRS2):
                moba(i)
            b = B_ROWS1 - 2
            for n in range(2):
                ready(b + n + 1)
                stationary(slot_of(b + n), bank[n][:, 0:T], xm, xml)
            moba_turn(PAIRS2 - 1)
            pe.wait_ge(fa, 2 * PAIRS2 + 2)
            memory_scores("pm5", 0)
            moba_out(PAIRS2 - 1)
            finish("pm5", "p5", B_ROWS1, S["n4", "half"])
            warm_up(WARM_SETUP)
            for t in range(NT):
                turn_x("n4", t)
            ffn("f1", B_FFN1, "n4")


def _columns(w, c0, width=P):
    k = w.shape[0] // P
    part = w.reshape(k, P, -1)[:, :, c0:c0 + width]
    return part.transpose(1, 0, 2)


def _stream(v):
    blocks = []

    def add(x):
        blocks.append(np.ascontiguousarray(x).reshape(P, KT * P))

    w_in = v["w_in"][0]
    v1 = 6
    order = [4, 5, 0, 2, 1, 3, 7, 8, 9]
    for k in range(KT):
        add(w_in[k * P:(k + 1) * P, v1 * D:(v1 + 1) * D])
    for i in range(PAIRS1):
        for s in order:
            add(_columns(w_in, s * D + i * P))
    wc, wa, wo = v["w_out_conv"][0], v["w_out_attn"][0], v["w_o"][0]

    def skewed(n, first, second, rows):
        add(_columns(first, 0))
        add(_columns(second, 0))
        for j in range(1, n - 1):
            add(_columns(first, j * P))
            add(rows[(j - 1) * P:j * P])
            add(_columns(second, j * P))
        add(_columns(first, (n - 1) * P))
        add(_columns(second, (n - 1) * P))
        add(rows[(n - 2) * P:(n - 1) * P])
        add(rows[(n - 1) * P:n * P])

    skewed(KT, wc, wa, wo)
    aw = v["a_w_in_2"][0]
    q_w, hd = PAIRS2 * P, DH
    kc, vcmp, ks, vs, kw, vw, g, qm = (q_w, q_w + hd, q_w + 2 * hd, q_w + 3 * hd, q_w + 4 * hd,
                                       q_w + 5 * hd, q_w + 6 * hd, q_w + 6 * hd + 36)

    def beside(a, b):
        return np.concatenate([_columns(aw, a, hd), _columns(aw, b, hd)], axis=2)

    kv_a, kv_b = v["a_w_mem_kv_2"][0], v["b_w_mem_kv_2"][0]

    def wide(w):
        t = _columns(w, 0, T)
        return [t[:, n * 4:(n + 1) * 4] for n in range(t.shape[1] // 4)]

    for n in range(2):
        add(_columns(kv_a, n * P))
    add(beside(kc, vcmp))
    add(beside(ks, kw))
    for t in wide(np.concatenate([aw[:, vs:vs + hd], aw[:, vw:vw + hd], aw[:, g:g + 36],
                                  np.zeros((D, P - 36), aw.dtype)], axis=1)):
        add(t)
    cmp_w1 = wide(v["a_cmp_w1_k_2"][0]) + wide(v["a_cmp_w1_v_2"][0])
    fill = [_columns(aw, qm), _columns(aw, qm + P)] + wide(kv_a[:, T:2 * T])
    for n in range(len(PAIR_BANK)):
        for t in cmp_w1[2 * n:2 * n + 2]:
            add(t)
        add(fill[FILL_BLOCK.index(n)] if n in FILL_BLOCK else _columns(aw, QUERY_BLOCK.index(n) * P))
    for k in range(KT):
        add(v["a_w_out_2"][0][k * P:(k + 1) * P])
    for n in range(2):
        add(_columns(kv_b, n * P))

    def ffn(layer):
        w, half_w = v["ffn_w_in_2"][layer], FT * P
        skewed(FT, w[:, :half_w], w[:, half_w:], v["ffn_w_out_2"][layer])

    ffn(0)
    for t in wide(kv_b[:, T:2 * T]):
        add(t)
    kv, bw = v["shared_w_kv_2"], v["b_w_in_2"][0]
    t = _columns(kv, PAIRS2 * P, 512)
    for n in range(4):
        add(t[:, 2 * n:2 * n + 2])
    for t in wide(kv[:, PAIRS2 * P + 512:2 * PAIRS2 * P]):
        add(t)
    for i in range(PAIRS2):
        add(_columns(bw, i * P))
        add(_columns(kv, i * P))
    for i in range(2):
        add(_columns(bw, (PAIRS2 + i) * P))
    for k in range(KT):
        add(v["b_w_out_2"][0][k * P:(k + 1) * P])
    ffn(1)
    assert len(blocks) == N_BLOCKS, len(blocks)
    return np.stack(blocks)


def _alibi():
    delta = P + np.arange(P)[:, None] - np.arange(T)[None, :]
    count = ((delta <= 128).astype(np.float64) + (delta % 4 == 0) + (delta % 16 == 0))
    ok = (delta >= 0) & (count > 0)
    out = np.empty((2 * PAIRS1, P, T), np.float32)
    for h in range(2 * PAIRS1):
        slope = 2.0 ** (-8.0 * (h + 1) / (2 * PAIRS1))
        out[h] = np.where(ok, slope * delta - np.log(np.maximum(count, 1)), MASKED)
    return np.ascontiguousarray(out.reshape(PAIRS1, 2, P, T).transpose(0, 2, 1, 3)).reshape(PAIRS1, P, 2 * T)


def _distance_hot():
    delta = T - 1 - np.arange(RELW)
    n = np.maximum(delta, 0)
    nf = np.maximum(n, 1).astype(np.float32)
    large = 16 + (np.log(nf / np.float32(16)) / np.float32(np.log(8.0)) * np.float32(16)).astype(np.int32)
    bucket = np.where(n < 16, n, np.minimum(large, 31))
    hot = np.zeros((33, RELW), np.float32)
    for m in range(RELW):
        if delta[m] >= 0:
            hot[bucket[m], m] = -1.0
        else:
            hot[32, m] = 1.0
    return hot


def _tiles(x):
    y = x.reshape(x.shape[:-1] + (x.shape[-1] // P, P))
    return np.ascontiguousarray(np.moveaxis(y, -1, 0))


def kernel(**inputs):
    from concourse import bacc
    from concourse.bass_utils import run_bass_kernel_spmd

    v = {k: np.asarray(x) for k, x in inputs.items()}
    gains = [v["norm_g"][0], v["final_g"], v["ln1_g_2"][0], v["ln1_b_2"][0], v["ln2_g_2"][0], v["ln2_b_2"][0],
             v["ln1_g_2"][1], v["ln1_b_2"][1], v["ln2_g_2"][1], v["ln2_b_2"][1]]
    conv = np.concatenate([v["conv_w"][0], v["conv_w"][0][0:1]])
    conv_f = np.stack([np.concatenate([v["ffn_conv_w_2"][n], v["ffn_conv_b_2"][n][None]]) for n in range(2)])
    pe_kv = np.stack([v["a_cmp_pe_k_2"][0], v["a_cmp_pe_v_2"][0]])
    w2 = np.stack([v["a_cmp_w2_k_2"][0], v["a_cmp_w2_v_2"][0]])
    arrays = {
        "x": v["x"],
        "stream": _stream(v),
        "gains_t": _tiles(np.stack(gains)),
        "conv_t": np.ascontiguousarray(_tiles(conv).transpose(0, 2, 1)),
        "conv_f_t": np.ascontiguousarray(_tiles(conv_f).transpose(0, 1, 3, 2)),
        "b_merge_t": _tiles(v["b_merge"][0].reshape(2, D)),
        "pe_t": np.ascontiguousarray(pe_kv.reshape(2, 16, 2, DH).transpose(2, 3, 0, 1)).reshape(P, 2, 16),
        "w2_t": np.ascontiguousarray(w2.reshape(2, 2, P, DH).transpose(2, 0, 1, 3)),
        "mem_t": np.ascontiguousarray(v["mem_2"][0].T.reshape(KT, P, T).transpose(1, 0, 2)),
        "rel_bias_2": v["rel_bias_2"],
        "distance_hot": _distance_hot(),
        "alibi": _alibi(),
        "final_g": v["final_g"],
        "ln1_g_2": v["ln1_g_2"], "ln1_b_2": v["ln1_b_2"],
        "ln2_g_2": v["ln2_g_2"], "ln2_b_2": v["ln2_b_2"],
    }
    nc = bacc.Bacc("TRN2", target_bir_lowering=False, num_devices=1)
    a = {n: nc.dram_tensor(f"in_{n}", x.shape, mybir.dt.from_np(x.dtype), kind="ExternalInput").ap()
         for n, x in arrays.items()}
    a["out"] = nc.dram_tensor("out", (1, T, D), F32, kind="ExternalOutput").ap()
    build_program(nc, a)
    r = run_bass_kernel_spmd(nc, [{f"in_{n}": x for n, x in arrays.items()}], core_ids=[0])
    return r.results[0]["out"]
```
